# Optimizing a Trainium2 kernel written in Bass

```python
import math
import jax, jax.numpy as jnp
from jax import lax
import numpy as np

D_MODEL = 1024
BATCH = 1
SEQ = 512
DEPTH = 1

N_META = 16
CHUNK = 128
ROPE_BASE = 10000.0
EPS = 1e-6
MLA_HEADS = 8
MLA_Q_LORA = 384
MLA_KV_LORA = 256
MLA_NOPE = 64
MLA_ROPE = 32
MLA_V = 64
MLA_QK = MLA_NOPE + MLA_ROPE
RET_HEADS = 8
RET_DK = 64
RET_DV = 128
PEER_HEADS = 8
PEER_NKEYS = 128
PEER_EXPERTS = PEER_NKEYS * PEER_NKEYS
PEER_DQ = 128
PEER_TOPK = 16
PEER_BLOCK = 256
IN_SIZES = (MLA_Q_LORA, MLA_KV_LORA, MLA_ROPE, RET_HEADS * RET_DK, RET_HEADS * RET_DK,
            RET_HEADS * RET_DV, RET_HEADS * RET_DV, D_MODEL, D_MODEL)
IN_WIDTH = sum(IN_SIZES)


def rmsnorm(x, g):
    xf = x.astype(jnp.float32)
    y = xf * lax.rsqrt(jnp.mean(xf * xf, axis=-1, keepdims=True) + EPS)
    return (y * g.astype(jnp.float32)).astype(x.dtype)

def rope(x, pos):
    half = x.shape[-1] // 2
    inv = ROPE_BASE ** (-jnp.arange(half, dtype=jnp.float32) / half)
    ang = pos.astype(jnp.float32)[:, None] * inv[None, :]
    cos, sin = jnp.cos(ang), jnp.sin(ang)
    xf = x.astype(jnp.float32)
    x1, x2 = xf[..., :half], xf[..., half:]
    return jnp.concatenate([x1 * cos - x2 * sin, x1 * sin + x2 * cos], -1).astype(x.dtype)

def causal_block_attention(q, k, v):
    B, H, L, dqk = q.shape
    dv = v.shape[-1]
    nblk = -(-L // CHUNK)
    Lp = nblk * CHUNK
    qp = jnp.pad(q, ((0, 0), (0, 0), (0, Lp - L), (0, 0)))
    kpos = jnp.arange(L)
    scale = 1.0 / math.sqrt(dqk)

    def one_block(i):
        qb = lax.dynamic_slice_in_dim(qp, i * CHUNK, CHUNK, axis=2)
        s = jnp.einsum('bhqd,bhkd->bhqk', qb, k).astype(jnp.float32) * scale
        qpos = i * CHUNK + jnp.arange(CHUNK)
        s = jnp.where(kpos[None, :] <= qpos[:, None], s, -jnp.inf)
        p = jax.nn.softmax(s, axis=-1)
        return jnp.einsum('bhqk,bhkd->bhqd', p.astype(v.dtype), v)

    out = lax.map(one_block, jnp.arange(nblk))
    out = out.transpose(1, 2, 0, 3, 4).reshape(B, H, Lp, dv)
    return out[:, :, :L]

def mla_branch(c_q, c_kv, k_pe, pos, g_q_lora, w_uq, g_kv_lora, w_ukv, g_qk_q, g_qk_k):
    B, L, _ = c_q.shape
    q = (rmsnorm(c_q, g_q_lora) @ w_uq).reshape(B, L, MLA_HEADS, MLA_QK)
    kv = (rmsnorm(c_kv, g_kv_lora) @ w_ukv).reshape(B, L, MLA_HEADS, MLA_NOPE + MLA_V)
    k_nope, v = kv[..., :MLA_NOPE], kv[..., MLA_NOPE:]
    k = jnp.concatenate([k_nope, jnp.broadcast_to(k_pe[:, :, None, :], (B, L, MLA_HEADS, MLA_ROPE))], -1)
    q = rmsnorm(q, g_qk_q).transpose(0, 2, 1, 3)
    k = rmsnorm(k, g_qk_k).transpose(0, 2, 1, 3)
    q = jnp.concatenate([q[..., :MLA_NOPE], rope(q[..., MLA_NOPE:], pos)], -1)
    k = jnp.concatenate([k[..., :MLA_NOPE], rope(k[..., MLA_NOPE:], pos)], -1)
    o = causal_block_attention(q, k, v.transpose(0, 2, 1, 3))
    return o.transpose(0, 2, 1, 3).reshape(B, L, MLA_HEADS * MLA_V)

def retention_branch(q, k, v, gate, pos, g_gn):
    B, L, _ = q.shape
    H, C = RET_HEADS, CHUNK
    q = rope(q.reshape(B, L, H, RET_DK).transpose(0, 2, 1, 3), pos)
    k = rope(k.reshape(B, L, H, RET_DK).transpose(0, 2, 1, 3), pos) * (RET_DK ** -0.5)
    v = v.reshape(B, L, H, RET_DV).transpose(0, 2, 1, 3)
    P = (-N_META) % C
    Lp = L + P
    NC = Lp // C
    padf = lambda t: jnp.pad(t, ((0, 0), (0, 0), (P, 0), (0, 0))).reshape(B, H, NC, C, t.shape[-1])
    qc, kc, vc = padf(q), padf(k), padf(v)

    log_gamma = jnp.log(1.0 - 2.0 ** (-5.0 - jnp.arange(H, dtype=jnp.float32)))
    idx = jnp.arange(C, dtype=jnp.float32)
    diff = idx[:, None] - idx[None, :]
    decay = jnp.where(diff[None] >= 0, jnp.exp(jnp.maximum(diff, 0.0)[None] * log_gamma[:, None, None]), 0.0)
    zeta = jnp.exp((C - 1 - idx)[None, :] * log_gamma[:, None])
    xi = jnp.exp((idx + 1)[None, :] * log_gamma[:, None])
    gamma_c = jnp.exp(C * log_gamma)

    scores = jnp.einsum('bhncd,bhnmd->bhncm', qc, kc) * decay[None, :, None]
    inner = jnp.einsum('bhncm,bhnme->bhnce', scores, vc)
    chunk_kv = jnp.einsum('bhnmd,bhnme->bhnde', kc * zeta[None, :, None, :, None], vc)

    def step(state, kv_n):
        return gamma_c[None, :, None, None] * state + kv_n, state

    init = jnp.zeros((B, H, RET_DK, RET_DV), chunk_kv.dtype)
    _, prev_states = lax.scan(step, init, jnp.moveaxis(chunk_kv, 2, 0))
    prev_states = jnp.moveaxis(prev_states, 0, 2)
    cross = jnp.einsum('bhncd,bhnde->bhnce', qc, prev_states) * xi[None, :, None, :, None]
    y = (inner + cross).reshape(B, H, Lp, RET_DV)[:, :, P:]

    yf = y.astype(jnp.float32)
    mu = jnp.mean(yf, -1, keepdims=True)
    var = jnp.mean((yf - mu) ** 2, -1, keepdims=True)
    yn = ((yf - mu) * lax.rsqrt(var + EPS)).transpose(0, 2, 1, 3).reshape(B, L, H * RET_DV)
    yn = (yn * g_gn.astype(jnp.float32)).astype(gate.dtype)
    return jax.nn.silu(gate) * yn

def mixer_sublayer(h, pos, g_mix, w_in, g_q_lora, w_uq, g_kv_lora, w_ukv, g_qk_q, g_qk_k,
                   w_mla_out, g_ret_gn, w_ret_out, w_mix_out):
    hn = rmsnorm(h, g_mix)
    z = hn @ w_in
    c_q, c_kv, k_pe, r_q, r_k, r_v, r_g, za, zr = jnp.split(z, np.cumsum(IN_SIZES)[:-1].tolist(), axis=-1)
    y_a = mla_branch(c_q, c_kv, k_pe, pos, g_q_lora, w_uq, g_kv_lora, w_ukv, g_qk_q, g_qk_k) @ w_mla_out
    y_r = retention_branch(r_q, r_k, r_v, r_g, pos, g_ret_gn) @ w_ret_out
    merged = jax.nn.sigmoid(za) * y_a + jax.nn.sigmoid(zr) * y_r
    return merged @ w_mix_out

def peer_sublayer(h, g_ffn, w_peer_q, keys_1, keys_2, peer_u, peer_v):
    shape = h.shape
    x = rmsnorm(h, g_ffn).reshape(-1, shape[-1])
    T = x.shape[0]
    q = (x @ w_peer_q).reshape(T, PEER_HEADS, PEER_DQ)
    half = PEER_DQ // 2
    s1 = jnp.einsum('thd,kd->thk', q[..., :half], keys_1).astype(jnp.float32)
    s2 = jnp.einsum('thd,kd->thk', q[..., half:], keys_2).astype(jnp.float32)
    v1, i1 = lax.top_k(s1, PEER_TOPK)
    v2, i2 = lax.top_k(s2, PEER_TOPK)
    cand = (v1[..., :, None] + v2[..., None, :]).reshape(T, PEER_HEADS, PEER_TOPK * PEER_TOPK)
    sc, ci = lax.top_k(cand, PEER_TOPK)
    e1 = jnp.take_along_axis(i1, ci // PEER_TOPK, axis=-1)
    e2 = jnp.take_along_axis(i2, ci % PEER_TOPK, axis=-1)
    eidx = (e1 * PEER_NKEYS + e2).reshape(T, PEER_HEADS * PEER_TOPK)
    gates = jax.nn.softmax(sc, axis=-1).reshape(T, PEER_HEADS * PEER_TOPK).astype(x.dtype)

    pad = (-T) % PEER_BLOCK
    nb = (T + pad) // PEER_BLOCK
    xb = jnp.pad(x, ((0, pad), (0, 0))).reshape(nb, PEER_BLOCK, -1)
    ib = jnp.pad(eidx, ((0, pad), (0, 0))).reshape(nb, PEER_BLOCK, -1)
    gb = jnp.pad(gates, ((0, pad), (0, 0))).reshape(nb, PEER_BLOCK, -1)

    def block(args):
        xt, it, gt = args
        act = jax.nn.gelu(jnp.einsum('td,tkd->tk', xt, peer_u[it]), approximate=False)
        return jnp.einsum('tk,tkd->td', gt * act, peer_v[it])

    y = lax.map(block, (xb, ib, gb)).reshape(nb * PEER_BLOCK, -1)[:T]
    return y.reshape(shape)

def first_inputs(seed: int = 0) -> dict:
    key = jax.random.key(seed)
    ks = jax.random.split(key, 20)
    f32 = jnp.float32
    nrm = lambda k, s, sc: jax.random.normal(k, s, f32) * sc
    gain = lambda k, s: 1.0 + 0.02 * jax.random.normal(k, s, f32)
    return {
        "x": nrm(ks[0], (BATCH, SEQ, D_MODEL), 1.0),
        "meta_tokens": nrm(ks[1], (N_META, D_MODEL), 1.0),
        "g_mix": gain(ks[2], (DEPTH, D_MODEL)),
        "w_in": nrm(ks[3], (DEPTH, D_MODEL, IN_WIDTH), D_MODEL ** -0.5),
        "g_q_lora": gain(ks[4], (DEPTH, MLA_Q_LORA)),
        "w_uq": nrm(ks[5], (DEPTH, MLA_Q_LORA, MLA_HEADS * MLA_QK), MLA_Q_LORA ** -0.5),
        "g_kv_lora": gain(ks[6], (DEPTH, MLA_KV_LORA)),
        "w_ukv": nrm(ks[7], (DEPTH, MLA_KV_LORA, MLA_HEADS * (MLA_NOPE + MLA_V)), MLA_KV_LORA ** -0.5),
        "g_qk_q": gain(ks[8], (DEPTH, MLA_QK)),
        "g_qk_k": gain(ks[9], (DEPTH, MLA_QK)),
        "w_mla_out": nrm(ks[10], (DEPTH, MLA_HEADS * MLA_V, D_MODEL), (MLA_HEADS * MLA_V) ** -0.5),
        "g_ret_gn": gain(ks[11], (DEPTH, RET_HEADS * RET_DV)),
        "w_ret_out": nrm(ks[12], (DEPTH, RET_HEADS * RET_DV, D_MODEL), (RET_HEADS * RET_DV) ** -0.5),
        "w_mix_out": nrm(ks[13], (DEPTH, D_MODEL, D_MODEL), D_MODEL ** -0.5),
        "g_ffn": gain(ks[14], (DEPTH, D_MODEL)),
        "w_peer_q": nrm(ks[15], (DEPTH, D_MODEL, PEER_HEADS * PEER_DQ), D_MODEL ** -0.5),
        "peer_keys_1": nrm(ks[16], (DEPTH, PEER_NKEYS, PEER_DQ // 2), (PEER_DQ // 2) ** -0.5),
        "peer_keys_2": nrm(ks[17], (DEPTH, PEER_NKEYS, PEER_DQ // 2), (PEER_DQ // 2) ** -0.5),
        "peer_u": nrm(ks[18], (DEPTH, PEER_EXPERTS, D_MODEL), D_MODEL ** -0.5),
        "peer_v": nrm(ks[19], (DEPTH, PEER_EXPERTS, D_MODEL), PEER_HEADS ** -0.5),
    }

def first_block(x, meta_tokens, g_mix, w_in, g_q_lora, w_uq, g_kv_lora, w_ukv, g_qk_q, g_qk_k,
              w_mla_out, g_ret_gn, w_ret_out, w_mix_out, g_ffn, w_peer_q, peer_keys_1,
              peer_keys_2, peer_u, peer_v):
    B = x.shape[0]
    meta = jnp.broadcast_to(meta_tokens.astype(x.dtype)[None], (B, N_META, x.shape[-1]))
    h = jnp.concatenate([meta, x], axis=1)
    pos = jnp.arange(h.shape[1])
    for layer in range(DEPTH):
        h = h + mixer_sublayer(h, pos, g_mix[layer], w_in[layer], g_q_lora[layer], w_uq[layer],
                               g_kv_lora[layer], w_ukv[layer], g_qk_q[layer], g_qk_k[layer],
                               w_mla_out[layer], g_ret_gn[layer], w_ret_out[layer], w_mix_out[layer])
        if layer == DEPTH - 1:
            h = h[:, N_META:]
        h = h + peer_sublayer(h, g_ffn[layer], w_peer_q[layer], peer_keys_1[layer], peer_keys_2[layer],
                              peer_u[layer], peer_v[layer])
    return h


GLA_HEADS = 4
GLA_DK = 64
GLA_DV = 128
GLA_GATE_RANK = 16
GLA_GATE_TAU = 16.0
GLA_CHUNK = 64
GLA_QK = GLA_HEADS * GLA_DK
GLA_V = GLA_HEADS * GLA_DV
ATTN_HEADS = 8
ATTN_HEAD_DIM = 64
ATTN_DIM = ATTN_HEADS * ATTN_HEAD_DIM
DILATED_PAIRS = ((128, 1), (512, 4), (2048, 16))
ATTN_BLOCK = 128
MIX_WIDTH = GLA_V + ATTN_DIM
IN_SPLITS = (GLA_QK, GLA_QK, GLA_V, GLA_V, GLA_GATE_RANK, ATTN_DIM, ATTN_DIM, ATTN_DIM)
IN_WIDTH_2 = sum(IN_SPLITS)
D_FF = 2816
CONV_WIDTH = 3
N_MOD = 6


def rms_norm(x, g):
    xf = x.astype(jnp.float32)
    y = xf * lax.rsqrt(jnp.mean(xf * xf, axis=-1, keepdims=True) + EPS)
    return (y * g.astype(jnp.float32)).astype(x.dtype)

def alibi_slopes(n):
    return jnp.asarray([2.0 ** (-8.0 * (h + 1) / n) for h in range(n)], dtype=jnp.float32)

def gla_group(q, k, v, log_a, r, norm_g):
    B, S, H, _ = q.shape
    n = S // GLA_CHUNK

    def chunks(t):
        return t.reshape(B, n, GLA_CHUNK, H, t.shape[-1]).transpose(1, 0, 3, 2, 4).astype(jnp.float32)

    qc = chunks(q) * (GLA_DK ** -0.5)
    kc, vc, gc = chunks(k), chunks(v), chunks(log_a)
    causal = jnp.tril(jnp.ones((GLA_CHUNK, GLA_CHUNK), dtype=bool))

    def step(state, inp):
        qi, ki, vi, gi = inp
        b = jnp.cumsum(gi, axis=-2)
        b_last = b[..., -1, :]
        o_inter = jnp.einsum('bhck,bhkv->bhcv', qi * jnp.exp(b), state)
        diff = b[:, :, :, None, :] - b[:, :, None, :, :]
        decay = jnp.exp(jnp.where(causal[:, :, None], diff, -jnp.inf))
        scores = jnp.einsum('bhik,bhjk,bhijk->bhij', qi, ki, decay)
        o = o_inter + jnp.einsum('bhij,bhjv->bhiv', scores, vi)
        state = state * jnp.exp(b_last)[..., None] + jnp.einsum(
            'bhck,bhcv->bhkv', ki * jnp.exp(b_last[:, :, None, :] - b), vi)
        return state, o

    state0 = jnp.zeros((B, H, GLA_DK, GLA_DV), jnp.float32)
    _, o = lax.scan(step, state0, (qc, kc, vc, gc))
    o = o.transpose(1, 0, 3, 2, 4).reshape(B, S, H, GLA_DV)
    o = rms_norm(o, norm_g).reshape(B, S, H * GLA_DV)
    return (o * jax.nn.silu(r.astype(jnp.float32))).astype(r.dtype)

def dilated_branch(q, k, v, slopes, window, dilation):
    B, S, H, E = q.shape
    L = S // dilation
    span = window // dilation
    nb = -(-L // ATTN_BLOCK)
    pad = nb * ATTN_BLOCK - L

    def to_blocks(t):
        t = t.reshape(B, L, dilation, H, E).transpose(0, 2, 3, 1, 4)
        t = jnp.pad(t, ((0, 0), (0, 0), (0, 0), (0, pad), (0, 0)))
        return t.reshape(B, dilation, H, nb, ATTN_BLOCK, E)

    def with_prev(t):
        prev = jnp.pad(t, ((0, 0), (0, 0), (0, 0), (1, 0), (0, 0), (0, 0)))[:, :, :, :-1]
        return jnp.concatenate([prev, t], axis=4)

    qb = to_blocks(q)
    kw = with_prev(to_blocks(k))
    vw = with_prev(to_blocks(v))
    s = jnp.einsum('bdhnqe,bdhnke->bdhnqk', qb, kw).astype(jnp.float32) * (E ** -0.5)
    iq = jnp.arange(ATTN_BLOCK)[:, None]
    ik = jnp.arange(2 * ATTN_BLOCK)[None, :]
    rel = iq + ATTN_BLOCK - ik
    key_idx = jnp.arange(nb)[:, None, None] * ATTN_BLOCK + ik - ATTN_BLOCK
    valid = (rel >= 0) & (rel <= span) & (key_idx >= 0)
    alibi = -slopes[:, None, None, None] * (dilation * rel).astype(jnp.float32)
    s = jnp.where(valid, s + alibi, -jnp.inf)
    m = jnp.max(s, axis=-1, keepdims=True)
    p = jnp.exp(s - m)
    den = jnp.sum(p, axis=-1, keepdims=True)
    o = jnp.einsum('bdhnqk,bdhnke->bdhnqe', p, vw.astype(jnp.float32)) / den
    lse = (m + jnp.log(den))[..., 0]
    o = o.reshape(B, dilation, H, nb * ATTN_BLOCK, E)[:, :, :, :L]
    o = o.transpose(0, 3, 1, 2, 4).reshape(B, S, H, E)
    lse = lse.reshape(B, dilation, H, nb * ATTN_BLOCK)[:, :, :, :L]
    lse = lse.transpose(0, 3, 1, 2).reshape(B, S, H)
    return o, lse

def dilated_attention_group(q, k, v):
    slopes = alibi_slopes(ATTN_HEADS)
    outs, lses = [], []
    for window, dilation in DILATED_PAIRS:
        o, lse = dilated_branch(q, k, v, slopes, window, dilation)
        outs.append(o)
        lses.append(lse)
    weights = jax.nn.softmax(jnp.stack(lses, axis=0), axis=0)
    return jnp.einsum('gbsh,gbshe->bshe', weights, jnp.stack(outs, axis=0))

def causal_depthwise_conv(u, w, b):
    K, C = w.shape
    y = lax.conv_general_dilated(u, w[:, None, :], window_strides=(1,), padding=[(K - 1, 0)],
                                 dimension_numbers=('NWC', 'WIO', 'NWC'), feature_group_count=C)
    return y + b

def second_inputs(seed: int = 0) -> dict:
    key = jax.random.key(seed)
    ks = jax.random.split(key, 17)
    f32 = jnp.float32
    L = DEPTH

    def nrm(k, shape, scale):
        return jax.random.normal(k, shape, f32) * scale

    return {
        "x": nrm(ks[0], (BATCH, SEQ, D_MODEL), 1.0),
        "c": nrm(ks[1], (BATCH, D_MODEL), 1.0),
        "w_ada": nrm(ks[2], (L, D_MODEL, N_MOD * D_MODEL), 0.5 * D_MODEL ** -0.5),
        "b_ada": nrm(ks[3], (L, N_MOD * D_MODEL), 0.02),
        "norm1_g": 1.0 + nrm(ks[4], (L, D_MODEL), 0.02),
        "w_in": nrm(ks[5], (L, D_MODEL, IN_WIDTH_2), D_MODEL ** -0.5),
        "gla_w_gate": nrm(ks[6], (L, GLA_GATE_RANK, GLA_QK), GLA_GATE_RANK ** -0.5),
        "gla_b_gate": nrm(ks[7], (L, GLA_QK), 0.02),
        "gla_norm_g": 1.0 + nrm(ks[8], (L, GLA_DV), 0.02),
        "q_norm_g": 1.0 + nrm(ks[9], (L, ATTN_HEAD_DIM), 0.02),
        "k_norm_g": 1.0 + nrm(ks[10], (L, ATTN_HEAD_DIM), 0.02),
        "w_out": nrm(ks[11], (L, MIX_WIDTH, D_MODEL), MIX_WIDTH ** -0.5),
        "norm2_g": 1.0 + nrm(ks[12], (L, D_MODEL), 0.02),
        "w_up": nrm(ks[13], (L, D_MODEL, 2 * D_FF), D_MODEL ** -0.5),
        "conv_w": nrm(ks[14], (L, CONV_WIDTH, 2 * D_FF), CONV_WIDTH ** -0.5),
        "conv_b": nrm(ks[15], (L, 2 * D_FF), 0.02),
        "w_down": nrm(ks[16], (L, D_FF, D_MODEL), D_FF ** -0.5),
    }

def second_block(x, c, w_ada, b_ada, norm1_g, w_in, gla_w_gate, gla_b_gate, gla_norm_g,
              q_norm_g, k_norm_g, w_out, norm2_g, w_up, conv_w, conv_b, w_down):
    B, S, _ = x.shape
    cond = jax.nn.silu(c)
    split_at = np.cumsum(IN_SPLITS)[:-1].tolist()
    for l in range(DEPTH):
        mod = (cond @ w_ada[l] + b_ada[l])[:, None, :]
        sh1, sc1, g1, sh2, sc2, g2 = jnp.split(mod, N_MOD, axis=-1)

        h = rms_norm(x, norm1_g[l]) * (1 + sc1) + sh1
        proj = h @ w_in[l]
        gq, gk, gv, gr, glr, aq, ak, av = jnp.split(proj, split_at, axis=-1)
        log_a = jax.nn.log_sigmoid((glr @ gla_w_gate[l] + gla_b_gate[l]).astype(jnp.float32)) / GLA_GATE_TAU
        y_gla = gla_group(gq.reshape(B, S, GLA_HEADS, GLA_DK), gk.reshape(B, S, GLA_HEADS, GLA_DK),
                          gv.reshape(B, S, GLA_HEADS, GLA_DV), log_a.reshape(B, S, GLA_HEADS, GLA_DK),
                          gr, gla_norm_g[l])
        qa = rms_norm(aq.reshape(B, S, ATTN_HEADS, ATTN_HEAD_DIM), q_norm_g[l])
        ka = rms_norm(ak.reshape(B, S, ATTN_HEADS, ATTN_HEAD_DIM), k_norm_g[l])
        y_att = dilated_attention_group(qa, ka, av.reshape(B, S, ATTN_HEADS, ATTN_HEAD_DIM))
        mixed = jnp.concatenate([y_gla.astype(x.dtype), y_att.reshape(B, S, ATTN_DIM).astype(x.dtype)], axis=-1)
        x = x + g1 * (mixed @ w_out[l])

        h = rms_norm(x, norm2_g[l]) * (1 + sc2) + sh2
        u = causal_depthwise_conv(h @ w_up[l], conv_w[l], conv_b[l])
        u_gate, u_val = jnp.split(u, 2, axis=-1)
        x = x + g2 * ((jax.nn.silu(u_gate) * u_val) @ w_down[l])
    return x


def setup_inputs(seed=0):
    out = dict(first_inputs(seed))
    for name, value in second_inputs(seed + 1).items():
        if name != "x":
            out[name + "_2"] = value
    return out


def reference(
    x, meta_tokens, g_mix, w_in, g_q_lora, w_uq, g_kv_lora, w_ukv, g_qk_q, g_qk_k, w_mla_out,
    g_ret_gn, w_ret_out, w_mix_out, g_ffn, w_peer_q, peer_keys_1, peer_keys_2, peer_u, peer_v,
    c_2, w_ada_2, b_ada_2, norm1_g_2, w_in_2, gla_w_gate_2, gla_b_gate_2, gla_norm_g_2,
    q_norm_g_2, k_norm_g_2, w_out_2, norm2_g_2, w_up_2, conv_w_2, conv_b_2, w_down_2,
):
    x = first_block(
        x, meta_tokens, g_mix, w_in, g_q_lora, w_uq, g_kv_lora, w_ukv, g_qk_q, g_qk_k,
        w_mla_out, g_ret_gn, w_ret_out, w_mix_out, g_ffn, w_peer_q, peer_keys_1, peer_keys_2,
        peer_u, peer_v,
    )
    return second_block(
        x, c_2, w_ada_2, b_ada_2, norm1_g_2, w_in_2, gla_w_gate_2, gla_b_gate_2, gla_norm_g_2,
        q_norm_g_2, k_norm_g_2, w_out_2, norm2_g_2, w_up_2, conv_w_2, conv_b_2, w_down_2,
    )


_drawn_inputs = setup_inputs


def setup_inputs(seed=0):
    import zlib

    import numpy as np

    out = dict(_drawn_inputs(seed))
    spreads = {}
    factors = {'g_q_lora': 7.537,
     'g_kv_lora': 6.575,
     'g_qk_q': 7.953,
     'g_qk_k': 7.256,
     'g_ret_gn': 3.468,
     'norm1_g_2': 8.0,
     'gla_b_gate_2': 8.0,
     'gla_norm_g_2': 8.0,
     'q_norm_g_2': 8.0,
     'k_norm_g_2': 8.0,
     'norm2_g_2': 8.0,
     'conv_b_2': 8.0}
    for name, (base, spread) in spreads.items():
        noise = np.random.default_rng([zlib.crc32(name.encode()), seed]).standard_normal(out[name].shape)
        drawn = base * np.exp(spread * noise) if base else spread * noise
        out[name] = __import__('jax').numpy.asarray(drawn.astype(out[name].dtype))
    for name, factor in factors.items():
        out[name] = (out[name] * factor).astype(out[name].dtype)
    return out
```

```python
from contextlib import ExitStack

import numpy as np
import concourse.bass as bass
from concourse import mybir
from concourse.alu_op_type import AluOpType as ALU

ACT = mybir.ActivationFunctionType
AX = mybir.AxisListType
F32 = mybir.dt.float32
BF16 = mybir.dt.bfloat16
U32 = mybir.dt.uint32

P = 128
D = 1024
KD = D // P
SEQ = 512
NT = SEQ // P
META = 16
KEYS = SEQ + META
EPS = 1e-6
NEG = -1e30
BANK = 512

MLA_H, MLA_QL, MLA_KVL, NOPE, ROPE, MLA_V = 8, 384, 256, 64, 32, 64
QK = NOPE + ROPE
RET_H, RET_DK, RET_DV = 8, 64, 128
PEER_H, NKEYS, TOPK = 8, 128, 16
PICKS = PEER_H * TOPK
HALF = SEQ // 2
GLA_H, GLA_DK, GLA_DV, GLA_CHUNK, GLA_RANK, GLA_TAU = 4, 64, 128, 64, 16, 16.0
DIL_H, DIL_E = 8, 64
DFF = 2816
NF = DFF // P


def shape_constants():
    out = {}
    pos = np.concatenate([META + np.arange(SEQ), np.arange(META)]).astype(np.float32)

    def rope_table(half, heads_dim):
        inv = (10000.0 ** (-np.arange(half, dtype=np.float32) / half)).astype(np.float32)
        ang = pos[:, None] * inv[None, :]
        c, s = np.cos(ang), np.sin(ang)
        full = np.zeros((5 * P, 2, 2 * half), np.float32)
        full[:KEYS, 0] = np.concatenate([c, c], 1)
        full[:KEYS, 1] = np.concatenate([-s, s], 1)
        return full.reshape(5, P, 2, 2 * half).transpose(1, 0, 2, 3).copy()

    out["c_rope_ret"] = rope_table(RET_DK // 2, RET_DK)
    out["c_rope_mla"] = rope_table(ROPE // 2, ROPE)
    p = np.arange(P)[:, None].astype(np.float64)
    gamma = 1.0 - 2.0 ** (-5.0 - np.arange(RET_H))
    c = np.arange(SEQ)[None, :].astype(np.float64)
    diff = c - p
    dec = np.where(diff >= 0, gamma[:, None, None] ** np.maximum(diff, 0)[None], 0.0)
    out["c_decay"] = (dec * RET_DK ** -0.5).transpose(1, 0, 2).astype(np.float32).copy()
    dm = META + c - p[:META]
    out["c_decay_meta"] = (gamma[:, None, None] ** dm[None] * RET_DK ** -0.5).transpose(1, 0, 2).astype(np.float32).copy()
    col = np.arange(KEYS)[None, :]
    delta = META + 3 * P + p - col
    out["c_causal"] = np.where(delta >= 0, 0.0, NEG).astype(np.float32)[:, None, :].copy()
    delta = 3 * P + p - np.arange(SEQ)[None, :]
    mult = (delta <= 128).astype(int) + (delta % 4 == 0) + (delta % 16 == 0)
    scale = DIL_E ** -0.5
    bias = []
    for h in range(DIL_H):
        slope = 2.0 ** (-8.0 * (h + 1) / DIL_H)
        b = (-slope * delta + np.log(np.maximum(mult, 1))) / scale
        bias.append(np.where((delta >= 0) & (mult > 0), b, NEG))
    out["c_dilated"] = np.stack(bias, 1).astype(np.float32)
    j, i = np.arange(P)[:, None], np.arange(P)[None, :]
    out["c_gla_mask"] = np.where((j <= i) & (j // GLA_CHUNK == i // GLA_CHUNK), GLA_DK ** -0.5, 0.0).astype(np.float32)
    keep = np.ones((P, SEQ), np.float32)
    keep[:, ::GLA_CHUNK] = 0.0
    out["c_scan_keep"] = keep
    out["c_ident"] = np.eye(P, dtype=np.float32)
    out["c_iota"] = np.tile(np.arange(P, dtype=np.float32), (P, 1))
    return out


class Link:

    def __init__(self, engine, sem):
        self.engine, self.sem, self.n = engine, sem, 0

    def __call__(self, ins):
        ins.then_inc(self.sem, 1)
        self.n += 1
        self.engine.wait_ge(self.sem, self.n)


class Phase:

    def __init__(self, nc, name):
        self.nc, self.name, self.stack, self.sems = nc, name, ExitStack(), []

    def __enter__(self):
        return self

    def __exit__(self, *a):
        self.stack.__exit__(*a)
        if self.sems:
            self.nc.clear_and_free_semaphores(self.sems)
            self.nc.all_engine_barrier(sem_only=True)

    def sb(self, name, shape, dt=F32):
        return self.stack.enter_context(self.nc.sbuf_tensor(f"{self.name}_{name}", list(shape), dt))

    def ps(self, name, shape, dt=F32):
        return self.stack.enter_context(self.nc.psum_tensor(f"{self.name}_{name}", list(shape), dt))

    def sem(self, name):
        self.sems.append(self.nc.alloc_semaphore(name=f"{self.name}_{name}"))
        return self.sems[-1]

    def block(self):
        return self.stack.enter_context(self.nc.Block())


def bc(ap, axis, n):
    v = ap.unsqueeze(axis)
    shape = list(v.shape)
    shape[axis] = n
    return v.to_broadcast(shape)


def norm_transpose(nc, name, consts, resid, hT, gain_dram, meta=None, mod=None, load=None):
    ident = consts["ident"]
    with Phase(nc, name) as ph:
        gain = ph.sb("gain", [P, KD])
        shift = ph.sb("shift", [P, KD])
        fac = ph.sb("fac", [P, KD])
        ssq = ph.sb("ssq", [P, 5])
        ms = ph.sb("ms", [P, 5])
        rstd = ph.sb("rstd", [P, 5])
        half = ph.sb("half", [P, 5])
        junk = ph.sb("junk", [P, D])
        xn = ph.sb("xn", [P, 2, D])
        tp = ph.ps("tp", [P, 4, BANK])
        loaded, gained, sums, means, roots, scaled, turned = (
            ph.sem(n) for n in ("loaded", "gained", "sums", "means", "roots", "scaled", "turned"))
        act_out, dve_out, ready, dve_link, pool_link = (
            ph.sem(n) for n in ("act_out", "dve_out", "ready", "dve_link", "pool_link"))
        tiles = [(t, P, t * P) for t in range(NT)] + ([(NT, META, SEQ)] if meta is not None else [])
        src = lambda t, rows: resid[:, t, :] if t < NT else meta[0:META, :]
        block = ph.block()

        @block.sync
        def _(sp):
            sp.dma_start(gain[:], gain_dram).then_inc(gained, 16)
            if load is not None:
                x_dram, meta_dram = load
                for t in range(NT):
                    sp.dma_start(resid[:, t, :], x_dram[t * P:(t + 1) * P, :]).then_inc(loaded, 16)
                    sp.wait_ge(loaded, 16 * (t + 1))
                sp.dma_start(meta[0:META, :], meta_dram).then_inc(loaded, 16)

        @block.scalar
        def _(act):
            for i, (t, rows, col) in enumerate(tiles):
                if load is not None:
                    act.wait_ge(loaded, 16 * (i + 1))
                act.activation(junk[0:rows, :], src(t, rows), ACT.Square, accum_out=ssq[0:rows, t:t + 1]).then_inc(sums, 1)
                act.wait_ge(sums, i + 1)
            act.wait_ge(ready, 1)
            for i, (t, rows, col) in enumerate(tiles):
                act.wait_ge(turned, 2 * i + 1)
                for k in range(4):
                    ins = act.activation(hT[:, k, col:col + rows], tp[:, (2 * i) % 4, k * P:k * P + rows], ACT.Identity,
                                         bias=shift[:, k:k + 1], scale=fac[:, k:k + 1])
                ins.then_inc(act_out, 1)

        @block.gpsimd
        def _(pool):
            link = Link(pool, pool_link)
            link(pool.memset(half[:], -0.5))
            for i, (t, rows, col) in enumerate(tiles):
                pool.wait_ge(means, i + 1)
                pool.tensor_tensor(rstd[0:rows, t:t + 1], ms[0:rows, t:t + 1], half[0:rows, t:t + 1], ALU.pow).then_inc(roots, 1)

        @block.vector
        def _(dve):
            link = Link(dve, dve_link)
            dve.wait_ge(gained, 16)
            if mod is None:
                link(dve.memset(shift[:], 0.0))
                dve.tensor_copy(fac[:], gain[:]).then_inc(ready, 1)
            else:
                sc, sh = mod
                link(dve.tensor_copy(shift[:], sh))
                dve.scalar_tensor_tensor(fac[:], sc, 1.0, gain[:], ALU.add, ALU.mult).then_inc(ready, 1)
            dve.wait_ge(ready, 1)
            n = len(tiles)
            for i in range(n + 1):
                if i < n:
                    t, rows, col = tiles[i]
                    dve.wait_ge(sums, i + 1)
                    dve.tensor_scalar(ms[0:rows, t:t + 1], ssq[0:rows, t:t + 1], 1.0 / D, EPS, ALU.mult, ALU.add).then_inc(means, 1)
                    dve.wait_ge(roots, i + 1)
                    if i >= 2:
                        dve.wait_ge(turned, 2 * (i - 1))
                    dve.tensor_scalar(xn[0:rows, i % 2, :], src(t, rows), rstd[0:rows, t:t + 1], None, ALU.mult).then_inc(scaled, 1)
                if i >= 1:
                    t, rows, col = tiles[i - 1]
                    dve.wait_ge(turned, 2 * i)
                    for k in range(4):
                        ins = dve.tensor_scalar(hT[:, 4 + k, col:col + rows], tp[:, (2 * i - 1) % 4, k * P:k * P + rows],
                                                fac[:, 4 + k:5 + k], shift[:, 4 + k:5 + k], ALU.mult, ALU.add)
                    ins.then_inc(dve_out, 1)

        @block.tensor
        def _(pe):
            for i, (t, rows, col) in enumerate(tiles):
                pe.wait_ge(scaled, i + 1)
                if i >= 2:
                    pe.wait_ge(act_out, i - 1)
                for k in range(4):
                    ins = pe.transpose(tp[:, (2 * i) % 4, k * P:k * P + rows], xn[0:rows, i % 2, k * P:(k + 1) * P], ident[0:rows, 0:rows])
                ins.then_inc(turned, 1)
                if i >= 2:
                    pe.wait_ge(dve_out, i - 1)
                for k in range(4, 8):
                    ins = pe.transpose(tp[:, (2 * i + 1) % 4, (k - 4) * P:(k - 4) * P + rows], xn[0:rows, i % 2, k * P:(k + 1) * P], ident[0:rows, 0:rows])
                ins.then_inc(turned, 1)


def project(nc, name, hT, jobs, ring=3):
    with Phase(nc, name) as ph:
        w = ph.sb("w", [P, ring, KD, BANK])
        acc = ph.ps("acc", [P, 8, BANK])
        landed = [ph.sem(f"landed{i}") for i in range(ring)]
        tok_done, feat_done, tok_out, feat_out = (
            ph.sem(n) for n in ("tok_done", "feat_done", "tok_out", "feat_out"))
        tok_until = np.cumsum([len(o[1]) if o[0] == "tok" else 0 for _, o in jobs]).tolist()
        feat_until = np.cumsum([len(o[2]) if o[0] == "feat" else 0 for _, o in jobs]).tolist()
        block = ph.block()

        @block.sync
        def _(sp):
            for i, (wd, out) in enumerate(jobs):
                if i >= ring:
                    if tok_until[i - ring]:
                        sp.wait_ge(tok_done, tok_until[i - ring])
                    if feat_until[i - ring]:
                        sp.wait_ge(feat_done, feat_until[i - ring])
                n = wd.shape[1]
                sp.dma_start(w[:, i % ring, :, 0:n], wd.rearrange("(k p) n -> p k n", p=P)).then_inc(landed[i % ring], 16)

        @block.tensor
        def _(pe):
            n_tok = n_feat = 0
            for i, (wd, out) in enumerate(jobs):
                n = wd.shape[1]
                slot = w[:, i % ring]
                pe.wait_ge(landed[i % ring], 16 * (i // ring + 1))
                if out[0] == "tok":
                    for rows, col, dst in out[1]:
                        if n_tok >= 4:
                            pe.wait_ge(tok_out, n_tok - 3)
                        for k in range(KD):
                            ins = pe.matmul(acc[0:rows, n_tok % 4, 0:n], hT[:, k, col:col + rows], slot[:, k, 0:n],
                                            start=(k == 0), stop=(k == KD - 1))
                        ins.then_inc(tok_done, 1)
                        n_tok += 1
                else:
                    for j, dst in enumerate(out[2]):
                        m = min(P, n - j * P)
                        if n_feat >= 4:
                            pe.wait_ge(feat_out, n_feat - 3)
                        for k in range(KD):
                            ins = pe.matmul(acc[0:m, 4 + n_feat % 4, :], slot[:, k, j * P:j * P + m], hT[:, k, 0:SEQ],
                                            start=(k == 0), stop=(k == KD - 1))
                        ins.then_inc(feat_done, 1)
                        n_feat += 1

        @block.vector
        def _(dve):
            c = 0
            for wd, out in jobs:
                if out[0] == "tok":
                    for rows, col, dst in out[1]:
                        dve.wait_ge(tok_done, c + 1)
                        dve.tensor_copy(dst, acc[0:rows, c % 4, 0:wd.shape[1]]).then_inc(tok_out, 1)
                        c += 1

        @block.scalar
        def _(act):
            c = 0
            for wd, out in jobs:
                if out[0] == "feat":
                    for dst in out[2]:
                        act.wait_ge(feat_done, c + 1)
                        act.activation(dst, acc[0:dst.shape[0], 4 + c % 4, :], out[1]).then_inc(feat_out, 1)
                        c += 1


def out_project(nc, name, actT, w_dram, kchunks, resid, gate=None, out_dram=None):
    with Phase(nc, name) as ph:
        ring = 6
        w = ph.sb("w", [P, ring, D])
        tmp = ph.sb("tmp", [P, 2, BANK])
        acc = ph.ps("acc", [P, 8, BANK])
        landed = [ph.sem(f"landed{i}") for i in range(ring)]
        used, done, gated, added, stored = (ph.sem(n) for n in ("used", "done", "gated", "added", "stored"))
        block = ph.block()

        @block.sync
        def _(sp):
            for k in range(kchunks):
                if k >= ring:
                    sp.wait_ge(used, k - ring + 1)
                sp.dma_start(w[:, k % ring, :], w_dram[k * P:(k + 1) * P, :]).then_inc(landed[k % ring], 16)
            if out_dram is not None:
                for t in range(NT):
                    sp.wait_ge(added, 2 * (t + 1))
                    sp.dma_start(out_dram[t * P:(t + 1) * P, :], resid[:, t, :]).then_inc(stored, 16)
                sp.wait_ge(stored, 16 * NT)

        @block.tensor
        def _(pe):
            for k in range(kchunks):
                pe.wait_ge(landed[k % ring], 16 * (k // ring + 1))
                for t in range(NT):
                    for h in range(2):
                        ins = pe.matmul(acc[:, 2 * t + h, :], actT[:, k, t * P:(t + 1) * P], w[:, k % ring, h * BANK:(h + 1) * BANK],
                                        start=(k == 0), stop=(k == kchunks - 1))
                        if k == kchunks - 1:
                            ins.then_inc(done, 1)
                if k < kchunks - 1:
                    ins.then_inc(used, 1)

        @block.vector
        def _(dve):
            for i in range(2 * NT):
                t, h = divmod(i, 2)
                dst = resid[:, t, h * BANK:(h + 1) * BANK]
                dve.wait_ge(done, i + 1)
                if gate is None:
                    dve.tensor_tensor(dst, acc[:, i, :], dst, ALU.add).then_inc(added, 1)
                else:
                    dve.tensor_tensor(tmp[:, i % 2, :], acc[:, i, :], gate[:, h * BANK:(h + 1) * BANK], ALU.mult).then_inc(gated, 1)
                    dve.wait_ge(gated, i + 1)
                    dve.tensor_tensor(dst, tmp[:, i % 2, :], dst, ALU.add).then_inc(added, 1)


def attention(nc, name, consts, qT, kT, v, vmeta, table_dram, meta, scale, oT):
    ident = consts["ident"]
    keys = meta + SEQ
    H = 8
    nh = table_dram.shape[1]
    with Phase(nc, name) as ph:
        table = ph.sb("table", [P, nh, keys])
        s = ph.sb("s", [P, 2, keys])
        prob = ph.sb("prob", [P, 2, keys])
        probT = ph.sb("probT", [P, 2, NT, SEQ])
        probTm = ph.sb("probTm", [META, 2, SEQ])
        negmax = ph.sb("negmax", [P, 4 * H])
        rsum = ph.sb("rsum", [P, 4 * H])
        rinv = ph.sb("rinv", [P, 4 * H])
        S = ph.ps("S", [P, 2, 2 * BANK])
        T = ph.ps("T", [P, 2, BANK])
        M = ph.ps("M", [P, BANK])
        O = ph.ps("O", [P, BANK])
        tabled, scores, biased, exped, inverted, normed, turned, turned_m, copied, copied_m, pv, out = (
            ph.sem(n) for n in ("tabled", "scores", "biased", "exped", "inverted", "normed", "turned",
                                "turned_m", "copied", "copied_m", "pv", "out"))
        units = [(h, n) for h in range(H) for n in range(NT)]
        block = ph.block()

        @block.sync
        def _(sp):
            sp.dma_start(table[:], table_dram).then_inc(tabled, 16)

        @block.tensor
        def _(pe):
            def score(u):
                h, n = units[u]
                L = meta + (n + 1) * P
                if u >= 2:
                    pe.wait_ge(biased, u - 1)
                q = qT(h)[:, n * P:(n + 1) * P]
                first = min(L, BANK)
                ins = pe.matmul(S[:, u % 2, 0:first], q, kT(h)[:, 0:first], start=True, stop=True)
                if L > BANK:
                    ins = pe.matmul(S[:, u % 2, BANK:L], q, kT(h)[:, BANK:L], start=True, stop=True)
                ins.then_inc(scores, 1)

            def turn(u):
                h, n = units[u]
                pe.wait_ge(normed, u + 1)
                if u >= 2:
                    pe.wait_ge(copied, u - 1)
                for j in range(n + 1):
                    ins = pe.transpose(T[:, u % 2, j * P:(j + 1) * P], prob[:, u % 2, meta + j * P:meta + (j + 1) * P], ident[:])
                ins.then_inc(turned, 1)
                if meta:
                    if n == 0 and h >= 1:
                        pe.wait_ge(copied_m, h)
                    pe.transpose(M[0:meta, n * P:(n + 1) * P], prob[:, u % 2, 0:meta], ident[:]).then_inc(turned_m, 1)

            def values(h):
                pe.wait_ge(copied, NT * (h + 1))
                if meta:
                    pe.wait_ge(copied_m, h + 1)
                if h >= 1:
                    pe.wait_ge(out, h)
                base = 64 * (h % 2)
                for j in range(NT):
                    ins = pe.matmul(O[base:base + 64, j * P:], v[:, j, h * 64:(h + 1) * 64], probT[:, h % 2, j, j * P:],
                                    start=(j == 0), stop=(j == NT - 1 and not meta))
                if meta:
                    ins = pe.matmul(O[base:base + 64, :], vmeta[0:meta, h * 64:(h + 1) * 64], probTm[0:meta, h % 2, :],
                                    start=False, stop=True)
                ins.then_inc(pv, 1)

            n_u = len(units)
            for u in range(n_u + 2):
                if u < n_u:
                    score(u)
                if 1 <= u <= n_u:
                    turn(u - 1)
                if u >= NT + 1 and (u - 1) % NT == 0 and (u - 1) // NT <= H:
                    values((u - 1) // NT - 1)

        @block.vector
        def _(dve):
            def bias(u):
                h, n = units[u]
                L = meta + (n + 1) * P
                off = (NT - 1 - n) * P
                dve.wait_ge(scores, u + 1)
                if u >= 2:
                    dve.wait_ge(exped, u - 1)
                dve.tensor_tensor_reduce(s[:, u % 2, 0:L], S[:, u % 2, 0:L], table[:, h % nh, off:off + L], -scale, 3e38,
                                         ALU.add, ALU.min, negmax[:, u:u + 1]).then_inc(biased, 1)

            def norm(u):
                h, n = units[u]
                L = meta + (n + 1) * P
                dve.wait_ge(exped, u + 1)
                dve.reciprocal(rinv[:, u:u + 1], rsum[:, u:u + 1]).then_inc(inverted, 1)
                dve.wait_ge(inverted, u + 1)
                dve.tensor_scalar(prob[:, u % 2, 0:L], prob[:, u % 2, 0:L], rinv[:, u:u + 1], None, ALU.mult).then_inc(normed, 1)

            def collect(h):
                base = 64 * (h % 2)
                dve.wait_ge(pv, h + 1)
                dve.tensor_copy(oT[base:base + 64, h // 2, :], O[base:base + 64, :]).then_inc(out, 1)

            dve.wait_ge(tabled, 16)
            n_u = len(units)
            for u in range(n_u + 3):
                if u < n_u:
                    bias(u)
                if 1 <= u <= n_u:
                    norm(u - 1)
                if u >= NT + 2 and (u - 2) % NT == 0 and (u - 2) // NT <= H:
                    collect((u - 2) // NT - 1)

        @block.scalar
        def _(act):
            def expo(u):
                h, n = units[u]
                L = meta + (n + 1) * P
                act.wait_ge(biased, u + 1)
                if u >= 2:
                    act.wait_ge(turned, u - 1)
                    if meta:
                        act.wait_ge(turned_m, u - 1)
                act.activation(prob[:, u % 2, 0:L], s[:, u % 2, 0:L], ACT.Exp, bias=negmax[:, u:u + 1], scale=-1.0,
                               accum_out=rsum[:, u:u + 1]).then_inc(exped, 1)

            def copy(u):
                h, n = units[u]
                act.wait_ge(turned, u + 1)
                if n == 0 and h >= 2:
                    act.wait_ge(pv, h - 1)
                act.activation(probT[:, h % 2, 0:n + 1, n * P:(n + 1) * P],
                               T[:, u % 2, 0:(n + 1) * P].rearrange("p (j q) -> p j q", q=P), ACT.Copy).then_inc(copied, 1)
                if meta and n == NT - 1:
                    act.wait_ge(turned_m, u + 1)
                    act.activation(probTm[0:meta, h % 2, :], M[0:meta, :], ACT.Copy).then_inc(copied_m, 1)

            n_u = len(units)
            for u in range(n_u + 1):
                if u < n_u:
                    expo(u)
                if u >= 1:
                    copy(u - 1)


def retention(nc, consts, rq, rk, rv, rgT, gain_dram, decay_dram, decay_meta_dram, rope_dram):
    ident = consts["ident"]
    H = RET_H
    with Phase(nc, "ret") as ph:
        rope = ph.sb("rope", [P, 5, 2, RET_DK])
        gain = ph.sb("gain", [P, H])
        decay = ph.sb("decay", [P, H, SEQ])
        decay_m = ph.sb("decay_m", [META, H, SEQ])
        a = ph.sb("a", [P, 2, BANK])
        b = ph.sb("b", [P, 2, BANK])
        qT = ph.sb("qT", [P, 4, SEQ])
        kT = ph.sb("kT", [P, 4, KEYS])
        wide = [SEQ - j * P for j in range(NT)]
        at = [sum(wide[:j]) for j in range(NT)]
        m = ph.sb("m", [P, 2, sum(wide)])
        mm = ph.sb("mm", [META, 2, SEQ])
        stats = ph.sb("stats", [P, NT, 6])
        mv = ph.sb("mv", [P, H, NT, 2])
        var = ph.sb("var", [P, H, NT])
        rstd = ph.sb("rstd", [P, H, NT])
        half = ph.sb("half", [P, NT])
        yn = ph.sb("yn", [P, 2, NT, P])
        S = ph.ps("S", [P, 3, BANK])
        Y = ph.ps("Y", [P, 2, BANK])
        T = ph.ps("T", [P, 2, BANK])
        names = ("tables", "cosed", "swapped", "roped", "turned", "copied", "scored", "decayed", "pv",
                 "meaned", "rooted", "normed", "yturned", "gated", "dve_link", "pool_link")
        (tables, cosed, swapped, roped, turned, copied, scored, decayed, pv, meaned, rooted, normed,
         yturned, gated, dve_link, pool_link) = (ph.sem(n) for n in names)
        jobs = [(rq, t, P, qT, t * P) for t in range(NT)] + [(rk, t, P, kT, t * P) for t in range(NT)] + [(rk, NT, META, kT, SEQ)]
        heads = lambda x: x.rearrange("p (h e) -> p h e", e=RET_DK)
        block = ph.block()

        @block.sync
        def _(sp):
            sp.dma_start(rope[:], rope_dram).then_inc(tables, 16)
            sp.dma_start(decay[:], decay_dram).then_inc(tables, 16)
            sp.dma_start(decay_m[:], decay_meta_dram).then_inc(tables, 16)
            sp.dma_start(gain[:], gain_dram).then_inc(tables, 16)

        @block.gpsimd
        def _(pool):
            link = Link(pool, pool_link)
            link(pool.memset(half[:], -0.5))
            pool.wait_ge(tables, 64)
            for i, (src, t, rows, dst, col) in enumerate(jobs):
                x, o = heads(src[0:rows, t, :]), heads(b[0:rows, i % 2, :])
                if i >= 2:
                    pool.wait_ge(roped, i - 1)
                e = RET_DK // 2
                for lo, hi in ((0, e), (e, 0)):
                    ins = pool.tensor_tensor(o[:, :, lo:lo + e], x[:, :, hi:hi + e], bc(rope[0:rows, t, 1, lo:lo + e], 1, H), ALU.mult)
                ins.then_inc(swapped, 1)
            for h in range(H):
                pool.wait_ge(meaned, h + 1)
                pool.tensor_tensor(rstd[:, h, :], var[:, h, :], half[:], ALU.pow).then_inc(rooted, 1)

        @block.vector
        def _(dve):
            link = Link(dve, dve_link)
            dve.wait_ge(tables, 64)
            for i, (src, t, rows, dst, col) in enumerate(jobs):
                if i >= 2:
                    dve.wait_ge(turned, i - 1)
                x, o = heads(src[0:rows, t, :]), heads(a[0:rows, i % 2, :])
                dve.tensor_tensor(o, x, bc(rope[0:rows, t, 0, :], 1, H), ALU.mult).then_inc(cosed, 1)
                dve.wait_ge(cosed, i + 1)
                dve.wait_ge(swapped, i + 1)
                dve.tensor_tensor(a[0:rows, i % 2, :], a[0:rows, i % 2, :], b[0:rows, i % 2, :], ALU.add).then_inc(roped, 1)

            def mask(h):
                for j in range(NT + 1):
                    i = h * (NT + 1) + j
                    dve.wait_ge(scored, i + 1)
                    if h >= 2 and j == 0:
                        dve.wait_ge(pv, h - 1)
                    if j < NT:
                        dve.tensor_tensor(m[:, h % 2, at[j]:at[j] + wide[j]], S[:, i % 3, 0:wide[j]], decay[:, h, 0:wide[j]], ALU.mult).then_inc(decayed, 1)
                    else:
                        dve.tensor_tensor(mm[0:META, h % 2, :], S[0:META, i % 3, :], decay_m[0:META, h, :], ALU.mult).then_inc(decayed, 1)

            def norm(h):
                dve.wait_ge(pv, h + 1)
                for n in range(NT):
                    ins = dve.bn_stats(stats[:, n, :], Y[:, h % 2, n * P:(n + 1) * P])
                link(ins)
                for n in range(NT):
                    ins = dve.bn_aggr(mv[:, h, n, :], stats[:, n, :])
                link(ins)
                dve.tensor_scalar(var[:, h, :], mv[:, h, :, 1], EPS, None, ALU.add).then_inc(meaned, 1)
                dve.wait_ge(rooted, h + 1)
                if h >= 2:
                    dve.wait_ge(yturned, h - 1)
                for n in range(NT):
                    ins = dve.tensor_scalar(yn[:, h % 2, n, :], Y[:, h % 2, n * P:(n + 1) * P], mv[:, h, n, 0:1], rstd[:, h, n:n + 1], ALU.subtract, ALU.mult)
                ins.then_inc(normed, 1)

            def gate(h):
                dve.wait_ge(yturned, h + 1)
                dve.scalar_tensor_tensor(rgT[:, h, :], T[:, h % 2, :], gain[:, h:h + 1], rgT[:, h, :], ALU.mult, ALU.mult).then_inc(gated, 1)

            for h in range(H + 2):
                if h < H:
                    mask(h)
                if 1 <= h <= H:
                    norm(h - 1)
                if h >= 2:
                    gate(h - 2)

        @block.scalar
        def _(act):
            for i, (src, t, rows, dst, col) in enumerate(jobs):
                act.wait_ge(turned, i + 1)
                act.activation(dst[:, :, col:col + rows], T[:, i % 2, :].rearrange("p (c q) -> p c q", q=P)[:, :, 0:rows], ACT.Copy).then_inc(copied, 1)

        @block.tensor
        def _(pe):
            for i, (src, t, rows, dst, col) in enumerate(jobs):
                pe.wait_ge(roped, i + 1)
                if i >= 2:
                    pe.wait_ge(copied, i - 1)
                for c in range(4):
                    ins = pe.transpose(T[:, i % 2, c * P:c * P + rows], a[0:rows, i % 2, c * P:(c + 1) * P], ident[0:rows, 0:rows])
                ins.then_inc(turned, 1)
            pe.wait_ge(copied, len(jobs))

            def score(h):
                base = 64 * (h % 2)
                for j in range(NT + 1):
                    i = h * (NT + 1) + j
                    if i >= 3:
                        pe.wait_ge(decayed, i - 2)
                    k = kT[base:base + 64, h // 2, j * P:(j + 1) * P] if j < NT else kT[base:base + 64, h // 2, SEQ:KEYS]
                    if j < NT:
                        pe.matmul(S[:, i % 3, 0:wide[j]], k, qT[base:base + 64, h // 2, j * P:], start=True, stop=True).then_inc(scored, 1)
                    else:
                        pe.matmul(S[0:META, i % 3, :], k, qT[base:base + 64, h // 2, :], start=True, stop=True).then_inc(scored, 1)

            def values(h):
                pe.wait_ge(decayed, (NT + 1) * (h + 1))
                if h >= 2:
                    pe.wait_ge(normed, h - 1)
                e = slice(h * RET_DV, (h + 1) * RET_DV)
                for n in range(NT):
                    o = Y[:, h % 2, n * P:(n + 1) * P]
                    pe.matmul(o, mm[0:META, h % 2, n * P:(n + 1) * P], rv[0:META, NT, e], start=True, stop=False)
                    for j in range(n + 1):
                        c = at[j] + (n - j) * P
                        ins = pe.matmul(o, m[:, h % 2, c:c + P], rv[:, j, e], start=False, stop=(j == n))
                ins.then_inc(pv, 1)

            def turn(h):
                pe.wait_ge(normed, h + 1)
                if h >= 2:
                    pe.wait_ge(gated, h - 1)
                for n in range(NT):
                    ins = pe.transpose(T[:, h % 2, n * P:(n + 1) * P], yn[:, h % 2, n, :], ident[:])
                ins.then_inc(yturned, 1)

            for h in range(H + 2):
                if h < H:
                    score(h)
                if 1 <= h <= H:
                    values(h - 1)
                if h >= 2:
                    turn(h - 2)


def mla_prepare(nc, consts, cq, ckv, w_uq_dram, w_ukv_dram, g_ql_dram, g_kvl_dram, g_q_dram, g_k_dram, rope_dram, qT, kT, v):
    ident = consts["ident"]
    H = MLA_H
    with Phase(nc, "mla") as ph:
        wq = ph.sb("wq", [P, 3, H * QK])
        wkv = ph.sb("wkv", [P, 2, H * (NOPE + MLA_V)])
        gl = ph.sb("gl", [P, 5])
        gqk = ph.sb("gqk", [P, 2, QK])
        rope = ph.sb("rope", [P, 5, 2, ROPE])
        ssq = ph.sb("ssq", [P, 9])
        ms = ph.sb("ms", [P, 9])
        rstd = ph.sb("rstd", [P, 9])
        ss8 = ph.sb("ss8", [P, 9, H])
        ms8 = ph.sb("ms8", [P, 9, H])
        rstd8 = ph.sb("rstd8", [P, 9, H])
        half = ph.sb("half", [P, 9])
        cn = ph.sb("cn", [P, 2, MLA_QL])
        cqT = ph.sb("cqT", [P, 3, SEQ])
        ckvT = ph.sb("ckvT", [P, 2, KEYS])
        x = ph.sb("x", [P, 2, H, QK])
        sq = ph.sb("sq", [P, 2, H * QK])
        ra = ph.sb("ra", [P, H, ROPE])
        rb = ph.sb("rb", [P, H, ROPE])
        A = ph.ps("A", [P, 2, 2, BANK])
        T = ph.ps("T", [P, 2, 2, BANK])
        names = ("loaded", "squares", "junked", "means", "roots", "scaled", "turned1", "copied1", "made", "filled",
                 "squared", "means8", "roots8", "normed", "swapped", "roped", "turned2", "copied2", "pool_link", "dve_link")
        (loaded, squares, junked, means, roots, scaled, turned1, copied1, made, filled, squared, means8, roots8,
         normed, swapped, roped, turned2, copied2, pool_link, dve_link) = (ph.sem(n) for n in names)
        lat = [(cq[:, t, :], P, 3, cqT, t * P, 0) for t in range(NT)]
        lat += [(ckv[:, t, 0:MLA_KVL], P, 2, ckvT, t * P, 3) for t in range(NT)]
        lat += [(ckv[0:META, NT, 0:MLA_KVL], META, 2, ckvT, SEQ, 3)]
        jobs = [(0, t, P) for t in range(NT)] + [(1, t, P) for t in range(NT)] + [(1, NT, META)]
        block = ph.block()

        @block.sync
        def _(sp):
            sp.dma_start(gl[:, 0:3], g_ql_dram).then_inc(loaded, 16)
            sp.dma_start(gl[:, 3:5], g_kvl_dram).then_inc(loaded, 16)
            sp.dma_start(gqk[:, 0, :], g_q_dram.partition_broadcast(P)).then_inc(loaded, 16)
            sp.dma_start(gqk[:, 1, :], g_k_dram.partition_broadcast(P)).then_inc(loaded, 16)
            sp.dma_start(rope[:], rope_dram).then_inc(loaded, 16)
            sp.dma_start(wq[:], w_uq_dram.rearrange("(k p) n -> p k n", p=P)).then_inc(loaded, 16)
            sp.dma_start(wkv[:], w_ukv_dram.rearrange("(k p) n -> p k n", p=P)).then_inc(loaded, 16)

        @block.scalar
        def _(act):
            for i, (src, rows, nch, dst, col, g) in enumerate(lat):
                act.activation(sq[0:rows, 0, 0:nch * P], src, ACT.Square, accum_out=ssq[0:rows, i:i + 1]).then_inc(squares, 1)
                act.wait_ge(squares, i + 1)

            def front(j):
                which, t, rows = jobs[j]
                act.wait_ge(made, j + 1)
                if j >= 2:
                    act.wait_ge(turned2, j - 1)
                if which == 0:
                    for b in range(2):
                        ins = act.activation(x[0:rows, j % 2, 4 * b:4 * b + 4, :], A[0:rows, j % 2, b, 0:4 * QK].rearrange("p (h e) -> p h e", e=QK), ACT.Copy)
                else:
                    for b in range(2):
                        kv = A[0:rows, j % 2, b, :].rearrange("p (h e) -> p h e", e=NOPE + MLA_V)
                        act.activation(x[0:rows, j % 2, 4 * b:4 * b + 4, 0:NOPE], kv[:, :, 0:NOPE], ACT.Copy)
                        act.activation(v[0:rows, t, 4 * b * 64:(4 * b + 4) * 64].rearrange("p (h e) -> p h e", e=MLA_V), kv[:, :, NOPE:], ACT.Copy)
                    ins = act.activation(x[0:rows, j % 2, :, NOPE:], bc(ckv[0:rows, t, MLA_KVL:], 1, H), ACT.Copy)
                ins.then_inc(filled, 1)
                act.wait_ge(filled, j + 1)
                if j >= 2:
                    act.wait_ge(means8, j - 1)
                act.activation(sq[0:rows, j % 2, :], x[0:rows, j % 2].rearrange("p h e -> p (h e)"), ACT.Square).then_inc(squared, 1)

            def back(j):
                which, t, rows = jobs[j]
                act.wait_ge(turned2, j + 1)
                col = 0 if t == NT else t * P + META * which
                dst = (qT, kT)[which][:, :, col:col + rows]
                for b in range(2):
                    ins = act.activation(dst[:, 4 * b:4 * b + 4, :], T[0:QK, j % 2, b, :].rearrange("p (h q) -> p h q", q=P)[:, :, 0:rows], ACT.Copy)
                ins.then_inc(copied2, 1)

            for j in range(len(jobs) + 1):
                if j < len(jobs):
                    front(j)
                if j >= 1:
                    back(j - 1)

        @block.gpsimd
        def _(pool):
            link = Link(pool, pool_link)
            link(pool.memset(half[:], -0.5))
            for i, (src, rows, nch, dst, col, g) in enumerate(lat):
                pool.wait_ge(means, i + 1)
                pool.tensor_tensor(rstd[0:rows, i:i + 1], ms[0:rows, i:i + 1], half[0:rows, 0:1], ALU.pow).then_inc(roots, 1)
            for j, (which, t, rows) in enumerate(jobs):
                pool.wait_ge(means8, j + 1)
                pool.tensor_tensor(rstd8[0:rows, j, :], ms8[0:rows, j, :], half[0:rows, 0:H], ALU.pow).then_inc(roots8, 1)
                pool.wait_ge(normed, j + 1)
                e = ROPE // 2
                for lo, hi in ((0, e), (e, 0)):
                    ins = pool.tensor_tensor(rb[0:rows, :, lo:lo + e], x[0:rows, j % 2, :, NOPE + hi:NOPE + hi + e], bc(rope[0:rows, t, 1, lo:lo + e], 1, H), ALU.mult)
                ins.then_inc(swapped, 1)

        @block.vector
        def _(dve):
            link = Link(dve, dve_link)
            dve.wait_ge(loaded, 16 * 7)
            for i, (src, rows, nch, dst, col, g) in enumerate(lat):
                dve.wait_ge(squares, i + 1)
                dve.tensor_scalar(ms[0:rows, i:i + 1], ssq[0:rows, i:i + 1], 1.0 / (nch * P), EPS, ALU.mult, ALU.add).then_inc(means, 1)
                dve.wait_ge(roots, i + 1)
                if i >= 2:
                    dve.wait_ge(turned1, i - 1)
                dve.tensor_scalar(cn[0:rows, i % 2, 0:nch * P], src, rstd[0:rows, i:i + 1], None, ALU.mult).then_inc(scaled, 1)
                dve.wait_ge(turned1, i + 1)
                for k in range(nch):
                    ins = dve.tensor_scalar(dst[:, k, col:col + rows], T[:, i % 2, 0, k * P:k * P + rows], gl[:, g + k:g + k + 1], None, ALU.mult)
                ins.then_inc(copied1, 1)
            for j, (which, t, rows) in enumerate(jobs):
                xj = x[0:rows, j % 2]
                dve.wait_ge(squared, j + 1)
                link(dve.tensor_reduce(ss8[0:rows, j, :], sq[0:rows, j % 2, :].rearrange("p (h e) -> p h e", e=QK), AX.X, ALU.add))
                dve.tensor_scalar(ms8[0:rows, j, :], ss8[0:rows, j, :], 1.0 / QK, EPS, ALU.mult, ALU.add).then_inc(means8, 1)
                dve.wait_ge(roots8, j + 1)
                link(dve.tensor_tensor(xj, xj, bc(rstd8[0:rows, j, :], 2, QK), ALU.mult))
                dve.tensor_tensor(xj, xj, bc(gqk[0:rows, which, :], 1, H), ALU.mult).then_inc(normed, 1)
                dve.wait_ge(normed, j + 1)
                link(dve.tensor_tensor(ra[0:rows], xj[:, :, NOPE:], bc(rope[0:rows, t, 0, :], 1, H), ALU.mult))
                dve.wait_ge(swapped, j + 1)
                dve.tensor_tensor(xj[:, :, NOPE:], ra[0:rows], rb[0:rows], ALU.add).then_inc(roped, 1)

        @block.tensor
        def _(pe):
            for i, (src, rows, nch, dst, col, g) in enumerate(lat):
                pe.wait_ge(scaled, i + 1)
                if i >= 2:
                    pe.wait_ge(copied1, i - 1)
                for k in range(nch):
                    ins = pe.transpose(T[:, i % 2, 0, k * P:k * P + rows], cn[0:rows, i % 2, k * P:(k + 1) * P], ident[0:rows, 0:rows])
                ins.then_inc(turned1, 1)
            pe.wait_ge(copied1, len(lat))
            pe.wait_ge(loaded, 16 * 7)

            def make(j):
                which, t, rows = jobs[j]
                if j >= 2:
                    pe.wait_ge(filled, j - 1)
                srcT, w, nch, n = ((cqT, wq, 3, 4 * QK), (ckvT, wkv, 2, BANK))[which]
                for b in range(2):
                    for k in range(nch):
                        ins = pe.matmul(A[0:rows, j % 2, b, 0:n], srcT[:, k, t * P:t * P + rows], w[:, k, b * n:(b + 1) * n],
                                        start=(k == 0), stop=(k == nch - 1))
                ins.then_inc(made, 1)

            def turn(j):
                which, t, rows = jobs[j]
                pe.wait_ge(roped, j + 1)
                if j >= 2:
                    pe.wait_ge(copied2, j - 1)
                for h in range(H):
                    ins = pe.transpose(T[0:QK, j % 2, h // 4, (h % 4) * P:(h % 4) * P + rows], x[0:rows, j % 2, h, :], ident[0:rows, 0:rows])
                ins.then_inc(turned2, 1)

            for j in range(len(jobs) + 1):
                if j < len(jobs):
                    make(j)
                if j >= 1:
                    turn(j - 1)


def merge(nc, oT, ygT, zaT, zrT, w_mla_dram, w_ret_dram):
    with Phase(nc, "merge") as ph:
        ring = 3
        w = ph.sb("w", [P, ring, 12, P])
        t1 = ph.sb("t1", [P, 2, BANK])
        t2 = ph.sb("t2", [P, 2, BANK])
        A = ph.ps("A", [P, 2, BANK])
        R = ph.ps("R", [P, 2, BANK])
        landed = [ph.sem(f"landed{i}") for i in range(ring)]
        a_done, r_done, gated, added = (ph.sem(n) for n in ("a_done", "r_done", "gated", "added"))
        block = ph.block()

        @block.sync
        def _(sp):
            for c in range(KD):
                if c >= ring:
                    sp.wait_ge(r_done, c - ring + 1)
                    sp.wait_ge(a_done, c - ring + 1)
                sp.dma_start(w[:, c % ring, 0:4, :], w_mla_dram[:, c * P:(c + 1) * P].rearrange("(k p) n -> p k n", p=P)).then_inc(landed[c % ring], 16)
                sp.dma_start(w[:, c % ring, 4:12, :], w_ret_dram[:, c * P:(c + 1) * P].rearrange("(k p) n -> p k n", p=P)).then_inc(landed[c % ring], 16)

        @block.tensor
        def _(pe):
            for c in range(KD):
                pe.wait_ge(landed[c % ring], 32 * (c // ring + 1))
                if c >= 2:
                    pe.wait_ge(gated, 2 * (c - 1))
                for k in range(4):
                    ins = pe.matmul(A[:, c % 2, :], w[:, c % ring, k, :], oT[:, k, :], start=(k == 0), stop=(k == 3))
                ins.then_inc(a_done, 1)
                for k in range(8):
                    ins = pe.matmul(R[:, c % 2, :], w[:, c % ring, 4 + k, :], ygT[:, k, :], start=(k == 0), stop=(k == 7))
                ins.then_inc(r_done, 1)

        @block.vector
        def _(dve):
            for c in range(KD):
                if c >= 2:
                    dve.wait_ge(added, c - 1)
                dve.wait_ge(a_done, c + 1)
                dve.tensor_tensor(t1[:, c % 2, :], A[:, c % 2, :], zaT[:, c, :], ALU.mult).then_inc(gated, 1)
                dve.wait_ge(r_done, c + 1)
                dve.tensor_tensor(t2[:, c % 2, :], R[:, c % 2, :], zrT[:, c, :], ALU.mult).then_inc(gated, 1)
                dve.wait_ge(gated, 2 * (c + 1))
                dve.tensor_tensor(zaT[:, c, :], t1[:, c % 2, :], t2[:, c % 2, :], ALU.add).then_inc(added, 1)


def peer_select(nc, consts, qT, keys_dram, iota_dram, e1T, e2T, gateT):
    ident = consts["ident"]
    H, K = PEER_H, TOPK
    with Phase(nc, "sel") as ph:
        keys = ph.sb("keys", [P, NKEYS])
        iota = ph.sb("iota", [P, P])
        s = ph.sb("s", [P, 2, H, 2, NKEYS])
        s2 = ph.sb("s2", [P, H, 2, NKEYS])
        best = ph.sb("best", [P, H, 2, K])
        idx = ph.sb("idx", [P, H, 2, K], U32)
        idxf = ph.sb("idxf", [P, H, 2, K])
        cand = ph.sb("cand", [P, H, K, K])
        cand2 = ph.sb("cand2", [P, H, K * K])
        top = ph.sb("top", [P, H, K])
        ci = ph.sb("ci", [P, H * K], U32)
        parts = ph.sb("parts", [P, 2, H * K], U32)
        partsf = ph.sb("partsf", [P, 2, H * K])
        hot = ph.sb("hot", [P, 2, H * K, K])
        shifted = ph.sb("shifted", [P, H, K])
        ex = ph.sb("ex", [P, H, K])
        den = ph.sb("den", [P, H])
        rden = ph.sb("rden", [P, H])
        picks = ph.sb("picks", [P, 3, H * K])
        S = ph.ps("S", [P, 4, BANK])
        T = ph.ps("T", [P, BANK])
        names = ("loaded", "scored", "copied", "used", "shiftd", "exped", "picked", "turned", "stored", "dve_link")
        loaded, scored, copied, used, shiftd, exped, picked, turned, stored, dve_link = (ph.sem(n) for n in names)
        block = ph.block()

        @block.sync
        def _(sp):
            sp.dma_start(keys[:], keys_dram).then_inc(loaded, 16)
            sp.dma_start(iota[:], iota_dram).then_inc(loaded, 16)

        @block.tensor
        def _(pe):
            def turn(t):
                pe.wait_ge(picked, t + 1)
                if t >= 1:
                    pe.wait_ge(stored, t)
                for i in range(3):
                    ins = pe.transpose(T[:, i * P:(i + 1) * P], picks[:, i, :], ident[:])
                ins.then_inc(turned, 1)

            pe.wait_ge(loaded, 32)
            for t in range(NT):
                if t >= 1:
                    pe.wait_ge(copied, t)
                for h in range(H):
                    for side in range(2):
                        r = slice(64 * side, 64 * side + 64)
                        ins = pe.matmul(S[:, 2 * side + h // 4, (h % 4) * NKEYS:(h % 4 + 1) * NKEYS], qT[r, h, t * P:(t + 1) * P], keys[r, :], start=True, stop=True)
                ins.then_inc(scored, 1)
                if t >= 1:
                    turn(t - 1)
            turn(NT - 1)

        @block.scalar
        def _(act):
            def store(t):
                act.wait_ge(turned, t + 1)
                for i, dst in enumerate((e1T, e2T, gateT)):
                    ins = act.activation(dst[:, t * P:(t + 1) * P], T[:, i * P:(i + 1) * P], ACT.Copy)
                ins.then_inc(stored, 1)

            for t in range(NT):
                act.wait_ge(scored, t + 1)
                if t >= 2:
                    act.wait_ge(used, t - 1)
                for b in range(4):
                    side, hs = b // 2, slice(4 * (b % 2), 4 * (b % 2) + 4)
                    ins = act.activation(s[:, t % 2, hs, side, :], S[:, b, :].rearrange("p (h k) -> p h k", h=4), ACT.Copy)
                ins.then_inc(copied, 1)
                if t >= 1:
                    store(t - 1)
                act.wait_ge(shiftd, t + 1)
                act.activation(ex[:], shifted[:], ACT.Exp).then_inc(exped, 1)
            store(NT - 1)

        @block.vector
        def _(dve):
            link = Link(dve, dve_link)
            dve.wait_ge(loaded, 32)
            for t in range(NT):
                st = s[:, t % 2]
                lists = [(h, c) for h in range(H) for c in range(2)]
                dve.wait_ge(copied, t + 1)
                for h, c in lists:
                    ins = dve.max(best[:, h, c, 0:8], st[:, h, c, :])
                link(ins)
                for h, c in lists:
                    ins = dve.max_index(idx[:, h, c, 0:8], best[:, h, c, 0:8], st[:, h, c, :])
                for h, c in lists:
                    ins = dve.match_replace(s2[:, h, c, :], best[:, h, c, 0:8], st[:, h, c, :], NEG)
                ins.then_inc(used, 1)
                dve.wait_ge(used, t + 1)
                for h, c in lists:
                    ins = dve.max(best[:, h, c, 8:16], s2[:, h, c, :])
                link(ins)
                for h, c in lists:
                    ins = dve.max_index(idx[:, h, c, 8:16], best[:, h, c, 8:16], s2[:, h, c, :])
                link(dve.tensor_tensor(cand[:], bc(best[:, :, 0, :], 3, K), bc(best[:, :, 1, :], 2, K), ALU.add))
                link(dve.tensor_copy(idxf[:], idx[:]))
                flat = cand[:].rearrange("p h a b -> p h (a b)")
                for h in range(H):
                    ins = dve.max(top[:, h, 0:8], flat[:, h, :])
                link(ins)
                for h in range(H):
                    ins = dve.max_index(ci[:, h * K:h * K + 8], top[:, h, 0:8], flat[:, h, :])
                for h in range(H):
                    ins = dve.match_replace(cand2[:, h, :], top[:, h, 0:8], flat[:, h, :], NEG)
                link(ins)
                for h in range(H):
                    ins = dve.max(top[:, h, 8:16], cand2[:, h, :])
                link(ins)
                for h in range(H):
                    ins = dve.max_index(ci[:, h * K + 8:h * K + 16], top[:, h, 8:16], cand2[:, h, :])
                link(ins)
                dve.tensor_tensor(shifted[:], top[:], bc(top[:, :, 0], 2, K), ALU.subtract).then_inc(shiftd, 1)
                dve.tensor_scalar(parts[:, 0, :], ci[:], 4, None, ALU.logical_shift_right)
                link(dve.tensor_scalar(parts[:, 1, :], ci[:], K - 1, None, ALU.bitwise_and))
                link(dve.tensor_copy(partsf[:], parts[:]))
                for c in range(2):
                    ins = dve.tensor_tensor(hot[:, c], bc(partsf[:, c, :], 2, K), bc(iota[:, 0:K], 1, H * K), ALU.is_equal)
                link(ins)
                for c in range(2):
                    o = hot[:, c].rearrange("p (h k) a -> p h k a", h=H)
                    ins = dve.tensor_tensor(o, o, bc(idxf[:, :, c, :], 2, K), ALU.mult)
                link(ins)
                if t >= 1:
                    dve.wait_ge(turned, t)
                for c in range(2):
                    dve.tensor_reduce(picks[:, c, :], hot[:, c], AX.X, ALU.add)
                dve.wait_ge(exped, t + 1)
                link(dve.tensor_reduce(den[:], ex[:], AX.X, ALU.add))
                link(dve.reciprocal(rden[:], den[:]))
                dve.tensor_tensor(picks[:, 2, :].rearrange("p (h k) -> p h k", h=H), ex[:], bc(rden[:], 2, K), ALU.mult).then_inc(picked, 1)


def peer_up(nc, half, xT, u_dram, act_buf):
    R = 4
    steps = NKEYS // R
    tok = slice(half * HALF, (half + 1) * HALF)
    with Phase(nc, f"up{half}") as ph:
        u = ph.sb("u", [P, R, KD, P])
        acc = ph.ps("acc", [P, R, BANK])
        landed = [ph.sem(f"landed{r}") for r in range(R)]
        done, out = ph.sem("done"), ph.sem("out")
        block = ph.block()

        @block.sync
        def _(sp):
            def load(r, i):
                sp.dma_start(u[:, r], u_dram[bass.ds(i * R + r, 1)].rearrange("o p k e -> (o p) k e")).then_inc(landed[r], 16)

            for r in range(R):
                load(r, 0)
            with sp.Fori(1, steps) as i:
                for r in range(R):
                    sp.wait_ge(done, (i - 1) * R + r + 1)
                    load(r, i)

        @block.tensor
        def _(pe):
            def chunk(r, i):
                pe.wait_ge(landed[r], (i + 1) * 16)
                for k in range(KD):
                    ins = pe.matmul(acc[:, r, 0:HALF], u[:, r, k, :], xT[:, k, tok], start=(k == 0), stop=(k == KD - 1))
                ins.then_inc(done, 1)

            for r in range(R):
                chunk(r, 0)
            with pe.Fori(1, steps) as i:
                for r in range(R):
                    pe.wait_ge(out, (i - 1) * R + r + 1)
                    chunk(r, i)

        @block.scalar
        def _(act):
            with act.Fori(0, steps) as i:
                for r in range(R):
                    act.wait_ge(done, i * R + r + 1)
                    act.activation(act_buf[:, bass.ds(i * R + r, 1), :], acc[:, r:r + 1, 0:HALF], ACT.Gelu).then_inc(out, 1)


def peer_gate(nc, half, iota_dram, e1T, e2T, gateT, act_buf):
    G = 4
    steps = HALF // (2 * G)
    with Phase(nc, f"gate{half}") as ph:
        iota = ph.sb("iota", [P, P])
        hot1 = ph.sb("hot1", [P, 2, G, P])
        hot2 = ph.sb("hot2", [P, 2, G, P])
        acc = ph.ps("acc", [P, 2, BANK])
        loaded, built, done, out = (ph.sem(n) for n in ("loaded", "built", "done", "out"))
        block = ph.block()

        @block.sync
        def _(sp):
            sp.dma_start(iota[:], iota_dram).then_inc(loaded, 16)

        @block.vector
        def _(dve):
            def hots(r, i):
                for g in range(G):
                    t = half * HALF + (i * 2 + r) * G + g
                    dve.tensor_scalar(hot1[:, r, g, :], iota[:], e1T[:, bass.ds(t, 1)], gateT[:, bass.ds(t, 1)], ALU.is_equal, ALU.mult)
                    ins = dve.tensor_scalar(hot2[:, r, g, :], iota[:], e2T[:, bass.ds(t, 1)], None, ALU.is_equal)
                ins.then_inc(built, 1)

            def weigh(r, i):
                a = act_buf[:, :, bass.ds((i * 2 + r) * G, G)]
                dve.tensor_tensor(a, acc[:, r, :].rearrange("p (g e) -> p e g", g=G), a, ALU.mult).then_inc(out, 1)

            dve.wait_ge(loaded, 16)
            hots(0, 0)
            with dve.Fori(0, steps - 1) as i:
                hots(1, i)
                dve.wait_ge(done, 2 * i + 1)
                weigh(0, i)
                hots(0, i + 1)
                dve.wait_ge(done, 2 * i + 2)
                weigh(1, i)
            hots(1, steps - 1)
            dve.wait_ge(done, 2 * steps - 1)
            weigh(0, steps - 1)
            dve.wait_ge(done, 2 * steps)
            weigh(1, steps - 1)

        @block.tensor
        def _(pe):
            def products(r, i):
                pe.wait_ge(built, 2 * i + r + 1)
                for g in range(G):
                    ins = pe.matmul(acc[:, r, g * P:(g + 1) * P], hot1[:, r, g, :], hot2[:, r, g, :], start=True, stop=True)
                ins.then_inc(done, 1)

            products(0, 0)
            products(1, 0)
            with pe.Fori(1, steps) as i:
                for r in range(2):
                    pe.wait_ge(out, 2 * i + r - 1)
                    products(r, i)


def peer_down(nc, consts, half, v_dram, act_buf, resid):
    ident = consts["ident"]
    R = 4
    steps = NKEYS // R
    with Phase(nc, f"down{half}") as ph:
        v = ph.sb("v", [P, R, D])
        yT = ph.sb("yT", [P, KD, HALF])
        Y = ph.ps("Y", [P, KD, HALF])
        T = ph.ps("T", [P, 4, BANK])
        landed = [ph.sem(f"landed{r}") for r in range(R)]
        done, copied, turned, added = (ph.sem(n) for n in ("done", "copied", "turned", "added"))
        block = ph.block()

        @block.sync
        def _(sp):
            def load(r, i):
                sp.dma_start(v[:, r:r + 1, :], v_dram[:, bass.ds(i * R + r, 1), :]).then_inc(landed[r], 16)

            for r in range(R):
                load(r, 0)
            with sp.Fori(1, steps) as i:
                for r in range(R):
                    sp.wait_ge(done, (i - 1) * R + r + 1)
                    load(r, i)

        @block.tensor
        def _(pe):
            def chunk(r, i, first=False, last=False):
                pe.wait_ge(landed[r], (i + 1) * 16)
                for k in range(KD):
                    ins = pe.matmul(Y[:, k:k + 1, :], v[:, r, k * P:(k + 1) * P], act_buf[:, bass.ds(i * R + r, 1), :],
                                    start=(first and k % 2 == 0), stop=last, skip_group_check=True)
                ins.then_inc(done, 1)

            for r in range(R):
                chunk(r, 0, first=(r == 0))
            with pe.Fori(1, steps - 1) as i:
                for r in range(R):
                    chunk(r, i)
            for r in range(R):
                chunk(r, steps - 1, last=(r == R - 1))
            pe.wait_ge(copied, KD)
            for b in range(4):
                t, h = divmod(b, 2)
                for k in range(4):
                    ins = pe.transpose(T[:, b, k * P:(k + 1) * P], yT[:, 4 * h + k, t * P:(t + 1) * P], ident[:])
                ins.then_inc(turned, 1)

        @block.scalar
        def _(act):
            act.wait_ge(done, NKEYS)
            for k in range(KD):
                act.activation(yT[:, k, :], Y[:, k, :], ACT.Copy).then_inc(copied, 1)

        @block.vector
        def _(dve):
            for b in range(4):
                t, h = divmod(b, 2)
                dst = resid[:, 2 * half + t, h * BANK:(h + 1) * BANK]
                dve.wait_ge(turned, b + 1)
                dve.tensor_tensor(dst, T[:, b, :], dst, ALU.add).then_inc(added, 1)


def peer(nc, consts, resid, d):
    with Phase(nc, "peer") as ph:
        xT = ph.sb("xT", [P, KD, SEQ])
        e1T = ph.sb("e1T", [P, SEQ])
        e2T = ph.sb("e2T", [P, SEQ])
        gateT = ph.sb("gateT", [P, SEQ])
        norm_transpose(nc, "n2", consts, resid, xT, d["g_ffn"])
        with Phase(nc, "peerq") as ph2:
            qT = ph2.sb("qT", [P, PEER_H, SEQ])
            jobs = [(d["w_peer_q"][:, 512 * i:512 * (i + 1)], ("feat", ACT.Copy, [qT[:, 4 * i + j, :] for j in range(4)])) for i in range(2)]
            project(nc, "p2", xT, jobs, ring=2)
            peer_select(nc, consts, qT, d["peer_keys"], d["c_iota"], e1T, e2T, gateT)
        act_buf = ph.sb("act_buf", [P, NKEYS, HALF])
        for half in range(2):
            peer_up(nc, half, xT, d["peer_u"], act_buf)
            peer_gate(nc, half, d["c_iota"], e1T, e2T, gateT, act_buf)
            peer_down(nc, consts, half, d["peer_v"], act_buf, resid)


def first_mixer(nc, consts, resid, d):
    with Phase(nc, "m1") as ph:
        gates = ph.sb("gates", [P, 3, KD, SEQ])
        rgT, zaT, zrT = gates[:, 0], gates[:, 1], gates[:, 2]
        oT = ph.sb("oT", [P, 4, SEQ])
        cq = ph.sb("cq", [P, NT, MLA_QL])
        ckv = ph.sb("ckv", [P, 5, MLA_KVL + ROPE])
        with Phase(nc, "m1r") as ph2:
            rq = ph2.sb("rq", [P, NT, 512])
            rk = ph2.sb("rk", [P, 5, 512])
            rv = ph2.sb("rv", [P, 5, 1024])
            with Phase(nc, "m1h") as ph3:
                hT = ph3.sb("hT", [P, KD, KEYS])
                with Phase(nc, "m1x") as ph4:
                    meta = ph4.sb("meta", [META, D])
                    norm_transpose(nc, "n1", consts, resid, hT, d["g_mix"], meta=meta, load=(d["x"], d["meta"]))
                w = d["w_in"]
                x_tiles = lambda dst, a, b: [(P, t * P, dst[:, t, a:b]) for t in range(NT)]
                all_tiles = lambda dst, a, b: x_tiles(dst, a, b) + [(META, SEQ, dst[0:META, NT, a:b])]
                jobs, c = [], 0
                for n, out in ((MLA_QL, ("tok", x_tiles(cq, 0, MLA_QL))), (288, ("tok", all_tiles(ckv, 0, 288))),
                               (512, ("tok", x_tiles(rq, 0, 512))), (512, ("tok", all_tiles(rk, 0, 512))),
                               (512, ("tok", all_tiles(rv, 0, 512))), (512, ("tok", all_tiles(rv, 512, 1024)))):
                    jobs.append((w[:, c:c + n], out))
                    c += n
                for g, fn in ((rgT, ACT.Silu), (zaT, ACT.Sigmoid), (zrT, ACT.Sigmoid)):
                    for half in range(2):
                        jobs.append((w[:, c:c + 512], ("feat", fn, [g[:, 4 * half + j, :] for j in range(4)])))
                        c += 512
                project(nc, "p1", hT, jobs, ring=3)
            retention(nc, consts, rq, rk, rv, rgT, d["g_ret_gn"], d["c_decay"], d["c_decay_meta"], d["c_rope_ret"])
        with Phase(nc, "m1a") as ph2:
            qT = ph2.sb("qT", [QK, MLA_H, SEQ])
            kT = ph2.sb("kT", [QK, MLA_H, KEYS])
            v = ph2.sb("v", [P, 5, MLA_H * MLA_V])
            mla_prepare(nc, consts, cq, ckv, d["w_uq"], d["w_ukv"], d["g_q_lora"], d["g_kv_lora"], d["g_qk_q"], d["g_qk_k"],
                        d["c_rope_mla"], qT, kT, v)
            attention(nc, "at1", consts, lambda h: qT[:, h, :], lambda h: kT[:, h, :], v, v[0:META, NT, :], d["c_causal"],
                      META, QK ** -0.5, oT)
        merge(nc, oT, rgT, zaT, zrT, d["w_mla_out"], d["w_ret_out"])
        out_project(nc, "o1", zaT, d["w_mix_out"], KD, resid)


def modulation(nc, consts, c_dram, w_dram, b_dram, mod, rows):
    ident = consts["ident"]
    n = 6 * KD
    R = 4
    with Phase(nc, "ada") as ph:
        cond = ph.sb("cond", [P, D])
        bias = ph.sb("bias", [P, n])
        w = ph.sb("w", [P, R, D])
        junk = ph.sb("junk", [P, 2, D])
        wide = ph.sb("wide", [P, 2 * KD, P])
        T = ph.ps("T", [P, 4, BANK])
        landed = [ph.sem(f"landed{r}") for r in range(R)]
        loaded, active, summed, widened, turned, copied = (ph.sem(x) for x in ("loaded", "active", "summed", "widened", "turned", "copied"))
        block = ph.block()

        @block.sync
        def _(sp):
            sp.dma_start(cond[:], c_dram.partition_broadcast(P)).then_inc(loaded, 16)
            sp.dma_start(bias[:], b_dram).then_inc(loaded, 16)
            for j in range(n):
                if j >= R:
                    sp.wait_ge(summed, j - R + 1)
                sp.dma_start(w[:, j % R, :], w_dram[j * P:(j + 1) * P, :]).then_inc(landed[j % R], 16)

        @block.scalar
        def _(act):
            act.wait_ge(loaded, 32)
            act.activation(cond[:], cond[:], ACT.Silu).then_inc(active, 1)
            for b in range(4):
                act.wait_ge(turned, b + 1)
                act.activation(rows[:, b // 2, (b % 2) * BANK:(b % 2 + 1) * BANK], T[:, b, :], ACT.Copy).then_inc(copied, 1)

        @block.vector
        def _(dve):
            dve.wait_ge(active, 1)
            for j in range(n):
                dve.wait_ge(landed[j % R], 16 * (j // R + 1))
                if j >= 2:
                    dve.wait_ge(summed, j - 1)
                dve.tensor_tensor_reduce(junk[:, j % 2, :], w[:, j % R, :], cond[:], 1.0, 0.0, ALU.mult, ALU.add, mod[:, j:j + 1]).then_inc(summed, 1)
            dve.wait_ge(summed, n)
            dve.tensor_tensor(mod[:], mod[:], bias[:], ALU.add).then_inc(widened, 1)
            dve.wait_ge(widened, 1)
            dve.tensor_copy(wide[:, 0:KD, :], bc(mod[:, 2 * KD:3 * KD], 2, P))
            dve.tensor_copy(wide[:, KD:, :], bc(mod[:, 5 * KD:], 2, P)).then_inc(widened, 1)

        @block.tensor
        def _(pe):
            pe.wait_ge(widened, 2)
            for b in range(4):
                for k in range(4):
                    ins = pe.transpose(T[:, b, k * P:(k + 1) * P], wide[:, 4 * b + k, :], ident[:])
                ins.then_inc(turned, 1)


def dilated_prepare(nc, consts, aq, ak, gq_dram, gk_dram, qT, kT):
    ident = consts["ident"]
    H = DIL_H
    with Phase(nc, "dp") as ph:
        gain = ph.sb("gain", [P, 2])
        sq = ph.sb("sq", [P, 2, 512])
        ss8 = ph.sb("ss8", [P, 8, H])
        ms8 = ph.sb("ms8", [P, 8, H])
        rstd8 = ph.sb("rstd8", [P, 8, H])
        half = ph.sb("half", [P, H])
        T = ph.ps("T", [P, 2, BANK])
        names = ("loaded", "squared", "summed", "means", "roots", "normed", "turned", "copied", "pool_link")
        loaded, squared, summed, means, roots, normed, turned, copied, pool_link = (ph.sem(x) for x in names)
        jobs = [(src, c, t) for c, src in enumerate((aq, ak)) for t in range(NT)]
        block = ph.block()

        @block.sync
        def _(sp):
            sp.dma_start(gain[:, 0:1], gq_dram).then_inc(loaded, 16)
            sp.dma_start(gain[:, 1:2], gk_dram).then_inc(loaded, 16)

        @block.gpsimd
        def _(pool):
            link = Link(pool, pool_link)
            link(pool.memset(half[:], -0.5))
            for j in range(len(jobs)):
                pool.wait_ge(means, j + 1)
                pool.tensor_tensor(rstd8[:, j, :], ms8[:, j, :], half[:], ALU.pow).then_inc(roots, 1)

        @block.scalar
        def _(act):
            act.wait_ge(loaded, 32)
            for j in range(len(jobs) + 2):
                if j < len(jobs):
                    src, c, t = jobs[j]
                    if j >= 2:
                        act.wait_ge(summed, j - 1)
                    act.activation(sq[:, j % 2, :], src[:, t, :], ACT.Square).then_inc(squared, 1)
                if j >= 2:
                    src, c, t = jobs[j - 2]
                    act.wait_ge(turned, j - 1)
                    act.activation((qT, kT)[c][:, :, t * P:(t + 1) * P], T[:, j % 2, :].rearrange("p (c q) -> p c q", q=P), ACT.Copy,
                                   scale=gain[:, c:c + 1]).then_inc(copied, 1)

        @block.vector
        def _(dve):
            for j in range(len(jobs) + 1):
                if j < len(jobs):
                    dve.wait_ge(squared, j + 1)
                    dve.tensor_reduce(ss8[:, j, :], sq[:, j % 2, :].rearrange("p (h e) -> p h e", e=DIL_E), AX.X, ALU.add).then_inc(summed, 1)
                    dve.wait_ge(summed, j + 1)
                    dve.tensor_scalar(ms8[:, j, :], ss8[:, j, :], 1.0 / DIL_E, EPS, ALU.mult, ALU.add).then_inc(means, 1)
                if j >= 1:
                    src, c, t = jobs[j - 1]
                    x = src[:, t, :].rearrange("p (h e) -> p h e", e=DIL_E)
                    dve.wait_ge(roots, j)
                    dve.tensor_tensor(x, x, bc(rstd8[:, j - 1, :], 2, DIL_E), ALU.mult).then_inc(normed, 1)

        @block.tensor
        def _(pe):
            for j, (src, c, t) in enumerate(jobs):
                pe.wait_ge(normed, j + 1)
                if j >= 2:
                    pe.wait_ge(copied, j - 1)
                for k in range(4):
                    ins = pe.transpose(T[:, j % 2, k * P:(k + 1) * P], src[:, t, k * P:(k + 1) * P], ident[:])
                ins.then_inc(turned, 1)


def gla(nc, consts, qkT, v, lowT, grT, d, mixT):
    ident = consts["ident"]
    H, C = GLA_H, GLA_CHUNK
    NC = SEQ // C
    with Phase(nc, "gla") as ph:
        wg = ph.sb("wg", [GLA_RANK, 2, P])
        bg = ph.sb("bg", [P, 2])
        gn = ph.sb("gn", [P, 1])
        mask = ph.sb("mask", [P, P])
        keep = ph.sb("keep", [P, SEQ])
        absz = ph.sb("absz", [P, 2, SEQ])
        minz = ph.sb("minz", [P, 2, SEQ])
        b = ph.sb("b", [P, 2, SEQ])
        dm = ph.sb("dm", [P, 2, SEQ])
        dl = ph.sb("dl", [P, 2, SEQ])
        e1 = ph.sb("e1", [P, 2, SEQ])
        e2 = ph.sb("e2", [P, 2, SEQ])
        e3 = ph.sb("e3", [P, 2, SEQ])
        e4 = ph.sb("e4", [P, 2, SEQ])
        qe = ph.sb("qe", [P, 2, SEQ])
        klT = ph.sb("klT", [P, NT, 2 * P])
        st = ph.sb("st", [P, NC, 2, GLA_DV])
        sm = ph.sb("sm", [P, 2, H, P])
        junk = ph.sb("junk", [P, P])
        ssq = ph.sb("ssq", [P, NT, H])
        ms = ph.sb("ms", [P, NT, H])
        rstd = ph.sb("rstd", [P, NT, H])
        half = ph.sb("half", [P, H])
        on = ph.sb("on", [P, 2, H, P])
        S = ph.ps("S", [P, 2, BANK])
        O = ph.ps("O", [P, 2, BANK])
        U = ph.ps("U", [P, 4, BANK])
        names = ("loaded", "logits", "absed", "mined", "exped", "logged", "decays", "relative", "e1_done", "e2_done", "e3_done",
                 "e4_done", "kl_done", "ready", "turned", "copied", "updates", "stated", "scored", "masked", "attended",
                 "squares", "means", "roots", "normed", "oturned", "gated", "dve_link", "pool_link", "junked")
        (loaded, logits, absed, mined, exped, logged, decays, relative, e1_done, e2_done, e3_done, e4_done, kl_done, ready,
         turned, copied, updates, stated, scored, masked, attended, squares, means, roots, normed, oturned, gated,
         dve_link, pool_link, junked) = (ph.sem(x) for x in names)
        q, k = qkT[:, 0:2, :], qkT[:, 2:4, :]
        qm, km, kl = e2, e3, e4
        chunks = lambda x: x[:].rearrange("p c (n i) -> p (c n) i", i=C)
        head = lambda h: slice(64 * (h % 2), 64 * (h % 2) + 64)
        block = ph.block()

        @block.sync
        def _(sp):
            sp.dma_start(wg[:], d["gla_w_gate"].rearrange("r (c p) -> r c p", p=P)).then_inc(loaded, 16)
            sp.dma_start(bg[:], d["gla_b_gate"]).then_inc(loaded, 16)
            sp.dma_start(gn[:], d["gla_norm_g"]).then_inc(loaded, 16)
            sp.dma_start(mask[:], d["c_gla_mask"]).then_inc(loaded, 16)
            sp.dma_start(keep[:], d["c_scan_keep"]).then_inc(loaded, 16)

        @block.gpsimd
        def _(pool):
            link = Link(pool, pool_link)
            link(pool.memset(half[:], -0.5))
            for t in range(NT):
                pool.wait_ge(means, t + 1)
                pool.tensor_tensor(rstd[:, t, :], ms[:, t, :], half[:], ALU.pow).then_inc(roots, 1)

        @block.scalar
        def _(act):
            act.wait_ge(logits, 1)
            for c in range(2):
                ins = act.activation(absz[:, c, :], S[:, c, :], ACT.Abs, bias=bg[:, c:c + 1])
            ins.then_inc(absed, 1)
            act.wait_ge(absed, 1)
            act.activation(absz[:], absz[:], ACT.Exp, scale=-1.0).then_inc(exped, 1)
            act.wait_ge(exped, 1)
            act.activation(absz[:], absz[:], ACT.Ln, bias=1.0).then_inc(logged, 1)
            act.wait_ge(decays, 2)
            act.activation(e1[:], b[:], ACT.Exp, scale=1.0 / GLA_TAU).then_inc(e1_done, 1)
            act.wait_ge(relative, 1)
            act.activation(e4[:], dl[:], ACT.Exp, scale=1.0 / GLA_TAU).then_inc(e4_done, 1)
            act.wait_ge(relative, 2)
            act.activation(e2[:], dm[:], ACT.Exp, scale=1.0 / GLA_TAU).then_inc(e2_done, 1)
            act.activation(e3[:], dm[:], ACT.Exp, scale=-1.0 / GLA_TAU).then_inc(e3_done, 1)
            act.wait_ge(turned, 1)
            for i in range(2):
                ins = act.activation(klT[:, 2 * i:2 * i + 2, :], O[:, i, :].rearrange("p (t e) -> p t e", t=2), ACT.Copy)
            ins.then_inc(copied, 1)
            for t in range(NT):
                act.wait_ge(attended, t + 1)
                for h in range(H):
                    act.activation(junk[:], O[:, h % 2, (h // 2) * P:(h // 2 + 1) * P], ACT.Square, accum_out=ssq[:, t, h:h + 1]).then_inc(squares, 1)
                    act.wait_ge(squares, t * H + h + 1)

        @block.vector
        def _(dve):
            link = Link(dve, dve_link)
            dve.wait_ge(loaded, 80)
            dve.wait_ge(logits, 1)
            dve.wait_ge(absed, 1)
            for c in range(2):
                ins = dve.tensor_scalar(minz[:, c, :], S[:, c, :], bg[:, c:c + 1], 0.0, ALU.add, ALU.min)
            ins.then_inc(mined, 1)
            dve.wait_ge(mined, 1)
            dve.wait_ge(logged, 1)
            link(dve.tensor_tensor(minz[:], minz[:], absz[:], ALU.subtract))
            for c in range(2):
                dve.tensor_tensor_scan(b[:, c, :], keep[:], minz[:, c, :], 0.0, ALU.mult, ALU.add).then_inc(decays, 1)
            dve.wait_ge(decays, 2)
            dve.tensor_tensor(chunks(dl), bc(chunks(b)[:, :, C - 1], 2, C), chunks(b), ALU.subtract).then_inc(relative, 1)
            dve.tensor_tensor(chunks(dm), chunks(b), bc(chunks(b)[:, :, C // 2 - 1], 2, C), ALU.subtract).then_inc(relative, 1)
            dve.wait_ge(e4_done, 1)
            dve.tensor_tensor(kl[:], k, e4[:], ALU.mult).then_inc(kl_done, 1)
            dve.wait_ge(e1_done, 1)
            dve.scalar_tensor_tensor(qe[:].rearrange("p c t -> p (c t)"), q.rearrange("p c t -> p (c t)"), GLA_DK ** -0.5,
                                     e1[:].rearrange("p c t -> p (c t)"), ALU.mult, ALU.mult).then_inc(ready, 1)
            dve.wait_ge(e2_done, 1)
            dve.tensor_tensor(qm[:], q, e2[:], ALU.mult).then_inc(ready, 1)
            dve.wait_ge(e3_done, 1)
            dve.tensor_tensor(km[:], k, e3[:], ALU.mult).then_inc(ready, 1)
            link(dve.memset(st[:, 0], 0.0))
            dve.wait_ge(updates, 1)
            for n in range(1, NC):
                m = n - 1
                col = ((m // 2) % 2) * 2 * P
                for c in range(2):
                    up = U[:, (m % 2) * 2 + m // 4, col + c * P:col + (c + 1) * P]
                    ins = dve.scalar_tensor_tensor(st[:, n, c, :], st[:, m, c, :], e1[:, c, m * C + C - 1:m * C + C], up, ALU.mult, ALU.add)
                ins.then_inc(stated, 1)
                dve.wait_ge(stated, n)

            def mask_scores(t):
                dve.wait_ge(scored, t + 1)
                if t >= 2:
                    dve.wait_ge(attended, t - 1)
                for odd in range(2):
                    ins = dve.tensor_tensor(sm[:, t % 2, 2 * odd:2 * odd + 2, :], S[:, odd, 0:2 * P].rearrange("p (h i) -> p h i", i=P),
                                            bc(mask[:], 1, 2), ALU.mult)
                ins.then_inc(masked, 1)

            def norm(t):
                dve.wait_ge(squares, (t + 1) * H)
                dve.tensor_scalar(ms[:, t, :], ssq[:, t, :], 1.0 / GLA_DV, EPS, ALU.mult, ALU.add).then_inc(means, 1)
                dve.wait_ge(roots, t + 1)
                if t >= 2:
                    dve.wait_ge(oturned, t - 1)
                for h in range(H):
                    ins = dve.tensor_scalar(on[:, t % 2, h, :], O[:, h % 2, (h // 2) * P:(h // 2 + 1) * P], rstd[:, t, h:h + 1], None, ALU.mult)
                ins.then_inc(normed, 1)

            def gate(t):
                dve.wait_ge(oturned, t + 1)
                dve.scalar_tensor_tensor(mixT[:, 0:H, t * P:(t + 1) * P], U[:, t % 2, :].rearrange("p (h i) -> p h i", i=P), gn[:, 0:1],
                                         grT[:, :, t * P:(t + 1) * P], ALU.mult, ALU.mult).then_inc(gated, 1)

            for t in range(NT):
                mask_scores(t)
                norm(t)
                gate(t)

        @block.tensor
        def _(pe):
            pe.wait_ge(loaded, 80)
            for c in range(2):
                ins = pe.matmul(S[:, c, :], wg[:, c, :], lowT[0:GLA_RANK, :], start=True, stop=True)
            ins.then_inc(logits, 1)
            pe.wait_ge(kl_done, 1)
            for t in range(NT):
                for c in range(2):
                    ins = pe.transpose(O[:, t // 2, (t % 2) * 2 * P + c * P:(t % 2) * 2 * P + (c + 1) * P], kl[:, c, t * P:(t + 1) * P], ident[:])
            ins.then_inc(turned, 1)
            pe.wait_ge(copied, 1)
            for n in range(NC - 1):
                r = slice(64 * (n % 2), 64 * (n % 2) + 64)
                col = ((n // 2) % 2) * 2 * P
                for h in range(H):
                    c0 = col + (h // 2) * P
                    ins = pe.matmul(U[head(h), (n % 2) * 2 + n // 4, c0:c0 + P], klT[r, n // 2, 64 * h:64 * h + 64],
                                    v[r, n // 2, h * P:(h + 1) * P], start=True, stop=True)
            ins.then_inc(updates, 1)
            pe.wait_ge(ready, 3)
            pe.wait_ge(mined, 1)

            def score(t):
                if t >= 1:
                    pe.wait_ge(masked, t)
                for h in range(H):
                    ins = pe.matmul(S[:, h % 2, (h // 2) * P:(h // 2 + 1) * P], km[head(h), h // 2, t * P:(t + 1) * P],
                                    qm[head(h), h // 2, t * P:(t + 1) * P], start=True, stop=True)
                ins.then_inc(scored, 1)

            def attend(t):
                pe.wait_ge(masked, t + 1)
                if t >= 1:
                    pe.wait_ge(normed, t)
                pe.wait_ge(stated, min(2 * t + 1, NC - 1))
                for h in range(H):
                    cols = slice((h // 2) * P, (h // 2 + 1) * P)
                    pe.matmul(O[:, h % 2, cols], sm[:, t % 2, 2 * (h % 2) + h // 2, :], v[:, t, h * P:(h + 1) * P], start=True, stop=True)
                    for n in (2 * t, 2 * t + 1):
                        r = slice(64 * (n % 2), 64 * (n % 2) + 64)
                        ins = pe.matmul(O[r, h % 2, cols], qe[head(h), h // 2, n * C:(n + 1) * C], st[head(h), n, h // 2, :],
                                        start=False, stop=False, skip_group_check=True)
                ins.then_inc(attended, 1)

            def turn(t):
                pe.wait_ge(normed, t + 1)
                if t >= 2:
                    pe.wait_ge(gated, t - 1)
                if t == 0:
                    pe.wait_ge(stated, NC - 1)
                for h in range(H):
                    ins = pe.transpose(U[:, t % 2, h * P:(h + 1) * P], on[:, t % 2, h, :], ident[:])
                ins.then_inc(oturned, 1)

            for t in range(NT):
                score(t)
                attend(t)
                turn(t)


def ffn_up(nc, hT, w_dram, cw_dram, cb_dram, gT):
    R = 2
    steps = NF // R
    with Phase(nc, "ffn") as ph:
        w = ph.sb("w", [P, R, 2, KD, P])
        cw = ph.sb("cw", [P, NF * 6])
        cb = ph.sb("cb", [P, NF * 2])
        u = ph.sb("u", [P, R, 2, SEQ])
        sl = ph.sb("sl", [P, R, SEQ])
        acc = ph.ps("acc", [P, 2 * R, BANK])
        landed = [ph.sem(f"landed{r}") for r in range(R)]
        names = ("loaded", "done", "biased", "tap1", "conved", "silued", "out")
        loaded, done, biased, tap1, conved, silued, out = (ph.sem(x) for x in names)
        block = ph.block()

        @block.sync
        def _(sp):
            def load(r, i):
                sp.dma_start(w[:, r], w_dram[bass.ds(i * R + r, 1)].rearrange("o p g k n -> (o p) g k n")).then_inc(landed[r], 16)

            sp.dma_start(cw[:], cw_dram.rearrange("p i g j -> p (i g j)")).then_inc(loaded, 16)
            sp.dma_start(cb[:], cb_dram.rearrange("p i g -> p (i g)")).then_inc(loaded, 16)
            for r in range(R):
                load(r, 0)
            with sp.Fori(1, steps) as i:
                for r in range(R):
                    sp.wait_ge(done, (i - 1) * R + r + 1)
                    load(r, i)

        @block.tensor
        def _(pe):
            def chunk(r, i):
                pe.wait_ge(landed[r], (i + 1) * 16)
                for g in range(2):
                    for k in range(KD):
                        ins = pe.matmul(acc[:, 2 * r + g, :], w[:, r, g, k, :], hT[:, k, :], start=(k == 0), stop=(k == KD - 1))
                ins.then_inc(done, 1)

            for r in range(R):
                chunk(r, 0)
            with pe.Fori(1, steps) as i:
                for r in range(R):
                    pe.wait_ge(conved, (i - 1) * R + r + 1)
                    chunk(r, i)

        @block.scalar
        def _(act):
            def chunk(r, i, first=False):
                c = i * R + r
                if not first:
                    act.wait_ge(out, c - R + 1)
                act.wait_ge(done, c + 1)
                for g in range(2):
                    ins = act.activation(u[:, r, g, :], acc[:, 2 * r + g, :], ACT.Identity, bias=cb[:, bass.ds(c * 2 + g, 1)],
                                         scale=cw[:, bass.ds(c * 6 + g * 3 + 2, 1)])
                ins.then_inc(biased, 1)
                act.wait_ge(conved, c + 1)
                act.activation(sl[:, r, :], u[:, r, 0, :], ACT.Silu).then_inc(silued, 1)

            act.wait_ge(loaded, 32)
            for r in range(R):
                chunk(r, 0, first=True)
            with act.Fori(1, steps) as i:
                for r in range(R):
                    chunk(r, i)

        @block.vector
        def _(dve):
            dve.wait_ge(loaded, 32)
            with dve.Fori(0, steps) as i:
                for r in range(R):
                    c = i * R + r
                    dve.wait_ge(biased, c + 1)
                    for j, s in ((1, tap1), (0, conved)):
                        lag = 2 - j
                        for g in range(2):
                            ins = dve.scalar_tensor_tensor(u[:, r, g, lag:], acc[:, 2 * r + g, 0:SEQ - lag], cw[:, bass.ds(c * 6 + g * 3 + j, 1)],
                                                           u[:, r, g, lag:], ALU.mult, ALU.add)
                        ins.then_inc(s, 1)
                        if j == 1:
                            dve.wait_ge(tap1, c + 1)
                    dve.wait_ge(conved, c + 1)
                    dve.wait_ge(silued, c + 1)
                    dve.tensor_tensor(gT[:, bass.ds(c, 1), :], sl[:, r:r + 1, :], u[:, r, 1:2, :], ALU.mult).then_inc(out, 1)


def second_block(nc, consts, resid, d, out, stop):
    with Phase(nc, "m2") as ph:
        mod = ph.sb("mod", [P, 6 * KD])
        rows = ph.sb("rows", [P, 2, D])
        part = lambda i: mod[:, i * KD:(i + 1) * KD]
        modulation(nc, consts, d["c"], d["w_ada"], d["b_ada"], mod, rows)
        with Phase(nc, "m2m") as ph2:
            mixT = ph2.sb("mixT", [P, KD, SEQ])
            aq, ak, av = (ph2.sb(n, [P, NT, 512]) for n in ("aq", "ak", "av"))
            with Phase(nc, "m2g") as ph3:
                qkT = ph3.sb("qkT", [P, 4, SEQ])
                gv = ph3.sb("gv", [P, NT, 512])
                grT = ph3.sb("grT", [P, 4, SEQ])
                lowT = ph3.sb("lowT", [GLA_RANK, SEQ])
                with Phase(nc, "m2h") as ph4:
                    hT = ph4.sb("hT", [P, KD, SEQ])
                    norm_transpose(nc, "n3", consts, resid, hT, d["norm1_g"], mod=(part(1), part(0)))
                    tok = lambda dst: ("tok", [(P, t * P, dst[:, t, :]) for t in range(NT)])
                    feat = lambda fn, dst: ("feat", fn, [dst[:, j, :] for j in range(4)])
                    jobs, c = [], 0
                    for n, o in ((512, feat(ACT.Copy, qkT)), (512, tok(gv)), (512, feat(ACT.Silu, grT)),
                                 (GLA_RANK, ("feat", ACT.Copy, [lowT[:, :]])), (512, tok(aq)), (512, tok(ak)), (512, tok(av))):
                        jobs.append((d["w_in_2"][:, c:c + n], o))
                        c += n
                    project(nc, "p3", hT, jobs, ring=3)
                gla(nc, consts, qkT, gv, lowT, grT, d, mixT)
            with Phase(nc, "m2a") as ph3:
                qT = ph3.sb("qT", [P, 4, SEQ])
                kT = ph3.sb("kT", [P, 4, SEQ])
                dilated_prepare(nc, consts, aq, ak, d["q_norm_g"], d["k_norm_g"], qT, kT)
                at = lambda x: lambda h: x[64 * (h % 2):64 * (h % 2) + 64, h // 2, :]
                attention(nc, "at2", consts, at(qT), at(kT), av, None, d["c_dilated"], 0, DIL_E ** -0.5, mixT[:, 4:8, :])
            out_project(nc, "o2", mixT, d["w_out_2"], KD, resid, gate=rows[:, 0, :])
        if stop == 3:
            return
        gT = ph.sb("gT", [P, NF, SEQ])
        with Phase(nc, "m2f") as ph2:
            hT = ph2.sb("hT", [P, KD, SEQ])
            norm_transpose(nc, "n4", consts, resid, hT, d["norm2_g"], mod=(part(4), part(3)))
            ffn_up(nc, hT, d["w_up"], d["conv_w"], d["conv_b"], gT)
        out_project(nc, "o3", gT, d["w_down"], NF, resid, gate=rows[:, 1, :], out_dram=out)


def program(nc, d, out, stop=9):
    with Phase(nc, "all") as ph:
        resid = ph.sb("resid", [P, NT, D])
        ident = ph.sb("ident", [P, P])
        consts = {"ident": ident}
        with Phase(nc, "c") as ph2:
            s = ph2.sem("consts")
            block = ph2.block()

            @block.sync
            def _(sp):
                sp.dma_start(ident[:], d["c_ident"]).then_inc(s, 16)
                sp.wait_ge(s, 16)
        first_mixer(nc, consts, resid, d)
        if stop > 1:
            peer(nc, consts, resid, d)
        if stop > 2:
            second_block(nc, consts, resid, d, out, stop)
        if stop < 4:
            with Phase(nc, "dump") as ph2:
                s = ph2.sem("dumped")
                block = ph2.block()

                @block.sync
                def _(sp):
                    sp.dma_start(out.rearrange("(t p) n -> p t n", p=P), resid[:]).then_inc(s, 16)
                    sp.wait_ge(s, 16)


def lay_out(inputs):
    a = {k: np.asarray(v) for k, v in inputs.items()}
    cols = lambda g: np.ascontiguousarray(g.reshape(-1, P).T)
    o = {"x": a["x"][0], "meta": a["meta_tokens"]}
    for n in ("w_in", "w_uq", "w_ukv", "w_mla_out", "w_ret_out", "w_mix_out", "w_peer_q"):
        o[n] = a[n][0]
    for n in ("g_mix", "g_q_lora", "g_kv_lora", "g_ret_gn", "g_ffn"):
        o[n] = cols(a[n][0])
    o["g_qk_q"], o["g_qk_k"] = a["g_qk_q"][0], a["g_qk_k"][0]
    o["peer_keys"] = np.concatenate([a["peer_keys_1"][0].T, a["peer_keys_2"][0].T], 0)
    o["peer_u"] = a["peer_u"][0].reshape(P, P, KD, P).transpose(1, 3, 2, 0)
    o["peer_v"] = a["peer_v"][0].reshape(P, P, D)
    o["c"] = a["c_2"][0]
    o["w_ada"] = a["w_ada_2"][0].T
    o["b_ada"] = cols(a["b_ada_2"][0])
    for n in ("norm1_g", "norm2_g"):
        o[n] = cols(a[n + "_2"][0])
    o["w_in_2"], o["w_out_2"], o["w_down"] = a["w_in_2"][0], a["w_out_2"][0], a["w_down_2"][0]
    o["gla_w_gate"], o["gla_b_gate"] = a["gla_w_gate_2"][0], cols(a["gla_b_gate_2"][0])
    o["gla_norm_g"] = cols(a["gla_norm_g_2"][0])
    o["q_norm_g"] = cols(np.concatenate([a["q_norm_g_2"][0]] * 2))
    o["k_norm_g"] = cols(np.concatenate([a["k_norm_g_2"][0]] * 2))
    o["w_up"] = a["w_up_2"][0].reshape(KD, P, 2, NF, P).transpose(3, 1, 2, 0, 4)
    o["conv_w"] = a["conv_w_2"][0].reshape(3, 2, NF, P).transpose(3, 2, 1, 0)
    o["conv_b"] = a["conv_b_2"][0].reshape(2, NF, P).transpose(2, 1, 0)
    o.update(shape_constants())
    return {k: np.ascontiguousarray(v) for k, v in o.items()}


def build(nc, arrays, stop=9):
    d = {n: nc.dram_tensor(f"in_{n}", a.shape, mybir.dt.from_np(a.dtype), kind="ExternalInput").ap() for n, a in arrays.items()}
    out = nc.dram_tensor("out", (SEQ, D), F32, kind="ExternalOutput").ap()
    program(nc, d, out, stop)


def kernel(**inputs):
    import concourse.bacc as bacc
    from concourse.bass_utils import run_bass_kernel_spmd

    arrays = lay_out(inputs)
    nc = bacc.Bacc("TRN2", target_bir_lowering=False, num_devices=1)
    build(nc, arrays)
    r = run_bass_kernel_spmd(nc, [{f"in_{n}": a for n, a in arrays.items()}], core_ids=[0])
    return r.results[0]["out"].reshape(1, SEQ, D)
```

```python
from contextlib import ExitStack

import numpy as np
import concourse.bass as bass
from concourse import mybir
from concourse.alu_op_type import AluOpType as ALU

ACT = mybir.ActivationFunctionType
AX = mybir.AxisListType
F32 = mybir.dt.float32
F32R = mybir.dt.float32r
U32 = mybir.dt.uint32

P = 128
D = 1024
KD = D // P
SEQ = 512
NT = SEQ // P
META = 16
KEYS = SEQ + META
EPS = 1e-6
NEG = -1e30
BANK = 512

MLA_H, MLA_QL, MLA_KVL, NOPE, ROPE, MLA_V = 8, 384, 256, 64, 32, 64
QK = NOPE + ROPE
RET_H, RET_DK, RET_DV = 8, 64, 128
PEER_H, NKEYS, TOPK = 8, 128, 16
PICKS = PEER_H * TOPK
HALF = SEQ // 2
GLA_H, GLA_DK, GLA_DV, GLA_CHUNK, GLA_RANK, GLA_TAU = 4, 64, 128, 64, 16, 16.0
DIL_H, DIL_E = 8, 64
DFF = 2816
NF = DFF // P


def shape_constants():
    out = {}
    pos = np.concatenate([META + np.arange(SEQ), np.arange(META)]).astype(np.float32)

    def rope_table(half, heads_dim):
        inv = (10000.0 ** (-np.arange(half, dtype=np.float32) / half)).astype(np.float32)
        ang = pos[:, None] * inv[None, :]
        c, s = np.cos(ang), np.sin(ang)
        full = np.zeros((5 * P, 2, 2 * half), np.float32)
        full[:KEYS, 0] = np.concatenate([c, c], 1)
        full[:KEYS, 1] = np.concatenate([-s, s], 1)
        return full.reshape(5, P, 2, 2 * half).transpose(1, 0, 2, 3).copy()

    out["c_rope_ret"] = rope_table(RET_DK // 2, RET_DK)
    out["c_rope_mla"] = rope_table(ROPE // 2, ROPE)
    p = np.arange(P)[:, None].astype(np.float64)
    gamma = 1.0 - 2.0 ** (-5.0 - np.arange(RET_H))
    c = np.arange(SEQ)[None, :].astype(np.float64)
    diff = c - p
    dec = np.where(diff >= 0, gamma[:, None, None] ** np.maximum(diff, 0)[None], 0.0)
    out["c_decay"] = (dec * RET_DK ** -0.5).transpose(1, 0, 2).astype(np.float32).copy()
    dm = META + c - p[:META]
    out["c_decay_meta"] = (gamma[:, None, None] ** dm[None] * RET_DK ** -0.5).transpose(1, 0, 2).astype(np.float32).copy()
    col = np.arange(KEYS)[None, :]
    delta = META + 3 * P + p - col
    out["c_causal"] = np.where(delta >= 0, 0.0, NEG).astype(np.float32)[:, None, :].copy()
    delta = 3 * P + p - np.arange(SEQ)[None, :]
    mult = (delta <= 128).astype(int) + (delta % 4 == 0) + (delta % 16 == 0)
    scale = DIL_E ** -0.5
    bias = []
    for h in range(DIL_H):
        slope = 2.0 ** (-8.0 * (h + 1) / DIL_H)
        b = (-slope * delta + np.log(np.maximum(mult, 1))) / scale
        bias.append(np.where((delta >= 0) & (mult > 0), b, NEG))
    out["c_dilated"] = np.stack(bias, 1).astype(np.float32)
    j, i = np.arange(P)[:, None], np.arange(P)[None, :]
    out["c_gla_mask"] = np.where((j <= i) & (j // GLA_CHUNK == i // GLA_CHUNK), GLA_DK ** -0.5, 0.0).astype(np.float32)
    keep = np.ones((P, SEQ), np.float32)
    keep[:, ::GLA_CHUNK] = 0.0
    out["c_scan_keep"] = keep
    out["c_ident"] = np.eye(P, dtype=np.float32)
    out["c_iota"] = np.tile(np.arange(P, dtype=np.float32), (P, 1))
    return out


class Link:

    def __init__(self, engine, sem):
        self.engine, self.sem, self.n = engine, sem, 0

    def __call__(self, ins):
        ins.then_inc(self.sem, 1)
        self.n += 1
        self.engine.wait_ge(self.sem, self.n)


class Phase:

    KEEP = 90
    past = []

    def __init__(self, nc, name):
        self.nc, self.name, self.stack, self.sems = nc, name, ExitStack(), []

    def __enter__(self):
        return self

    def __exit__(self, *a):
        self.stack.__exit__(*a)
        Phase.past.extend(self.sems)
        if len(Phase.past) > Phase.KEEP:
            self.nc.clear_and_free_semaphores(Phase.past)
            self.nc.all_engine_barrier(sem_only=True)
            Phase.past = []

    def sb(self, name, shape, dt=F32):
        return self.stack.enter_context(self.nc.sbuf_tensor(f"{self.name}_{name}", list(shape), dt))

    def ps(self, name, shape, dt=F32):
        return self.stack.enter_context(self.nc.psum_tensor(f"{self.name}_{name}", list(shape), dt))

    def sem(self, name):
        self.sems.append(self.nc.alloc_semaphore(name=f"{self.name}_{name}"))
        return self.sems[-1]

    def block(self):
        return self.stack.enter_context(self.nc.Block())


def bc(ap, axis, n):
    v = ap.unsqueeze(axis)
    shape = list(v.shape)
    shape[axis] = n
    return v.to_broadcast(shape)


class Early:

    def __init__(self, raw, loads):
        self.raw, self.loads = raw, loads(raw)


class Tables:

    def __init__(self, ph, **tables):
        self.tiles = {name: ph.sb(name, shape) for name, (shape, _) in tables.items()}
        self.loads = [(self.tiles[name][:], src) for name, (_, src) in tables.items()]

    def __getitem__(self, name):
        return self.tiles[name]


def load_early(sp, sem, early):
    loads = [x for e in early for x in e.loads]
    for dst, src in loads:
        sp.dma_start(dst, src).then_inc(sem, 16)
    if loads:
        sp.wait_ge(sem, 16 * len(loads))


def norm_transpose(nc, name, consts, resid, hs, gain_dram, meta=None, mod=None, load=None, tokens=range(NT), early=()):
    ident = consts["ident"]
    with Phase(nc, name) as ph:
        gain = ph.sb("gain", [P, KD])
        shift = ph.sb("shift", [P, KD])
        fac = ph.sb("fac", [P, KD])
        ssq = ph.sb("ssq", [P, 5])
        ms = ph.sb("ms", [P, 5])
        rstd = ph.sb("rstd", [P, 5])
        half = ph.sb("half", [P, 5])
        junk = ph.ps("junk", [P, D])
        xn = ph.sb("xn", [P, 2, D])
        whole = ph.sb("whole", [P, 2, KD, P])
        tp = ph.ps("tp", [P, 4, BANK])
        loaded = [ph.sem(f"loaded{t}") for t in range(NT + 1)]
        early_landed, gained, sums, means, roots, scaled, turned = (
            ph.sem(n) for n in ("early_landed", "gained", "sums", "means", "roots", "scaled", "turned"))
        act_out, dve_out, hi_made, lo_made, ready, dve_link, pool_link = (
            ph.sem(n) for n in ("act_out", "dve_out", "hi_made", "lo_made", "ready", "dve_link", "pool_link"))
        tiles = [(t, P, i * P) for i, t in enumerate(tokens)] + ([(NT, META, SEQ)] if meta is not None else [])
        src = lambda t, rows: resid[:, t, :] if t < NT else meta[0:META, :]
        block = ph.block()

        @block.sync
        def _(sp):
            sp.dma_start(gain[:], gain_dram).then_inc(gained, 16)
            if load is not None:
                x_dram, meta_dram = load
                for t in range(NT):
                    sp.dma_start(resid[:, t, :], x_dram[t * P:(t + 1) * P, :]).then_inc(loaded[t], 16)
                sp.dma_start(meta[0:META, :], meta_dram).then_inc(loaded[NT], 16)
            load_early(sp, early_landed, early)

        @block.scalar
        def _(act):
            for i, (t, rows, col) in enumerate(tiles):
                if load is not None:
                    act.wait_ge(loaded[t], 16)
                act.activation(junk[0:rows, :], src(t, rows), ACT.Square, accum_out=ssq[0:rows, t:t + 1]).then_inc(sums, 1)
                act.wait_ge(sums, i + 1)
            act.wait_ge(ready, 1)
            for i, (t, rows, col) in enumerate(tiles):
                act.wait_ge(turned, 2 * i + 1)
                if i >= 2:
                    act.wait_ge(lo_made, i - 1)
                for k in range(4):
                    ins = act.activation(whole[:, i % 2, k, 0:rows], tp[:, (2 * i) % 4, k * P:k * P + rows], ACT.Identity,
                                         bias=shift[:, k:k + 1], scale=fac[:, k:k + 1])
                ins.then_inc(act_out, 1)
                act.wait_ge(act_out, i + 1)
                act.wait_ge(dve_out, i + 1)
                act.activation(hs[:, 0, :, col:col + rows], whole[:, i % 2, :, 0:rows], ACT.Copy).then_inc(hi_made, 1)

        @block.gpsimd
        def _(pool):
            link = Link(pool, pool_link)
            link(pool.memset(half[:], -0.5))

            def split(i):
                t, rows, col = tiles[i]
                pool.wait_ge(hi_made, i + 1)
                pool.tensor_tensor(hs[:, 1, :, col:col + rows], whole[:, i % 2, :, 0:rows],
                                   hs[:, 0, :, col:col + rows].bitcast(F32), ALU.subtract).then_inc(lo_made, 1)

            for i, (t, rows, col) in enumerate(tiles):
                if i >= 3:
                    split(i - 3)
                pool.wait_ge(means, i + 1)
                pool.tensor_tensor(rstd[0:rows, t:t + 1], ms[0:rows, t:t + 1], half[0:rows, t:t + 1], ALU.pow).then_inc(roots, 1)
            for i in range(max(0, len(tiles) - 3), len(tiles)):
                split(i)

        @block.vector
        def _(dve):
            link = Link(dve, dve_link)
            dve.wait_ge(gained, 16)
            if mod is None:
                link(dve.memset(shift[:], 0.0))
                dve.tensor_copy(fac[:], gain[:]).then_inc(ready, 1)
            else:
                sc, sh = mod
                link(dve.tensor_copy(shift[:], sh))
                dve.scalar_tensor_tensor(fac[:], sc, 1.0, gain[:], ALU.add, ALU.mult).then_inc(ready, 1)
            dve.wait_ge(ready, 1)
            n = len(tiles)
            for i in range(n + 1):
                if i < n:
                    t, rows, col = tiles[i]
                    dve.wait_ge(sums, i + 1)
                    dve.tensor_scalar(ms[0:rows, t:t + 1], ssq[0:rows, t:t + 1], 1.0 / D, EPS, ALU.mult, ALU.add).then_inc(means, 1)
                    dve.wait_ge(roots, i + 1)
                    if i >= 2:
                        dve.wait_ge(turned, 2 * (i - 1))
                    dve.tensor_scalar(xn[0:rows, i % 2, :], src(t, rows), rstd[0:rows, t:t + 1], None, ALU.mult).then_inc(scaled, 1)
                if i >= 1:
                    t, rows, col = tiles[i - 1]
                    dve.wait_ge(turned, 2 * i)
                    if i >= 3:
                        dve.wait_ge(lo_made, i - 2)
                    for k in range(4):
                        ins = dve.tensor_scalar(whole[:, (i - 1) % 2, 4 + k, 0:rows], tp[:, (2 * i - 1) % 4, k * P:k * P + rows],
                                                fac[:, 4 + k:5 + k], shift[:, 4 + k:5 + k], ALU.mult, ALU.add)
                    ins.then_inc(dve_out, 1)

        @block.tensor
        def _(pe):
            for i, (t, rows, col) in enumerate(tiles):
                pe.wait_ge(scaled, i + 1)
                if i >= 2:
                    pe.wait_ge(act_out, i - 1)
                for k in range(4):
                    ins = pe.transpose(tp[:, (2 * i) % 4, k * P:k * P + rows], xn[0:rows, i % 2, k * P:(k + 1) * P], ident[0:rows, 0:rows])
                ins.then_inc(turned, 1)
                if i >= 2:
                    pe.wait_ge(dve_out, i - 1)
                for k in range(4, 8):
                    ins = pe.transpose(tp[:, (2 * i + 1) % 4, (k - 4) * P:(k - 4) * P + rows], xn[0:rows, i % 2, k * P:(k + 1) * P], ident[0:rows, 0:rows])
                ins.then_inc(turned, 1)


def project_loads(jobs):
    wd = jobs[0][0]
    return lambda raw: [(raw[:, k, 0:wd.shape[1]], wd[k * P:(k + 1) * P, :]) for k in range(KD)]


def project(nc, name, hs, jobs, ring, early=()):
    RAW, CUT, AHEAD = KD, 4, 3
    with Phase(nc, name) as ph:
        raw = ring.raw
        cut = ph.sb("cut", [P, CUT, 2, BANK], F32R)
        acc = ph.ps("acc", [P, 8, BANK])
        landed = [ph.sem(f"landed{i}") for i in range(RAW)]
        early_landed, hi_made, lo_made, used, done, tok_out, feat_out = (
            ph.sem(n) for n in ("early_landed", "hi_made", "lo_made", "used", "done", "tok_out", "feat_out"))
        units = [(i, k) for i in range(len(jobs)) for k in range(KD)]
        outs = [(o[1] if o[0] == "tok" else o[2]) for _, o in jobs]
        first_out = np.cumsum([0] + [len(o) for o in outs]).tolist()
        left, n_tok, n_feat = [], 0, 0
        for i, (_, o) in enumerate(jobs):
            for _ in outs[i]:
                if o[0] == "tok":
                    n_tok += 1
                    left.append((tok_out, n_tok))
                else:
                    n_feat += 1
                    left.append((feat_out, n_feat))

        def freed(u):
            i, k = units[u]
            return (used, i * (KD - 1) + k + 1) if k < KD - 1 else (done, first_out[i + 1])

        block = ph.block()

        @block.sync
        def _(sp):
            for u, (i, k) in enumerate(units):
                if u < RAW:
                    continue
                sp.wait_ge(lo_made, u - RAW + 1)
                wd = jobs[i][0]
                sp.dma_start(raw[:, u % RAW, 0:wd.shape[1]], wd[k * P:(k + 1) * P, :]).then_inc(landed[u % RAW], 16)
            load_early(sp, early_landed, early)

        @block.tensor
        def _(pe):
            for u, (i, k) in enumerate(units):
                wd, out = jobs[i]
                n = wd.shape[1]
                hi, lo = cut[:, u % CUT, 0], cut[:, u % CUT, 1]
                pe.wait_ge(lo_made, u + 1)
                for j, dst in enumerate(outs[i]):
                    o = first_out[i] + j
                    if k == 0 and o >= 8:
                        pe.wait_ge(*left[o - 8])
                    first, last = k == 0, k == KD - 1
                    if out[0] == "tok":
                        rows, col, _ = dst
                        bank = acc[0:rows, o % 8, 0:n]
                        pe.matmul(bank, hs[:, 0, k, col:col + rows], hi[:, 0:n], start=first, stop=False)
                        pe.matmul(bank, hs[:, 0, k, col:col + rows], lo[:, 0:n], start=False, stop=False)
                        ins = pe.matmul(bank, hs[:, 1, k, col:col + rows], hi[:, 0:n], start=False, stop=last)
                    else:
                        c = slice(j * P, min((j + 1) * P, n))
                        bank = acc[0:c.stop - c.start, o % 8, :]
                        pe.matmul(bank, hi[:, c], hs[:, 0, k, 0:SEQ], start=first, stop=False)
                        pe.matmul(bank, hi[:, c], hs[:, 1, k, 0:SEQ], start=False, stop=False)
                        ins = pe.matmul(bank, lo[:, c], hs[:, 0, k, 0:SEQ], start=False, stop=last)
                    if last:
                        ins.then_inc(done, 1)
                if k < KD - 1:
                    ins.then_inc(used, 1)

        @block.vector
        def _(dve):
            def copy_out(i):
                wd, out = jobs[i]
                if out[0] == "tok":
                    for j, (rows, col, dst) in enumerate(outs[i]):
                        o = first_out[i] + j
                        dve.wait_ge(done, o + 1)
                        dve.tensor_copy(dst, acc[0:rows, o % 8, 0:wd.shape[1]]).then_inc(tok_out, 1)

            for u, (i, k) in enumerate(units):
                n = jobs[i][0].shape[1]
                if k == AHEAD and i >= 1:
                    copy_out(i - 1)
                dve.wait_ge(hi_made, u + 1)
                dve.tensor_tensor(cut[:, u % CUT, 1, 0:n], raw[:, u % RAW, 0:n], cut[:, u % CUT, 0, 0:n].bitcast(F32),
                                  ALU.subtract).then_inc(lo_made, 1)
            copy_out(len(jobs) - 1)

        @block.scalar
        def _(act):
            def copy_out(i):
                out = jobs[i][1]
                if out[0] == "feat":
                    for j, dst in enumerate(outs[i]):
                        o = first_out[i] + j
                        act.wait_ge(done, o + 1)
                        act.activation(dst, acc[0:dst.shape[0], o % 8, :], out[1]).then_inc(feat_out, 1)

            for u, (i, k) in enumerate(units):
                n = jobs[i][0].shape[1]
                if k == AHEAD and i >= 1:
                    copy_out(i - 1)
                if u >= RAW:
                    act.wait_ge(landed[u % RAW], 16 * (u // RAW))
                if u >= CUT:
                    act.wait_ge(*freed(u - CUT))
                act.activation(cut[:, u % CUT, 0, 0:n], raw[:, u % RAW, 0:n], ACT.Copy).then_inc(hi_made, 1)
            copy_out(len(jobs) - 1)


def out_loads(w_dram):
    return lambda raw: [(raw[:, r, :], w_dram[r * P:(r + 1) * P, :]) for r in range(2)]


def out_project(nc, name, actT, w_dram, kchunks, resid, ring, gate=None, out_dram=None):
    R = 2
    steps = kchunks // R
    with Phase(nc, name) as ph:
        raw = ring.raw
        wcut = ph.sb("wcut", [P, R, 2, D], F32R)
        acut = ph.sb("acut", [P, R, 2, SEQ], F32R)
        tmp = ph.sb("tmp", [P, 2, BANK])
        acc = ph.ps("acc", [P, 8, BANK])
        landed = [ph.sem(f"landed{i}") for i in range(R)]
        hi_made, lo_made, used, done, gated, added, stored = (
            ph.sem(n) for n in ("hi_made", "lo_made", "used", "done", "gated", "added", "stored"))
        block = ph.block()

        @block.sync
        def _(sp):
            def load(r, i):
                sp.dma_start(raw[:, r, :], w_dram[bass.ds((i * R + r) * P, P), :]).then_inc(landed[r], 16)

            with sp.Fori(1, steps) as i:
                for r in range(R):
                    sp.wait_ge(lo_made, (i - 1) * R + r + 1)
                    load(r, i)
            if out_dram is not None:
                for t in range(NT):
                    sp.wait_ge(added, 2 * (t + 1))
                    sp.dma_start(out_dram[t * P:(t + 1) * P, :], resid[:, t, :]).then_inc(stored, 16)
                sp.wait_ge(stored, 16 * NT)

        @block.scalar
        def _(act):
            def split(r, i, first=False):
                if not first:
                    act.wait_ge(landed[r], i * 16)
                    act.wait_ge(used, (i - 1) * R + r + 1)
                act.activation(acut[:, r, 0:1, :], actT[:, bass.ds(i * R + r, 1), :], ACT.Copy)
                act.activation(wcut[:, r, 0, :], raw[:, r, :], ACT.Copy).then_inc(hi_made, 1)

            for r in range(R):
                split(r, 0, first=True)
            with act.Fori(1, steps) as i:
                for r in range(R):
                    split(r, i)

        @block.tensor
        def _(pe):
            def chunk(r, i, first=False, last=False):
                pe.wait_ge(lo_made, i * R + r + 1)
                for t in range(NT):
                    rows = slice(t * P, (t + 1) * P)
                    for h in range(2):
                        cols = slice(h * BANK, (h + 1) * BANK)
                        bank = acc[:, 2 * t + h, :]
                        pe.matmul(bank, acut[:, r, 0, rows], wcut[:, r, 0, cols], start=first, stop=False)
                        pe.matmul(bank, acut[:, r, 0, rows], wcut[:, r, 1, cols], start=False, stop=False)
                        ins = pe.matmul(bank, acut[:, r, 1, rows], wcut[:, r, 0, cols], start=False, stop=last)
                        if last:
                            ins.then_inc(done, 1)
                if not last:
                    ins.then_inc(used, 1)

            for r in range(R):
                chunk(r, 0, first=(r == 0))
            with pe.Fori(1, steps - 1) as i:
                for r in range(R):
                    chunk(r, i)
            for r in range(R):
                chunk(r, steps - 1, last=(r == R - 1))

        @block.vector
        def _(dve):
            with dve.Fori(0, steps) as i:
                for r in range(R):
                    dve.wait_ge(hi_made, i * R + r + 1)
                    dve.tensor_tensor(acut[:, r, 1:2, :], actT[:, bass.ds(i * R + r, 1), :], acut[:, r, 0:1, :].bitcast(F32), ALU.subtract)
                    dve.tensor_tensor(wcut[:, r, 1, :], raw[:, r, :], wcut[:, r, 0, :].bitcast(F32), ALU.subtract).then_inc(lo_made, 1)
            for i in range(2 * NT):
                t, h = divmod(i, 2)
                dst = resid[:, t, h * BANK:(h + 1) * BANK]
                dve.wait_ge(done, i + 1)
                if gate is None:
                    dve.tensor_tensor(dst, acc[:, i, :], dst, ALU.add).then_inc(added, 1)
                else:
                    dve.tensor_tensor(tmp[:, i % 2, :], acc[:, i, :], gate[:, h * BANK:(h + 1) * BANK], ALU.mult).then_inc(gated, 1)
                    dve.wait_ge(gated, i + 1)
                    dve.tensor_tensor(dst, tmp[:, i % 2, :], dst, ALU.add).then_inc(added, 1)


def attention(nc, name, consts, qT, kT, v, vmeta, table, meta, scale, oT, early):
    ident = consts["ident"]
    keys = meta + SEQ
    H = 8
    nh = table.shape[1]
    with Phase(nc, name) as ph:
        s = ph.sb("s", [P, 3, keys])
        prob = ph.sb("prob", [P, 3, keys])
        probT = ph.sb("probT", [P, 2, NT, SEQ])
        probTm = ph.sb("probTm", [META, 2, SEQ])
        negmax = ph.sb("negmax", [P, 4 * H])
        rsum = ph.sb("rsum", [P, 4 * H])
        rinv = ph.sb("rinv", [P, 4 * H])
        S = ph.ps("S", [P, 2, 2 * BANK])
        T = ph.ps("T", [P, 2, BANK])
        M = ph.ps("M", [P, BANK])
        O = ph.ps("O", [P, BANK])
        early_landed, scores, biased, exped, inverted, normed, turned, turned_m, copied, copied_m, pv, out = (
            ph.sem(n) for n in ("early_landed", "scores", "biased", "exped", "inverted", "normed", "turned",
                                "turned_m", "copied", "copied_m", "pv", "out"))
        units = [(h, n) for h in range(H) for n in range(NT)]
        block = ph.block()

        @block.sync
        def _(sp):
            load_early(sp, early_landed, early)

        @block.tensor
        def _(pe):
            def score(u):
                h, n = units[u]
                L = meta + (n + 1) * P
                if u >= 2:
                    pe.wait_ge(biased, u - 1)
                q = qT(h)[:, n * P:(n + 1) * P]
                first = min(L, BANK)
                ins = pe.matmul(S[:, u % 2, 0:first], q, kT(h)[:, 0:first], start=True, stop=True)
                if L > BANK:
                    ins = pe.matmul(S[:, u % 2, BANK:L], q, kT(h)[:, BANK:L], start=True, stop=True)
                ins.then_inc(scores, 1)

            def turn(u):
                h, n = units[u]
                pe.wait_ge(normed, u + 1)
                if u >= 2:
                    pe.wait_ge(copied, u - 1)
                for j in range(n + 1):
                    ins = pe.transpose(T[:, u % 2, j * P:(j + 1) * P], prob[:, u % 3, meta + j * P:meta + (j + 1) * P], ident[:])
                ins.then_inc(turned, 1)
                if meta:
                    if n == 0 and h >= 1:
                        pe.wait_ge(copied_m, h)
                    pe.transpose(M[0:meta, n * P:(n + 1) * P], prob[:, u % 3, 0:meta], ident[:]).then_inc(turned_m, 1)

            def values(h):
                pe.wait_ge(copied, NT * (h + 1))
                if meta:
                    pe.wait_ge(copied_m, h + 1)
                if h >= 1:
                    pe.wait_ge(out, h)
                base = 64 * (h % 2)
                for j in range(NT):
                    ins = pe.matmul(O[base:base + 64, j * P:], v[:, j, h * 64:(h + 1) * 64], probT[:, h % 2, j, j * P:],
                                    start=(j == 0), stop=(j == NT - 1 and not meta))
                if meta:
                    ins = pe.matmul(O[base:base + 64, :], vmeta[0:meta, h * 64:(h + 1) * 64], probTm[0:meta, h % 2, :],
                                    start=False, stop=True)
                ins.then_inc(pv, 1)

            n_u = len(units)
            for u in range(n_u + 4):
                if u < n_u:
                    score(u)
                if 2 <= u <= n_u + 1:
                    turn(u - 2)
                if u >= NT + 3 and (u - 3) % NT == 0 and (u - 3) // NT <= H:
                    values((u - 3) // NT - 1)

        @block.vector
        def _(dve):
            def bias(u):
                h, n = units[u]
                L = meta + (n + 1) * P
                off = (NT - 1 - n) * P
                dve.wait_ge(scores, u + 1)
                if u >= 3:
                    dve.wait_ge(exped, u - 2)
                dve.tensor_tensor_reduce(s[:, u % 3, 0:L], S[:, u % 2, 0:L], table[:, h % nh, off:off + L], -scale, 3e38,
                                         ALU.add, ALU.min, negmax[:, u:u + 1]).then_inc(biased, 1)

            def norm(u):
                h, n = units[u]
                L = meta + (n + 1) * P
                dve.wait_ge(exped, u + 1)
                dve.reciprocal(rinv[:, u:u + 1], rsum[:, u:u + 1]).then_inc(inverted, 1)
                dve.wait_ge(inverted, u + 1)
                dve.tensor_scalar(prob[:, u % 3, 0:L], prob[:, u % 3, 0:L], rinv[:, u:u + 1], None, ALU.mult).then_inc(normed, 1)

            def collect(h):
                base = 64 * (h % 2)
                dve.wait_ge(pv, h + 1)
                dve.tensor_copy(oT[base:base + 64, h // 2, :], O[base:base + 64, :]).then_inc(out, 1)

            n_u = len(units)
            for u in range(n_u + 6):
                if u < n_u:
                    bias(u)
                if 1 <= u <= n_u:
                    norm(u - 1)
                if u >= NT + 5 and (u - 5) % NT == 0 and (u - 5) // NT <= H:
                    collect((u - 5) // NT - 1)

        @block.scalar
        def _(act):
            def expo(u):
                h, n = units[u]
                L = meta + (n + 1) * P
                act.wait_ge(biased, u + 1)
                if u >= 3:
                    act.wait_ge(turned, u - 2)
                    if meta:
                        act.wait_ge(turned_m, u - 2)
                act.activation(prob[:, u % 3, 0:L], s[:, u % 3, 0:L], ACT.Exp, bias=negmax[:, u:u + 1], scale=-1.0,
                               accum_out=rsum[:, u:u + 1]).then_inc(exped, 1)

            def copy(u):
                h, n = units[u]
                act.wait_ge(turned, u + 1)
                if n == 0 and h >= 2:
                    act.wait_ge(pv, h - 1)
                act.activation(probT[:, h % 2, 0:n + 1, n * P:(n + 1) * P],
                               T[:, u % 2, 0:(n + 1) * P].rearrange("p (j q) -> p j q", q=P), ACT.Copy).then_inc(copied, 1)
                if meta and n == NT - 1:
                    act.wait_ge(turned_m, u + 1)
                    act.activation(probTm[0:meta, h % 2, :], M[0:meta, :], ACT.Copy).then_inc(copied_m, 1)

            n_u = len(units)
            for u in range(n_u + 2):
                if u < n_u:
                    expo(u)
                if u >= 2:
                    copy(u - 2)


def retention(nc, consts, rq, rk, rv, rgT, gain, rope, decay_dram, decay_meta_dram, early):
    ident = consts["ident"]
    H = RET_H
    with Phase(nc, "ret") as ph:
        decay = ph.sb("decay", [P, H, SEQ])
        decay_m = ph.sb("decay_m", [META, H, SEQ])
        a = ph.sb("a", [P, 2, BANK])
        b = ph.sb("b", [P, 2, BANK])
        qT = ph.sb("qT", [P, 4, SEQ])
        kT = ph.sb("kT", [P, 4, KEYS])
        wide = [SEQ - j * P for j in range(NT)]
        at = [sum(wide[:j]) for j in range(NT)]
        m = ph.sb("m", [P, 2, sum(wide)])
        mm = ph.sb("mm", [META, 2, SEQ])
        stats = ph.sb("stats", [P, NT, 6])
        mv = ph.sb("mv", [P, H, NT, 2])
        var = ph.sb("var", [P, H, NT])
        rstd = ph.sb("rstd", [P, H, NT])
        half = ph.sb("half", [P, NT])
        yn = a[:].rearrange("p s (n e) -> p s n e", n=NT)
        S = ph.ps("S", [P, 4, BANK])
        Y = ph.ps("Y", [P, 2, BANK])
        T = ph.ps("T", [P, 2, BANK])
        names = ("early_landed", "tables", "cosed", "swapped", "roped", "turned", "copied", "scored", "decayed", "pv",
                 "meaned", "rooted", "normed", "yturned", "gated", "dve_link", "pool_link")
        (early_landed, tables, cosed, swapped, roped, turned, copied, scored, decayed, pv, meaned, rooted, normed,
         yturned, gated, dve_link, pool_link) = (ph.sem(n) for n in names)
        jobs = [(rq, t, P, qT, t * P) for t in range(NT)] + [(rk, t, P, kT, t * P) for t in range(NT)] + [(rk, NT, META, kT, SEQ)]
        heads = lambda x: x.rearrange("p (h e) -> p h e", e=RET_DK)
        block = ph.block()

        @block.sync
        def _(sp):
            sp.dma_start(decay[:], decay_dram).then_inc(tables, 16)
            sp.dma_start(decay_m[:], decay_meta_dram).then_inc(tables, 16)
            load_early(sp, early_landed, early)

        @block.gpsimd
        def _(pool):
            link = Link(pool, pool_link)
            link(pool.memset(half[:], -0.5))
            for i, (src, t, rows, dst, col) in enumerate(jobs):
                x, o = heads(src[0:rows, t, :]), heads(b[0:rows, i % 2, :])
                if i >= 2:
                    pool.wait_ge(roped, i - 1)
                e = RET_DK // 2
                for lo, hi in ((0, e), (e, 0)):
                    ins = pool.tensor_tensor(o[:, :, lo:lo + e], x[:, :, hi:hi + e], bc(rope[0:rows, t, 1, lo:lo + e], 1, H), ALU.mult)
                ins.then_inc(swapped, 1)
            for h in range(H):
                pool.wait_ge(meaned, h + 1)
                pool.tensor_tensor(rstd[:, h, :], var[:, h, :], half[:], ALU.pow).then_inc(rooted, 1)

        @block.vector
        def _(dve):
            link = Link(dve, dve_link)
            for i, (src, t, rows, dst, col) in enumerate(jobs):
                if i >= 2:
                    dve.wait_ge(turned, i - 1)
                x, o = heads(src[0:rows, t, :]), heads(a[0:rows, i % 2, :])
                dve.tensor_tensor(o, x, bc(rope[0:rows, t, 0, :], 1, H), ALU.mult).then_inc(cosed, 1)
                dve.wait_ge(cosed, i + 1)
                dve.wait_ge(swapped, i + 1)
                dve.tensor_tensor(a[0:rows, i % 2, :], a[0:rows, i % 2, :], b[0:rows, i % 2, :], ALU.add).then_inc(roped, 1)

            def mask(h):
                for j in range(NT + 1):
                    i = h * (NT + 1) + j
                    dve.wait_ge(scored, i + 1)
                    if h >= 2 and j == 0:
                        dve.wait_ge(pv, h - 1)
                    if j < NT:
                        dve.tensor_tensor(m[:, h % 2, at[j]:at[j] + wide[j]], S[:, i % 4, 0:wide[j]], decay[:, h, 0:wide[j]], ALU.mult).then_inc(decayed, 1)
                    else:
                        dve.tensor_tensor(mm[0:META, h % 2, :], S[0:META, i % 4, :], decay_m[0:META, h, :], ALU.mult).then_inc(decayed, 1)

            def norm(h):
                dve.wait_ge(pv, h + 1)
                for n in range(NT):
                    ins = dve.bn_stats(stats[:, n, :], Y[:, h % 2, n * P:(n + 1) * P])
                link(ins)
                for n in range(NT):
                    ins = dve.bn_aggr(mv[:, h, n, :], stats[:, n, :])
                link(ins)
                dve.tensor_scalar(var[:, h, :], mv[:, h, :, 1], EPS, None, ALU.add).then_inc(meaned, 1)
                dve.wait_ge(rooted, h + 1)
                if h >= 2:
                    dve.wait_ge(yturned, h - 1)
                for n in range(NT):
                    ins = dve.tensor_scalar(yn[:, h % 2, n, :], Y[:, h % 2, n * P:(n + 1) * P], mv[:, h, n, 0:1], rstd[:, h, n:n + 1], ALU.subtract, ALU.mult)
                ins.then_inc(normed, 1)

            def gate(h):
                dve.wait_ge(yturned, h + 1)
                dve.scalar_tensor_tensor(rgT[:, h, :], T[:, h % 2, :], gain[:, h:h + 1], rgT[:, h, :], ALU.mult, ALU.mult).then_inc(gated, 1)

            dve.wait_ge(tables, 32)
            for h in range(H + 3):
                if h < H:
                    mask(h)
                if 2 <= h <= H + 1:
                    norm(h - 2)
                if h >= 3:
                    gate(h - 3)

        @block.scalar
        def _(act):
            for i, (src, t, rows, dst, col) in enumerate(jobs):
                act.wait_ge(turned, i + 1)
                act.activation(dst[:, :, col:col + rows], T[:, i % 2, :].rearrange("p (c q) -> p c q", q=P)[:, :, 0:rows], ACT.Copy).then_inc(copied, 1)

        @block.tensor
        def _(pe):
            for i, (src, t, rows, dst, col) in enumerate(jobs):
                pe.wait_ge(roped, i + 1)
                if i >= 2:
                    pe.wait_ge(copied, i - 1)
                for c in range(4):
                    ins = pe.transpose(T[:, i % 2, c * P:c * P + rows], a[0:rows, i % 2, c * P:(c + 1) * P], ident[0:rows, 0:rows])
                ins.then_inc(turned, 1)
            pe.wait_ge(copied, len(jobs))

            def score(h):
                base = 64 * (h % 2)
                for j in range(NT + 1):
                    i = h * (NT + 1) + j
                    if i >= 4:
                        pe.wait_ge(decayed, i - 3)
                    k = kT[base:base + 64, h // 2, j * P:(j + 1) * P] if j < NT else kT[base:base + 64, h // 2, SEQ:KEYS]
                    if j < NT:
                        pe.matmul(S[:, i % 4, 0:wide[j]], k, qT[base:base + 64, h // 2, j * P:], start=True, stop=True).then_inc(scored, 1)
                    else:
                        pe.matmul(S[0:META, i % 4, :], k, qT[base:base + 64, h // 2, :], start=True, stop=True).then_inc(scored, 1)

            def values(h):
                pe.wait_ge(decayed, (NT + 1) * (h + 1))
                if h >= 2:
                    pe.wait_ge(normed, h - 1)
                e = slice(h * RET_DV, (h + 1) * RET_DV)
                for n in range(NT):
                    o = Y[:, h % 2, n * P:(n + 1) * P]
                    pe.matmul(o, mm[0:META, h % 2, n * P:(n + 1) * P], rv[0:META, NT, e], start=True, stop=False)
                    for j in range(n + 1):
                        c = at[j] + (n - j) * P
                        ins = pe.matmul(o, m[:, h % 2, c:c + P], rv[:, j, e], start=False, stop=(j == n))
                ins.then_inc(pv, 1)

            def turn(h):
                pe.wait_ge(normed, h + 1)
                if h >= 2:
                    pe.wait_ge(gated, h - 1)
                for n in range(NT):
                    ins = pe.transpose(T[:, h % 2, n * P:(n + 1) * P], yn[:, h % 2, n, :], ident[:])
                ins.then_inc(yturned, 1)

            for h in range(H + 3):
                if h < H:
                    score(h)
                if h >= 3:
                    turn(h - 3)
                if 1 <= h <= H:
                    values(h - 1)


def mla_prepare(nc, consts, cq, ckv, tables, qT, kT, v, early):
    ident = consts["ident"]
    H = MLA_H
    with Phase(nc, "mla") as ph:
        wq, wkv, rope = (tables[n] for n in ("wq", "wkv", "rope_mla"))
        gl = [tables["g_ql"][:, k:k + 1] for k in range(3)] + [tables["g_kvl"][:, k:k + 1] for k in range(2)]
        gqk = (tables["g_q"], tables["g_k"])
        ssq = ph.sb("ssq", [P, 9])
        ms = ph.sb("ms", [P, 9])
        rstd = ph.sb("rstd", [P, 9])
        ss8 = ph.sb("ss8", [P, 9, H])
        ms8 = ph.sb("ms8", [P, 9, H])
        rstd8 = ph.sb("rstd8", [P, 9, H])
        half = ph.sb("half", [P, 9])
        cn = ph.sb("cn", [P, 2, MLA_QL])
        cqT = ph.sb("cqT", [P, 3, SEQ])
        ckvT = ph.sb("ckvT", [P, 2, KEYS])
        x = ph.sb("x", [P, 3, H, QK])
        sq = ph.sb("sq", [P, 2, H * QK])
        ra = ph.sb("ra", [P, H, ROPE])
        rb = ph.sb("rb", [P, H, ROPE])
        A = ph.ps("A", [P, 2, 2, BANK])
        T = ph.ps("T", [P, 2, 2, BANK])
        names = ("early_landed", "squares", "junked", "means", "roots", "scaled", "turned1", "copied1", "made", "filled",
                 "squared", "means8", "roots8", "normed", "swapped", "roped", "turned2", "copied2", "pool_link", "dve_link")
        (early_landed, squares, junked, means, roots, scaled, turned1, copied1, made, filled, squared, means8, roots8,
         normed, swapped, roped, turned2, copied2, pool_link, dve_link) = (ph.sem(n) for n in names)
        lat = [(cq[:, t, :], P, 3, cqT, t * P, 0) for t in range(NT)]
        lat += [(ckv[:, t, 0:MLA_KVL], P, 2, ckvT, t * P, 3) for t in range(NT)]
        lat += [(ckv[0:META, NT, 0:MLA_KVL], META, 2, ckvT, SEQ, 3)]
        jobs = [(0, t, P) for t in range(NT)] + [(1, t, P) for t in range(NT)] + [(1, NT, META)]
        block = ph.block()

        @block.sync
        def _(sp):
            load_early(sp, early_landed, early)

        @block.scalar
        def _(act):
            for i, (src, rows, nch, dst, col, g) in enumerate(lat):
                act.activation(sq[0:rows, 0, 0:nch * P], src, ACT.Square, accum_out=ssq[0:rows, i:i + 1]).then_inc(squares, 1)
                act.wait_ge(squares, i + 1)

            def front(j):
                which, t, rows = jobs[j]
                act.wait_ge(made, j + 1)
                if j >= 3:
                    act.wait_ge(turned2, j - 2)
                if which == 0:
                    for b in range(2):
                        ins = act.activation(x[0:rows, j % 3, 4 * b:4 * b + 4, :], A[0:rows, j % 2, b, 0:4 * QK].rearrange("p (h e) -> p h e", e=QK), ACT.Copy)
                else:
                    for b in range(2):
                        kv = A[0:rows, j % 2, b, :].rearrange("p (h e) -> p h e", e=NOPE + MLA_V)
                        act.activation(x[0:rows, j % 3, 4 * b:4 * b + 4, 0:NOPE], kv[:, :, 0:NOPE], ACT.Copy)
                        act.activation(v[0:rows, t, 4 * b * 64:(4 * b + 4) * 64].rearrange("p (h e) -> p h e", e=MLA_V), kv[:, :, NOPE:], ACT.Copy)
                    ins = act.activation(x[0:rows, j % 3, :, NOPE:], bc(ckv[0:rows, t, MLA_KVL:], 1, H), ACT.Copy)
                ins.then_inc(filled, 1)
                act.wait_ge(filled, j + 1)
                if j >= 2:
                    act.wait_ge(means8, j - 1)
                act.activation(sq[0:rows, j % 2, :], x[0:rows, j % 3].rearrange("p h e -> p (h e)"), ACT.Square).then_inc(squared, 1)

            def back(j):
                which, t, rows = jobs[j]
                act.wait_ge(turned2, j + 1)
                col = 0 if t == NT else t * P + META * which
                dst = (qT, kT)[which][:, :, col:col + rows]
                for b in range(2):
                    ins = act.activation(dst[:, 4 * b:4 * b + 4, :], T[0:QK, j % 2, b, :].rearrange("p (h q) -> p h q", q=P)[:, :, 0:rows], ACT.Copy)
                ins.then_inc(copied2, 1)

            for j in range(len(jobs) + 2):
                if j < len(jobs):
                    front(j)
                if j >= 2:
                    back(j - 2)

        @block.gpsimd
        def _(pool):
            link = Link(pool, pool_link)
            link(pool.memset(half[:], -0.5))
            for i, (src, rows, nch, dst, col, g) in enumerate(lat):
                pool.wait_ge(means, i + 1)
                pool.tensor_tensor(rstd[0:rows, i:i + 1], ms[0:rows, i:i + 1], half[0:rows, 0:1], ALU.pow).then_inc(roots, 1)
            e = ROPE // 2
            for j in range(len(jobs) + 1):
                if j < len(jobs):
                    which, t, rows = jobs[j]
                    pool.wait_ge(means8, j + 1)
                    pool.tensor_tensor(rstd8[0:rows, j, :], ms8[0:rows, j, :], half[0:rows, 0:H], ALU.pow).then_inc(roots8, 1)
                if j == 0:
                    continue
                which, t, rows = jobs[j - 1]
                pool.wait_ge(normed, j)
                for lo, hi in ((0, e), (e, 0)):
                    ins = pool.tensor_tensor(rb[0:rows, :, lo:lo + e], x[0:rows, (j - 1) % 3, :, NOPE + hi:NOPE + hi + e], bc(rope[0:rows, t, 1, lo:lo + e], 1, H), ALU.mult)
                ins.then_inc(swapped, 1)

        @block.vector
        def _(dve):
            link = Link(dve, dve_link)
            def evacuate(i):
                src, rows, nch, dst, col, g = lat[i]
                dve.wait_ge(turned1, i + 1)
                for k in range(nch):
                    ins = dve.tensor_scalar(dst[:, k, col:col + rows], T[:, i % 2, 0, k * P:k * P + rows], gl[g + k], None, ALU.mult)
                ins.then_inc(copied1, 1)

            for i, (src, rows, nch, dst, col, g) in enumerate(lat):
                dve.wait_ge(squares, i + 1)
                dve.tensor_scalar(ms[0:rows, i:i + 1], ssq[0:rows, i:i + 1], 1.0 / (nch * P), EPS, ALU.mult, ALU.add).then_inc(means, 1)
                dve.wait_ge(roots, i + 1)
                if i >= 2:
                    dve.wait_ge(turned1, i - 1)
                dve.tensor_scalar(cn[0:rows, i % 2, 0:nch * P], src, rstd[0:rows, i:i + 1], None, ALU.mult).then_inc(scaled, 1)
                if i >= 1:
                    evacuate(i - 1)
            evacuate(len(lat) - 1)

            def mean_square(j):
                which, t, rows = jobs[j]
                dve.wait_ge(squared, j + 1)
                link(dve.tensor_reduce(ss8[0:rows, j, :], sq[0:rows, j % 2, :].rearrange("p (h e) -> p h e", e=QK), AX.X, ALU.add))
                dve.tensor_scalar(ms8[0:rows, j, :], ss8[0:rows, j, :], 1.0 / QK, EPS, ALU.mult, ALU.add).then_inc(means8, 1)

            def normalise(j):
                which, t, rows = jobs[j]
                xj = x[0:rows, j % 3]
                dve.wait_ge(roots8, j + 1)
                link(dve.tensor_tensor(xj, xj, bc(rstd8[0:rows, j, :], 2, QK), ALU.mult))
                dve.tensor_tensor(xj, xj, bc(gqk[which][0:rows, :], 1, H), ALU.mult).then_inc(normed, 1)
                dve.wait_ge(normed, j + 1)
                link(dve.tensor_tensor(ra[0:rows], xj[:, :, NOPE:], bc(rope[0:rows, t, 0, :], 1, H), ALU.mult))
                dve.wait_ge(swapped, j + 1)
                dve.tensor_tensor(xj[:, :, NOPE:], ra[0:rows], rb[0:rows], ALU.add).then_inc(roped, 1)

            for j in range(len(jobs) + 1):
                if j < len(jobs):
                    mean_square(j)
                if j >= 1:
                    normalise(j - 1)

        @block.tensor
        def _(pe):
            for i, (src, rows, nch, dst, col, g) in enumerate(lat):
                pe.wait_ge(scaled, i + 1)
                if i >= 2:
                    pe.wait_ge(copied1, i - 1)
                for k in range(nch):
                    ins = pe.transpose(T[:, i % 2, 0, k * P:k * P + rows], cn[0:rows, i % 2, k * P:(k + 1) * P], ident[0:rows, 0:rows])
                ins.then_inc(turned1, 1)
            pe.wait_ge(copied1, len(lat))

            def make(j):
                which, t, rows = jobs[j]
                if j >= 2:
                    pe.wait_ge(filled, j - 1)
                srcT, w, nch, n = ((cqT, wq, 3, 4 * QK), (ckvT, wkv, 2, BANK))[which]
                for b in range(2):
                    for k in range(nch):
                        ins = pe.matmul(A[0:rows, j % 2, b, 0:n], srcT[:, k, t * P:t * P + rows], w[:, k, b * n:(b + 1) * n],
                                        start=(k == 0), stop=(k == nch - 1))
                ins.then_inc(made, 1)

            def turn(j):
                which, t, rows = jobs[j]
                pe.wait_ge(roped, j + 1)
                if j >= 2:
                    pe.wait_ge(copied2, j - 1)
                for h in range(H):
                    ins = pe.transpose(T[0:QK, j % 2, h // 4, (h % 4) * P:(h % 4) * P + rows], x[0:rows, j % 3, h, :], ident[0:rows, 0:rows])
                ins.then_inc(turned2, 1)

            for j in range(len(jobs) + 2):
                if j < len(jobs):
                    make(j)
                if j >= 2:
                    turn(j - 2)


def merge_loads(w_mla_dram, w_ret_dram):
    cols = lambda w, c: w[:, c * P:(c + 1) * P].rearrange("(k p) n -> p k n", p=P)
    return lambda raw, c: [(raw[:, c % 2, 0:4, :], cols(w_mla_dram, c)), (raw[:, c % 2, 4:, :], cols(w_ret_dram, c))]


def merge(nc, oT, ygT, zaT, zrT, w_mla_dram, w_ret_dram, ring, early):
    KO, KY = 4, KD
    chunk_loads = merge_loads(w_mla_dram, w_ret_dram)
    with Phase(nc, "merge") as ph:
        N = 2
        raw = ring.raw
        wcut = ph.sb("wcut", [P, N, 2, KO + KY, P], F32R)
        acut = ph.sb("acut", [P, 2, KO + KY, SEQ], F32R)
        t1 = ph.sb("t1", [P, 2, BANK])
        t2 = ph.sb("t2", [P, 2, BANK])
        A = ph.ps("A", [P, 2, BANK])
        R = ph.ps("R", [P, 2, BANK])
        landed = [ph.sem(f"landed{i}") for i in range(N)]
        names = ("early_landed", "a_hi", "a_lo", "w_hi", "w_lo", "a_done", "r_done", "gated", "added")
        early_landed, a_hi, a_lo, w_hi, w_lo, a_done, r_done, gated, added = (ph.sem(n) for n in names)
        block = ph.block()

        @block.sync
        def _(sp):
            for c in range(KD):
                if c < N:
                    continue
                sp.wait_ge(w_lo, c - N + 1)
                for dst, src in chunk_loads(raw, c):
                    sp.dma_start(dst, src).then_inc(landed[c % N], 16)
            load_early(sp, early_landed, early)

        @block.scalar
        def _(act):
            def split(c):
                if c >= N:
                    act.wait_ge(landed[c % N], 32 * (c // N))
                    act.wait_ge(r_done, c - N + 1)
                act.activation(wcut[:, c % N, 0], raw[:, c % N], ACT.Copy).then_inc(w_hi, 1)

            split(0)
            for k in range(KO + KY):
                act.activation(acut[:, 0, k, :], oT[:, k, :] if k < KO else ygT[:, k - KO, :], ACT.Copy).then_inc(a_hi, 1)
            for c in range(1, KD):
                split(c)

        @block.tensor
        def _(pe):
            def product(bank, c, ks):
                for k in ks:
                    if c == 0:
                        pe.wait_ge(a_lo, k + 1)
                    pe.matmul(bank, wcut[:, c % N, 0, k, :], acut[:, 0, k, :], start=(k == ks[0]), stop=False)
                    pe.matmul(bank, wcut[:, c % N, 0, k, :], acut[:, 1, k, :], start=False, stop=False)
                    ins = pe.matmul(bank, wcut[:, c % N, 1, k, :], acut[:, 0, k, :], start=False, stop=(k == ks[-1]))
                return ins

            for c in range(KD):
                pe.wait_ge(w_lo, c + 1)
                if c >= 2:
                    pe.wait_ge(gated, 2 * (c - 1))
                product(A[:, c % 2, :], c, range(KO)).then_inc(a_done, 1)
                product(R[:, c % 2, :], c, range(KO, KO + KY)).then_inc(r_done, 1)

        @block.vector
        def _(dve):
            def split(c):
                dve.wait_ge(w_hi, c + 1)
                dve.tensor_tensor(wcut[:, c % N, 1], raw[:, c % N], wcut[:, c % N, 0].bitcast(F32), ALU.subtract).then_inc(w_lo, 1)

            split(0)
            for k in range(KO + KY):
                dve.wait_ge(a_hi, k + 1)
                dve.tensor_tensor(acut[:, 1, k, :], oT[:, k, :] if k < KO else ygT[:, k - KO, :], acut[:, 0, k, :].bitcast(F32), ALU.subtract).then_inc(a_lo, 1)
            split(1)
            for c in range(KD):
                if c >= 2:
                    dve.wait_ge(added, c - 1)
                dve.wait_ge(a_done, c + 1)
                dve.tensor_tensor(t1[:, c % 2, :], A[:, c % 2, :], zaT[:, c, :], ALU.mult).then_inc(gated, 1)
                dve.wait_ge(r_done, c + 1)
                dve.tensor_tensor(t2[:, c % 2, :], R[:, c % 2, :], zrT[:, c, :], ALU.mult).then_inc(gated, 1)
                if c + 2 < KD:
                    split(c + 2)
                dve.wait_ge(gated, 2 * (c + 1))
                dve.tensor_tensor(zaT[:, c, :], t1[:, c % 2, :], t2[:, c % 2, :], ALU.add).then_inc(added, 1)


def up_loads(wq_dram):
    KU = KD // 2
    return lambda raw: [(raw[:, r, :, :], wq_dram[r // 2, :, KU * (r % 2):KU * (r % 2) + KU]) for r in range(4)]


def peer_up(nc, consts, half, xs, wq_dram, u_dram, keys_dram, iota_dram, act_buf, picksT, ring, early):
    ident = consts["ident"]
    C, KU = 2, KD // 2
    R = 2 * C
    Q = PEER_H // C
    steps = Q + NKEYS // C
    H, K, TILES = PEER_H, TOPK, HALF // P
    SCORE, COPY, EXP, TURN, STORE = (Q, Q + 2), (Q + 1, Q + 3), (Q + 9, Q + 18), (Q + 12, Q + 21), (Q + 13, Q + 22)
    POOL = STORE[1] + 1

    free = NKEYS * HALF

    def take(*shape):
        nonlocal free
        free -= int(np.prod(shape))
        piece = act_buf[:].rearrange("p e t -> p (e t)")[:, free:free + int(np.prod(shape))]
        names = "abcd"[:len(shape)]
        return piece.rearrange(f"p ({' '.join(names)}) -> p {' '.join(names)}", **dict(zip(names, shape)))

    with Phase(nc, f"up{half}") as ph:
        raw = ring.raw
        cut = ph.sb("cut", [P, R, 2, KU, P], F32R)
        acc = ph.ps("acc", [P, C, BANK])
        qT = take(H, HALF)
        first_query = NKEYS - H
        keys = take(NKEYS)
        iota = take(P)
        s = take(TILES, H * 2, NKEYS)
        s2 = take(H, 2, NKEYS)
        best = take(H, 2, K)
        idx = take(H, 2, K).bitcast(U32)
        idxf = take(H, 2, K)
        cand = take(H, K, K)
        cand2 = take(H, K * K)
        top = take(H, K)
        ci = take(H * K).bitcast(U32)
        parts = take(2, H * K).bitcast(U32)
        partsf = take(2, H * K)
        hot = take(2, H * K, K)
        shifted = take(H, K)
        ex = take(H, K)
        den = take(H)
        rden = take(H)
        picks = take(3, H * K)
        assert (STORE[1] + 1 - Q) * C < free // HALF
        S = ph.ps("S", [P, 4, BANK])
        T = ph.ps("T", [P, BANK])
        landed = [ph.sem(f"landed{r}") for r in range(R)]
        names = ("early_landed", "loaded", "hi_made", "lo_pool", "lo_dve", "used", "out", "scored", "copied", "shiftd", "exped", "picked", "turned", "stored", "dve_link")
        early_landed, loaded, hi_made, lo_pool, lo_dve, used, out, scored, copied, shiftd, exped, picked, turned, stored, dve_link = (ph.sem(n) for n in names)
        block = ph.block()

        def wait_lo(engine, i, r, pool):
            if pool:
                engine.wait_ge(lo_pool, i * R + r + 1)
            else:
                engine.wait_ge(lo_dve, (i - POOL) * R + r + 1)

        @block.sync
        def _(sp):
            def load(r, i, src):
                ks = slice(KU * (r % 2), KU * (r % 2) + KU)
                sp.dma_start(raw[:, r], src[bass.ds(i * C + r // 2, 1), :, ks].rearrange("o p k e -> (o p) k e")).then_inc(landed[r], 16)

            sp.dma_start(keys, keys_dram).then_inc(loaded, 16)
            sp.dma_start(iota, iota_dram).then_inc(loaded, 16)
            for i in range(1, Q):
                for r in range(R):
                    wait_lo(sp, i - 1, r, True)
                    load(r, i, wq_dram)
            for lo, hi, pool in ((Q, POOL + 1, True), (POOL + 1, steps, False)):
                with sp.Fori(lo, hi) as i:
                    for r in range(R):
                        wait_lo(sp, i - 1, r, pool)
                        load(r, i - Q, u_dram)
            load_early(sp, early_landed, early)

        @block.scalar
        def _(act):
            def split(r, i, first=False):
                if not first:
                    act.wait_ge(landed[r], i * 16)
                    act.wait_ge(used, (i - 1) * R + r + 1)
                act.activation(cut[:, r, 0], raw[:, r], ACT.Copy).then_inc(hi_made, 1)

            def query(c):
                act.wait_ge(used, 2 * c + 2)
                act.activation(act_buf[:, first_query + c:first_query + c + 1, :], acc[:, c % 2:c % 2 + 1, 0:HALF], ACT.Copy).then_inc(out, 1)

            def gelu(b, c):
                act.wait_ge(used, 2 * (c + H) + 2)
                act.activation(act_buf[:, bass.ds(c, 1), :], acc[:, b:b + 1, 0:HALF], ACT.Gelu).then_inc(out, 1)

            def step(i):
                split(0, i)
                split(1, i)
                gelu(1, 2 * (i - Q) - 1)
                split(2, i)
                split(3, i)
                gelu(0, 2 * (i - Q))

            def copy_scores(t):
                act.wait_ge(scored, t + 1)
                for b in range(4):
                    side = b // 2
                    dst = s[:, t].rearrange("p (h c) k -> p h c k", h=H)[:, 4 * (b % 2):4 * (b % 2) + 4, side, :]
                    ins = act.activation(dst, S[:, b, :].rearrange("p (h k) -> p h k", h=4), ACT.Copy)
                ins.then_inc(copied, 1)

            def exponent(t):
                act.wait_ge(shiftd, t + 1)
                act.activation(ex, shifted, ACT.Exp).then_inc(exped, 1)

            def store(t):
                act.wait_ge(turned, t + 1)
                ins = act.activation(picksT[:, :, t * P:(t + 1) * P], T[:, 0:3 * P].rearrange("p (j t) -> p j t", j=3), ACT.Copy)
                ins.then_inc(stored, 1)

            for r in range(R):
                split(r, 0, first=True)
            query(0)
            for i in range(1, Q + 1):
                split(0, i)
                split(1, i)
                query(2 * i - 1)
                split(2, i)
                split(3, i)
                if i < Q:
                    query(2 * i)
                else:
                    gelu(0, 0)
            last = Q + 1
            for at, serve, t in sorted([(COPY[t], copy_scores, t) for t in range(TILES)] + [(EXP[t], exponent, t) for t in range(TILES)] +
                                       [(STORE[t], store, t) for t in range(TILES)], key=lambda x: x[0]):
                with act.Fori(last, at + 1) as i:
                    step(i)
                serve(t)
                last = at + 1
                if serve is exponent:
                    step(last)
                    last += 1
            with act.Fori(last, steps) as i:
                step(i)
            gelu(1, NKEYS - 1)

        @block.gpsimd
        def _(pool):
            with pool.Fori(0, POOL) as i:
                for r in range(R):
                    pool.wait_ge(hi_made, i * R + r + 1)
                    pool.tensor_tensor(cut[:, r, 1], raw[:, r], cut[:, r, 0].bitcast(F32), ALU.subtract).then_inc(lo_pool, 1)

        @block.vector
        def _(dve):
            link = Link(dve, dve_link)
            dve.wait_ge(loaded, 32)
            for t in range(TILES):
                st = s[:, t].rearrange("p (h c) k -> p h c k", h=H)
                lists = [(h, c) for h in range(H) for c in range(2)]
                dve.wait_ge(copied, t + 1)
                for h, c in lists:
                    ins = dve.max(best[:, h, c, 0:8], st[:, h, c, :])
                link(ins)
                for h, c in lists:
                    ins = dve.max_index(idx[:, h, c, 0:8], best[:, h, c, 0:8], st[:, h, c, :])
                for h, c in lists:
                    ins = dve.match_replace(s2[:, h, c, :], best[:, h, c, 0:8], st[:, h, c, :], NEG)
                link(ins)
                for h, c in lists:
                    ins = dve.max(best[:, h, c, 8:16], s2[:, h, c, :])
                link(ins)
                for h, c in lists:
                    ins = dve.max_index(idx[:, h, c, 8:16], best[:, h, c, 8:16], s2[:, h, c, :])
                link(dve.tensor_tensor(cand, bc(best[:, :, 0, :], 3, K), bc(best[:, :, 1, :], 2, K), ALU.add))
                link(dve.tensor_copy(idxf, idx))
                flat = cand.rearrange("p h a b -> p h (a b)")
                for h in range(H):
                    ins = dve.max(top[:, h, 0:8], flat[:, h, :])
                link(ins)
                for h in range(H):
                    ins = dve.max_index(ci[:, h * K:h * K + 8], top[:, h, 0:8], flat[:, h, :])
                for h in range(H):
                    ins = dve.match_replace(cand2[:, h, :], top[:, h, 0:8], flat[:, h, :], NEG)
                link(ins)
                for h in range(H):
                    ins = dve.max(top[:, h, 8:16], cand2[:, h, :])
                link(ins)
                for h in range(H):
                    ins = dve.max_index(ci[:, h * K + 8:h * K + 16], top[:, h, 8:16], cand2[:, h, :])
                link(ins)
                dve.tensor_tensor(shifted, top, bc(top[:, :, 0], 2, K), ALU.subtract).then_inc(shiftd, 1)
                dve.tensor_scalar(parts[:, 0, :], ci, 4, None, ALU.logical_shift_right)
                link(dve.tensor_scalar(parts[:, 1, :], ci, K - 1, None, ALU.bitwise_and))
                link(dve.tensor_copy(partsf, parts))
                for c in range(2):
                    ins = dve.tensor_tensor(hot[:, c], bc(partsf[:, c, :], 2, K), bc(iota[:, 0:K], 1, H * K), ALU.is_equal)
                link(ins)
                for c in range(2):
                    o = hot[:, c].rearrange("p (h k) a -> p h k a", h=H)
                    ins = dve.tensor_tensor(o, o, bc(idxf[:, :, c, :], 2, K), ALU.mult)
                link(ins)
                if t >= 1:
                    dve.wait_ge(turned, t)
                for c in range(2):
                    dve.tensor_reduce(picks[:, 1 - c, :], hot[:, c], AX.X, ALU.add)
                dve.wait_ge(exped, t + 1)
                link(dve.tensor_reduce(den, ex, AX.X, ALU.add))
                link(dve.reciprocal(rden, den))
                dve.tensor_tensor(picks[:, 2, :].rearrange("p (h k) -> p h k", h=H), ex, bc(rden, 2, K), ALU.mult).then_inc(picked, 1)
            with dve.Fori(POOL, steps) as i:
                for r in range(R):
                    dve.wait_ge(hi_made, i * R + r + 1)
                    dve.tensor_tensor(cut[:, r, 1], raw[:, r], cut[:, r, 0].bitcast(F32), ALU.subtract).then_inc(lo_dve, 1)

        @block.tensor
        def _(pe):
            def unit(r, i, pool, first=False):
                wait_lo(pe, i, r, pool)
                if r % 2 == 0 and not first:
                    pe.wait_ge(out, 2 * i + r // 2 - 1)
                bank = acc[:, r // 2, 0:HALF]
                for k in range(KU):
                    kx = KU * (r % 2) + k
                    pe.matmul(bank, cut[:, r, 0, k, :], xs[:, 0, kx, :], start=(kx == 0), stop=False)
                    pe.matmul(bank, cut[:, r, 0, k, :], xs[:, 1, kx, :], start=False, stop=False)
                    ins = pe.matmul(bank, cut[:, r, 1, k, :], xs[:, 0, kx, :], start=False, stop=(kx == KD - 1))
                ins.then_inc(used, 1)

            def score(t):
                if t == 0:
                    pe.wait_ge(loaded, 32)
                    pe.wait_ge(out, H)
                else:
                    pe.wait_ge(copied, t)
                for h in range(H):
                    for side in range(2):
                        r = slice(64 * side, 64 * side + 64)
                        ins = pe.matmul(S[:, 2 * side + h // 4, (h % 4) * NKEYS:(h % 4 + 1) * NKEYS], qT[r, h, t * P:(t + 1) * P], keys[r, :], start=True, stop=True)
                ins.then_inc(scored, 1)

            def turn(t):
                pe.wait_ge(picked, t + 1)
                if t >= 1:
                    pe.wait_ge(stored, t)
                for i in range(3):
                    ins = pe.transpose(T[:, i * P:(i + 1) * P], picks[:, i, :], ident[:])
                ins.then_inc(turned, 1)

            for r in range(R):
                unit(r, 0, True, first=True)
            last = 1
            for at, serve, t in sorted([(SCORE[t], score, t) for t in range(TILES)] + [(TURN[t], turn, t) for t in range(TILES)], key=lambda x: x[0]):
                with pe.Fori(last, at + 1) as i:
                    for r in range(R):
                        unit(r, i, True)
                serve(t)
                last = at + 1
            with pe.Fori(last, POOL) as i:
                for r in range(R):
                    unit(r, i, True)
            U = 4
            with pe.Fori(0, (steps - POOL) // U) as j:
                for n in range(U):
                    for r in range(R):
                        unit(r, POOL + j * U + n, False)
            for i in range(POOL + (steps - POOL) // U * U, steps):
                for r in range(R):
                    unit(r, i, False)


def peer_gate(nc, half, iota, picksT, act_buf, early):
    G = 4
    R = 4
    N = HALF // G
    steps = N // R
    e2T, e1T, gateT = (picksT[:, j, :] for j in range(3))
    with Phase(nc, f"gate{half}") as ph:
        scalars = ph.sb("scalars", [P, R, 2, 1])
        minus = ph.sb("minus", [P, HALF])
        square = ph.sb("square", [P, R, G // 2, P])
        hot1 = ph.sb("hot1", [P, R, G, P])
        hot2 = ph.sb("hot2", [P, R, G, P])
        acc = ph.ps("acc", [P, R, BANK])
        names = ("early_landed", "negated", "squared", "built_dve", "built_act", "fetched", "built_pool", "done", "out")
        early_landed, negated, squared, built_dve, built_act, fetched, built_pool, done, out = (ph.sem(n) for n in names)
        block = ph.block()

        @block.sync
        def _(sp):
            load_early(sp, early_landed, early)

        @block.vector
        def _(dve):
            def hots(r, n):
                t = n * G
                dve.tensor_scalar(hot1[:, r, 1, :], iota[:], e1T[:, bass.ds(t + 1, 1)], gateT[:, bass.ds(t + 1, 1)], ALU.is_equal, ALU.mult)
                dve.tensor_tensor(hot2[:, r], bc(iota[:], 1, G), bc(e2T[:, bass.ds(t, G)], 2, P), ALU.is_equal).then_inc(built_dve, 1)

            def weigh(r, n):
                a = act_buf[:, :, bass.ds(n * G, G)]
                dve.wait_ge(done, n + 1)
                dve.tensor_tensor(a, acc[:, r, :].rearrange("p (g e) -> p e g", g=G), a, ALU.mult).then_inc(out, 1)

            dve.tensor_scalar(minus[:], gateT[:], -1.0, None, ALU.mult).then_inc(negated, 1)
            hots(0, 0)
            hots(1, 1)
            with dve.Fori(0, steps - 1) as i:
                for r in range(R):
                    hots((r + 2) % R, i * R + r + 2)
                    weigh(r, i * R + r)
            for r in range(R):
                if r < 2:
                    hots(r + 2, N - R + r + 2)
                weigh(r, N - R + r)

        @block.scalar
        def _(act):
            def squares(r, n, first=False):
                if not first:
                    act.wait_ge(done, n - R + 1)
                for g in range(G // 2):
                    t = n * G + G // 2 + g
                    ins = act.activation(square[:, r, g, :], iota[:], ACT.Square, bias=e1T[:, bass.ds(t, 1)], scale=-1.0)
                ins.then_inc(squared, 1)

            def hots(r, n):
                act.wait_ge(squared, n + 1)
                for g in range(G // 2):
                    t = n * G + G // 2 + g
                    ins = act.activation(hot1[:, r, G // 2 + g, :], square[:, r, g, :], ACT.Relu, bias=gateT[:, bass.ds(t, 1)], scale=minus[:, bass.ds(t, 1)])
                ins.then_inc(built_act, 1)

            act.wait_ge(negated, 1)
            squares(0, 0, first=True)
            for n in range(1, R):
                squares(n, n, first=True)
                hots(n - 1, n - 1)
            with act.Fori(1, steps) as i:
                for r in range(R):
                    squares(r, i * R + r)
                    hots((r - 1) % R, i * R + r - 1)
            hots(R - 1, N - 1)

        @block.gpsimd
        def _(pool):
            def fetch(r, n, first=False):
                if not first:
                    pool.wait_ge(done, n - R + 1)
                pool.tensor_copy(scalars[:, r], picksT[:, 1:3, bass.ds(n * G, 1)]).then_inc(fetched, 1)

            def hot(r):
                pool.tensor_scalar(hot1[:, r, 0, :], iota[:], scalars[:, r, 0, :], scalars[:, r, 1, :], ALU.is_equal, ALU.mult).then_inc(built_pool, 1)

            fetch(0, 0, first=True)
            for n in range(1, R):
                pool.wait_ge(fetched, n)
                fetch(n, n, first=True)
                hot(n - 1)
            with pool.Fori(1, steps) as i:
                for r in range(R):
                    pool.wait_ge(fetched, i * R + r)
                    fetch(r, i * R + r)
                    hot((r - 1) % R)
            pool.wait_ge(fetched, N)
            hot(R - 1)

        @block.tensor
        def _(pe):
            def products(r, n, first=False):
                if not first:
                    pe.wait_ge(out, n - R + 1)
                pe.wait_ge(built_dve, n + 1)
                pe.wait_ge(built_act, n + 1)
                pe.wait_ge(built_pool, n + 1)
                for g in range(G):
                    ins = pe.matmul(acc[:, r, g * P:(g + 1) * P], hot1[:, r, g, :], hot2[:, r, g, :], start=True, stop=True)
                ins.then_inc(done, 1)

            for r in range(R):
                products(r, r, first=True)
            with pe.Fori(1, steps) as i:
                for r in range(R):
                    products(r, i * R + r)


def down_loads(v_dram):
    return lambda raw: [(raw[:, r], v_dram[:, r // 2, BANK * (r % 2):BANK * (r % 2) + BANK].rearrange("p (k e) -> p k e", e=P)) for r in range(4)]


def peer_down(nc, half, v_dram, act_buf, resid, ring, c_dram, w_dram, mod):
    C = 2
    R = 2 * C
    steps = NKEYS // C
    SUMS = 3 * KD
    with Phase(nc, f"down{half}") as ph:
        raw = ring.raw[:].rearrange("p r k e -> p r (k e)")
        vcut = ph.sb("vcut", [P, R, 2, BANK], F32R)
        acut = ph.sb("acut", [P, C, 2, HALF], F32R)
        cond = ph.sb("cond", [P, D])
        ada = ph.sb("ada", [P, D])
        junk = ph.sb("junk", [P, D])
        total = ph.sb("total", [P, 1])
        Y = ph.ps("Y", [P, 4, BANK])
        landed = [ph.sem(f"landed{r}") for r in range(R)]
        names = ("hi_made", "lo_made", "used", "added", "c_loaded", "c_active", "ada_loaded", "summed", "noted")
        hi_made, lo_made, used, added, c_loaded, c_active, ada_loaded, summed, noted = (ph.sem(n) for n in names)
        block = ph.block()

        @block.sync
        def _(sp):
            def load(r, i):
                h = r % 2
                sp.dma_start(raw[:, r:r + 1, :], v_dram[:, bass.ds(i * C + r // 2, 1), h * BANK:(h + 1) * BANK]).then_inc(landed[r], 16)

            def step(i):
                for r in range(R):
                    sp.wait_ge(lo_made, (i - 1) * R + r + 1)
                    load(r, i)

            sp.dma_start(cond[:], c_dram.partition_broadcast(P)).then_inc(c_loaded, 16)
            sp.dma_start(ada[:], w_dram[half * SUMS * P:(half * SUMS + 1) * P, :]).then_inc(ada_loaded, 16)
            step(1)
            with sp.Fori(1, SUMS) as j:
                step(2 * j)
                sp.wait_ge(summed, j)
                sp.dma_start(ada[:], w_dram[bass.ds((half * SUMS + j) * P, P), :]).then_inc(ada_loaded, 16)
                step(2 * j + 1)
            with sp.Fori(2 * SUMS, steps) as i:
                step(i)

        @block.scalar
        def _(act):
            def split(r, i, first=False):
                b = r // 2
                if r % 2 == 0:
                    if not first:
                        act.wait_ge(used, (i - 1) * R + r + 2)
                    act.activation(acut[:, b, 0:1, :], act_buf[:, bass.ds(i * C + b, 1), :], ACT.Copy)
                if not first:
                    act.wait_ge(landed[r], i * 16)
                act.activation(vcut[:, r, 0, :], raw[:, r, :], ACT.Copy).then_inc(hi_made, 1)

            for r in range(R):
                split(r, 0, first=True)
            act.wait_ge(c_loaded, 16)
            act.activation(cond[:], cond[:], ACT.Silu).then_inc(c_active, 1)
            with act.Fori(1, steps) as i:
                for r in range(R):
                    split(r, i)

        @block.vector
        def _(dve):
            def step(i):
                for r in range(R):
                    b = r // 2
                    dve.wait_ge(hi_made, i * R + r + 1)
                    if r % 2 == 0:
                        dve.tensor_tensor(acut[:, b, 1:2, :], act_buf[:, bass.ds(i * C + b, 1), :], acut[:, b, 0:1, :].bitcast(F32), ALU.subtract)
                    dve.tensor_tensor(vcut[:, r, 1, :], raw[:, r, :], vcut[:, r, 0, :].bitcast(F32), ALU.subtract).then_inc(lo_made, 1)
            step(0)
            dve.wait_ge(c_active, 1)
            with dve.Fori(0, SUMS) as j:
                step(2 * j + 1)
                dve.wait_ge(ada_loaded, 16 * (j + 1))
                dve.tensor_tensor_reduce(junk[:], ada[:], cond[:], 1.0, 0.0, ALU.mult, ALU.add, total[:]).then_inc(summed, 1)
                step(2 * j + 2)
                dve.wait_ge(summed, j + 1)
                dve.tensor_copy(mod[:, bass.ds(half * SUMS + j, 1)], total[:]).then_inc(noted, 1)
                dve.wait_ge(noted, j + 1)
            with dve.Fori(2 * SUMS + 1, steps) as i:
                step(i)
            for h in range(2):
                dve.wait_ge(used, 2 * NKEYS - 1 + h)
                for t in range(2):
                    dst = resid[:, 2 * half + t, h * BANK:(h + 1) * BANK]
                    dve.tensor_tensor(dst, Y[:, 2 * t + h, :], dst, ALU.add).then_inc(added, 1)

        @block.tensor
        def _(pe):
            def unit(r, i, first=False, last=False):
                h, b = r % 2, r // 2
                pe.wait_ge(lo_made, i * R + r + 1)
                for t in range(2):
                    bank, rows = Y[:, 2 * t + h, :], slice(t * P, (t + 1) * P)
                    pe.matmul(bank, acut[:, b, 0, rows], vcut[:, r, 0, :], start=first, stop=False)
                    pe.matmul(bank, acut[:, b, 0, rows], vcut[:, r, 1, :], start=False, stop=False)
                    ins = pe.matmul(bank, acut[:, b, 1, rows], vcut[:, r, 0, :], start=False, stop=last)
                ins.then_inc(used, 1)

            for r in range(R):
                unit(r, 0, first=(r < 2))
            U = 2
            with pe.Fori(0, (steps - 2) // U) as j:
                for n in range(U):
                    for r in range(R):
                        unit(r, 1 + j * U + n)
            for r in range(R):
                unit(r, steps - 1, last=(r >= 2))


def peer(nc, consts, resid, mod, d):
    for half in range(2):
        with Phase(nc, f"peer{half}") as ph:
            picksT = ph.sb("picksT", [P, 3, HALF])
            with Phase(nc, f"experts{half}") as ph2:
                raw = ph2.sb("raw", [P, 4, KD // 2, P])
                tables = Tables(ph2, iota=([P, P], d["c_iota"]))
                up_ring = Early(raw, up_loads(d["w_peer_q"]))
                down_ring = Early(raw, down_loads(d["peer_v"]))
                xs = ph2.sb("xs", [P, 2, KD, HALF], F32R)
                norm_transpose(nc, f"n2{half}", consts, resid, xs, d["g_ffn"], tokens=range(2 * half, 2 * half + 2), early=[up_ring])
                act_buf = ph2.sb("act_buf", [P, NKEYS, HALF])
                peer_up(nc, consts, half, xs, d["w_peer_q"], d["peer_u"], d["peer_keys"], d["c_iota"], act_buf, picksT, up_ring, [tables])
                peer_gate(nc, half, tables["iota"], picksT, act_buf, [down_ring])
                peer_down(nc, half, d["peer_v"], act_buf, resid, down_ring, d["c"], d["w_ada"], mod)


def first_mixer(nc, consts, resid, d):
    with Phase(nc, "m1") as ph:
        gates = ph.sb("gates", [P, 3, KD, SEQ])
        rgT, zaT, zrT = gates[:, 0], gates[:, 1], gates[:, 2]
        cq = ph.sb("cq", [P, NT, MLA_QL])
        ckv = ph.sb("ckv", [P, 5, MLA_KVL + ROPE])
        mla_tables = Tables(
            ph, g_ql=([P, 3], d["g_q_lora"]), g_kvl=([P, 2], d["g_kv_lora"]), g_q=([P, QK], d["g_qk_q"].partition_broadcast(P)),
            g_k=([P, QK], d["g_qk_k"].partition_broadcast(P)), rope_mla=([P, 5, 2, ROPE], d["c_rope_mla"]),
            wq=([P, 3, MLA_H * QK], d["w_uq"].rearrange("(k p) n -> p k n", p=P)),
            wkv=([P, 2, MLA_H * (NOPE + MLA_V)], d["w_ukv"].rearrange("(k p) n -> p k n", p=P)))
        ret_tables = Tables(ph, rope_ret=([P, 5, 2, RET_DK], d["c_rope_ret"]), g_ret=([P, RET_H], d["g_ret_gn"]))
        with Phase(nc, "m1r") as ph2:
            rq = ph2.sb("rq", [P, NT, 512])
            rk = ph2.sb("rk", [P, 5, 512])
            rv = ph2.sb("rv", [P, 5, 1024])
            with Phase(nc, "m1h") as ph3:
                hs = ph3.sb("hs", [P, 2, KD, KEYS], F32R)
                ring = Early(ph3.sb("raw", [P, KD, BANK]), project_loads([(d["w_in"][:, 0:MLA_QL], None)]))
                with Phase(nc, "m1x") as ph4:
                    meta = ph4.sb("meta", [META, D])
                    norm_transpose(nc, "n1", consts, resid, hs, d["g_mix"], meta=meta, load=(d["x"], d["meta"]), early=[ring])
                w = d["w_in"]
                x_tiles = lambda dst, a, b: [(P, t * P, dst[:, t, a:b]) for t in range(NT)]
                all_tiles = lambda dst, a, b: x_tiles(dst, a, b) + [(META, SEQ, dst[0:META, NT, a:b])]
                jobs, c = [], 0
                for n, out in ((MLA_QL, ("tok", x_tiles(cq, 0, MLA_QL))), (288, ("tok", all_tiles(ckv, 0, 288))),
                               (512, ("tok", x_tiles(rq, 0, 512))), (512, ("tok", all_tiles(rk, 0, 512))),
                               (512, ("tok", all_tiles(rv, 0, 512))), (512, ("tok", all_tiles(rv, 512, 1024)))):
                    jobs.append((w[:, c:c + n], out))
                    c += n
                for g, fn in ((rgT, ACT.Silu), (zaT, ACT.Sigmoid), (zrT, ACT.Sigmoid)):
                    for half in range(2):
                        jobs.append((w[:, c:c + 512], ("feat", fn, [g[:, 4 * half + j, :] for j in range(4)])))
                        c += 512
                project(nc, "p1", hs, jobs, ring, [ret_tables])
            retention(nc, consts, rq, rk, rv, rgT, ret_tables["g_ret"], ret_tables["rope_ret"], d["c_decay"], d["c_decay_meta"], [mla_tables])
        oT = ph.sb("oT", [P, 4, SEQ])
        out_ring = Early(ph.sb("out_ring", [P, 2, D]), out_loads(d["w_mix_out"]))
        two_chunks = merge_loads(d["w_mla_out"], d["w_ret_out"])
        merge_ring = Early(ph.sb("merge_ring", [P, 2, 12, P]), lambda raw: two_chunks(raw, 0) + two_chunks(raw, 1))
        with Phase(nc, "m1a") as ph2:
            qT = ph2.sb("qT", [QK, MLA_H, SEQ])
            kT = ph2.sb("kT", [QK, MLA_H, KEYS])
            v = ph2.sb("v", [P, 5, MLA_H * MLA_V])
            causal = Tables(ph2, causal=([P, 1, KEYS], d["c_causal"]))
            mla_prepare(nc, consts, cq, ckv, mla_tables, qT, kT, v, [causal])
            attention(nc, "at1", consts, lambda h: qT[:, h, :], lambda h: kT[:, h, :], v, v[0:META, NT, :], causal["causal"],
                      META, QK ** -0.5, oT, [merge_ring])
        merge(nc, oT, rgT, zaT, zrT, d["w_mla_out"], d["w_ret_out"], merge_ring, [out_ring])
        out_project(nc, "o1", zaT, d["w_mix_out"], KD, resid, out_ring)


def modulation(nc, consts, b_dram, mod, rows):
    ident = consts["ident"]
    with Phase(nc, "ada") as ph:
        bias = ph.sb("bias", [P, 6 * KD])
        wide = ph.sb("wide", [P, 2 * KD, P])
        T = ph.ps("T", [P, 4, BANK])
        loaded, widened, turned, copied = (ph.sem(x) for x in ("loaded", "widened", "turned", "copied"))
        block = ph.block()

        @block.sync
        def _(sp):
            sp.dma_start(bias[:], b_dram).then_inc(loaded, 16)

        @block.scalar
        def _(act):
            for b in range(4):
                act.wait_ge(turned, b + 1)
                act.activation(rows[:, b // 2, (b % 2) * BANK:(b % 2 + 1) * BANK], T[:, b, :], ACT.Copy).then_inc(copied, 1)

        @block.vector
        def _(dve):
            dve.wait_ge(loaded, 16)
            dve.tensor_tensor(mod[:], mod[:], bias[:], ALU.add).then_inc(widened, 1)
            dve.wait_ge(widened, 1)
            dve.tensor_copy(wide[:, 0:KD, :], bc(mod[:, 2 * KD:3 * KD], 2, P)).then_inc(widened, 1)
            dve.tensor_copy(wide[:, KD:, :], bc(mod[:, 5 * KD:], 2, P)).then_inc(widened, 1)

        @block.tensor
        def _(pe):
            for b in range(4):
                if b % 2 == 0:
                    pe.wait_ge(widened, 2 + b // 2)
                for k in range(4):
                    ins = pe.transpose(T[:, b, k * P:(k + 1) * P], wide[:, 4 * b + k, :], ident[:])
                ins.then_inc(turned, 1)


def dilated_prepare(nc, consts, aq, ak, gains, qT, kT, early):
    ident = consts["ident"]
    H = DIL_H
    with Phase(nc, "dp") as ph:
        sq = ph.sb("sq", [P, 2, 512])
        ss8 = ph.sb("ss8", [P, 8, H])
        ms8 = ph.sb("ms8", [P, 8, H])
        rstd8 = ph.sb("rstd8", [P, 8, H])
        half = ph.sb("half", [P, H])
        T = ph.ps("T", [P, 2, BANK])
        names = ("early_landed", "squared", "summed", "means", "roots", "normed", "turned", "copied", "pool_link")
        early_landed, squared, summed, means, roots, normed, turned, copied, pool_link = (ph.sem(x) for x in names)
        jobs = [(src, c, t) for c, src in enumerate((aq, ak)) for t in range(NT)]
        block = ph.block()

        @block.sync
        def _(sp):
            load_early(sp, early_landed, early)

        @block.gpsimd
        def _(pool):
            link = Link(pool, pool_link)
            link(pool.memset(half[:], -0.5))
            for j in range(len(jobs)):
                pool.wait_ge(means, j + 1)
                pool.tensor_tensor(rstd8[:, j, :], ms8[:, j, :], half[:], ALU.pow).then_inc(roots, 1)

        @block.scalar
        def _(act):
            for j in range(len(jobs) + 2):
                if j < len(jobs):
                    src, c, t = jobs[j]
                    if j >= 2:
                        act.wait_ge(summed, j - 1)
                    act.activation(sq[:, j % 2, :], src[:, t, :], ACT.Square).then_inc(squared, 1)
                if j >= 2:
                    src, c, t = jobs[j - 2]
                    act.wait_ge(turned, j - 1)
                    act.activation((qT, kT)[c][:, :, t * P:(t + 1) * P], T[:, j % 2, :].rearrange("p (c q) -> p c q", q=P), ACT.Copy,
                                   scale=gains[c][:, 0:1]).then_inc(copied, 1)

        @block.vector
        def _(dve):
            for j in range(len(jobs) + 1):
                if j < len(jobs):
                    dve.wait_ge(squared, j + 1)
                    dve.tensor_reduce(ss8[:, j, :], sq[:, j % 2, :].rearrange("p (h e) -> p h e", e=DIL_E), AX.X, ALU.add).then_inc(summed, 1)
                    dve.wait_ge(summed, j + 1)
                    dve.tensor_scalar(ms8[:, j, :], ss8[:, j, :], 1.0 / DIL_E, EPS, ALU.mult, ALU.add).then_inc(means, 1)
                if j >= 1:
                    src, c, t = jobs[j - 1]
                    x = src[:, t, :].rearrange("p (h e) -> p h e", e=DIL_E)
                    dve.wait_ge(roots, j)
                    dve.tensor_tensor(x, x, bc(rstd8[:, j - 1, :], 2, DIL_E), ALU.mult).then_inc(normed, 1)

        @block.tensor
        def _(pe):
            for j, (src, c, t) in enumerate(jobs):
                pe.wait_ge(normed, j + 1)
                if j >= 2:
                    pe.wait_ge(copied, j - 1)
                for k in range(4):
                    ins = pe.transpose(T[:, j % 2, k * P:(k + 1) * P], src[:, t, k * P:(k + 1) * P], ident[:])
                ins.then_inc(turned, 1)


def gla(nc, consts, qkT, v, lowT, grT, tables, mixT, early):
    ident = consts["ident"]
    H, C = GLA_H, GLA_CHUNK
    NC = SEQ // C
    with Phase(nc, "gla") as ph:
        wg, bg, gn, mask, keep = (tables[n] for n in ("wg", "bg", "gn", "mask", "keep"))
        absz = ph.sb("absz", [P, 2, SEQ])
        minz = ph.sb("minz", [P, 2, SEQ])
        b = ph.sb("b", [P, 2, SEQ])
        dm = ph.sb("dm", [P, 2, SEQ])
        dl = ph.sb("dl", [P, 2, SEQ])
        e1 = ph.sb("e1", [P, 2, SEQ])
        e2 = ph.sb("e2", [P, 2, SEQ])
        e3 = ph.sb("e3", [P, 2, SEQ])
        e4 = ph.sb("e4", [P, 2, SEQ])
        qe = ph.sb("qe", [P, 2, SEQ])
        klT = ph.sb("klT", [P, NT, 2 * P])
        st = ph.sb("st", [P, NC, 2, GLA_DV])
        sm = ph.sb("sm", [P, 2, H, P])
        junk = ph.sb("junk", [P, H, P])
        ssq = ph.sb("ssq", [P, NT, H])
        ms = ph.sb("ms", [P, NT, H])
        rstd = ph.sb("rstd", [P, NT, H])
        half = ph.sb("half", [P, H])
        on = ph.sb("on", [P, 2, H, P])
        S = ph.ps("S", [P, 2, BANK])
        O = ph.ps("O", [P, 2, BANK])
        U = ph.ps("U", [P, 4, BANK])
        names = ("early_landed", "logits", "absed", "mined", "exped", "logged", "decays", "relative", "e1_done", "e2_done", "e3_done",
                 "e4_done", "kl_done", "ready", "turned", "copied", "updates", "stated", "scored", "masked", "attended",
                 "squares", "means", "roots", "normed", "oturned", "gated", "dve_link", "pool_link", "junked")
        (early_landed, logits, absed, mined, exped, logged, decays, relative, e1_done, e2_done, e3_done, e4_done, kl_done, ready,
         turned, copied, updates, stated, scored, masked, attended, squares, means, roots, normed, oturned, gated,
         dve_link, pool_link, junked) = (ph.sem(x) for x in names)
        q, k = qkT[:, 0:2, :], qkT[:, 2:4, :]
        qm, km, kl = e2, e3, e4
        chunks = lambda x: x[:].rearrange("p c (n i) -> p (c n) i", i=C)
        head = lambda h: slice(64 * (h % 2), 64 * (h % 2) + 64)
        out_of = lambda t, h: (O[:, h % 2] if t % 2 == 0 else U[:, 2 + h % 2])[:, (h // 2) * P:(h // 2 + 1) * P]
        block = ph.block()

        @block.sync
        def _(sp):
            load_early(sp, early_landed, early)

        @block.gpsimd
        def _(pool):
            link = Link(pool, pool_link)
            link(pool.memset(half[:], -0.5))
            for t in range(NT):
                pool.wait_ge(means, t + 1)
                pool.tensor_tensor(rstd[:, t, :], ms[:, t, :], half[:], ALU.pow).then_inc(roots, 1)

        @block.scalar
        def _(act):
            act.wait_ge(logits, 1)
            for c in range(2):
                ins = act.activation(absz[:, c, :], S[:, c, :], ACT.Abs, bias=bg[:, c:c + 1])
            ins.then_inc(absed, 1)
            act.wait_ge(absed, 1)
            act.activation(absz[:], absz[:], ACT.Exp, scale=-1.0).then_inc(exped, 1)
            act.wait_ge(exped, 1)
            act.activation(absz[:], absz[:], ACT.Ln, bias=1.0).then_inc(logged, 1)
            act.wait_ge(decays, 2)
            act.activation(e1[:], b[:], ACT.Exp, scale=1.0 / GLA_TAU).then_inc(e1_done, 1)
            act.wait_ge(relative, 1)
            act.activation(e4[:], dl[:], ACT.Exp, scale=1.0 / GLA_TAU).then_inc(e4_done, 1)
            act.wait_ge(relative, 2)
            act.activation(e2[:], dm[:], ACT.Exp, scale=1.0 / GLA_TAU).then_inc(e2_done, 1)
            act.activation(e3[:], dm[:], ACT.Exp, scale=-1.0 / GLA_TAU).then_inc(e3_done, 1)
            act.wait_ge(turned, 1)
            for i in range(2):
                ins = act.activation(klT[:, 2 * i:2 * i + 2, :], O[:, i, :].rearrange("p (t e) -> p t e", t=2), ACT.Copy)
            ins.then_inc(copied, 1)
            for t in range(NT):
                if t >= 1:
                    act.wait_ge(squares, t)
                act.wait_ge(attended, t + 1)
                for h in range(H):
                    ins = act.activation(junk[:, h, :], out_of(t, h), ACT.Square, accum_out=ssq[:, t, h:h + 1])
                ins.then_inc(squares, 1)

        @block.vector
        def _(dve):
            link = Link(dve, dve_link)
            dve.wait_ge(logits, 1)
            dve.wait_ge(absed, 1)
            for c in range(2):
                ins = dve.tensor_scalar(minz[:, c, :], S[:, c, :], bg[:, c:c + 1], 0.0, ALU.add, ALU.min)
            ins.then_inc(mined, 1)
            dve.wait_ge(mined, 1)
            dve.wait_ge(logged, 1)
            link(dve.tensor_tensor(minz[:], minz[:], absz[:], ALU.subtract))
            for c in range(2):
                dve.tensor_tensor_scan(b[:, c, :], keep[:], minz[:, c, :], 0.0, ALU.mult, ALU.add).then_inc(decays, 1)
            dve.wait_ge(decays, 2)
            dve.tensor_tensor(chunks(dl), bc(chunks(b)[:, :, C - 1], 2, C), chunks(b), ALU.subtract).then_inc(relative, 1)
            dve.tensor_tensor(chunks(dm), chunks(b), bc(chunks(b)[:, :, C // 2 - 1], 2, C), ALU.subtract).then_inc(relative, 1)
            dve.wait_ge(e4_done, 1)
            dve.tensor_tensor(kl[:], k, e4[:], ALU.mult).then_inc(kl_done, 1)
            dve.wait_ge(e1_done, 1)
            dve.scalar_tensor_tensor(qe[:].rearrange("p c t -> p (c t)"), q.rearrange("p c t -> p (c t)"), GLA_DK ** -0.5,
                                     e1[:].rearrange("p c t -> p (c t)"), ALU.mult, ALU.mult).then_inc(ready, 1)
            dve.wait_ge(e2_done, 1)
            dve.tensor_tensor(qm[:], q, e2[:], ALU.mult).then_inc(ready, 1)
            dve.wait_ge(e3_done, 1)
            dve.tensor_tensor(km[:], k, e3[:], ALU.mult).then_inc(ready, 1)
            link(dve.memset(st[:, 0], 0.0))
            dve.wait_ge(updates, 1)
            for n in range(1, NC):
                m = n - 1
                col = ((m // 2) % 2) * 2 * P
                for c in range(2):
                    up = U[:, (m % 2) * 2 + m // 4, col + c * P:col + (c + 1) * P]
                    ins = dve.scalar_tensor_tensor(st[:, n, c, :], st[:, m, c, :], e1[:, c, m * C + C - 1:m * C + C], up, ALU.mult, ALU.add)
                ins.then_inc(stated, 1)
                dve.wait_ge(stated, n)

            def mask_scores(t):
                dve.wait_ge(scored, t + 1)
                if t >= 2:
                    dve.wait_ge(attended, t - 1)
                for odd in range(2):
                    ins = dve.tensor_tensor(sm[:, t % 2, 2 * odd:2 * odd + 2, :], S[:, odd, 0:2 * P].rearrange("p (h i) -> p h i", i=P),
                                            bc(mask[:], 1, 2), ALU.mult)
                ins.then_inc(masked, 1)

            def norm(t):
                dve.wait_ge(squares, t + 1)
                dve.tensor_scalar(ms[:, t, :], ssq[:, t, :], 1.0 / GLA_DV, EPS, ALU.mult, ALU.add).then_inc(means, 1)
                dve.wait_ge(roots, t + 1)
                if t >= 2:
                    dve.wait_ge(oturned, t - 1)
                for h in range(H):
                    ins = dve.tensor_scalar(on[:, t % 2, h, :], out_of(t, h), rstd[:, t, h:h + 1], None, ALU.mult)
                ins.then_inc(normed, 1)

            def gate(t):
                dve.wait_ge(oturned, t + 1)
                dve.scalar_tensor_tensor(mixT[:, 0:H, t * P:(t + 1) * P], U[:, t % 2, :].rearrange("p (h i) -> p h i", i=P), gn[:, 0:1],
                                         grT[:, :, t * P:(t + 1) * P], ALU.mult, ALU.mult).then_inc(gated, 1)

            mask_scores(0)
            for t in range(NT):
                if t + 1 < NT:
                    mask_scores(t + 1)
                norm(t)
                if t >= 1:
                    gate(t - 1)
            gate(NT - 1)

        @block.tensor
        def _(pe):
            for c in range(2):
                ins = pe.matmul(S[:, c, :], wg[:, c, :], lowT[0:GLA_RANK, :], start=True, stop=True)
            ins.then_inc(logits, 1)
            pe.wait_ge(kl_done, 1)
            for t in range(NT):
                for c in range(2):
                    ins = pe.transpose(O[:, t // 2, (t % 2) * 2 * P + c * P:(t % 2) * 2 * P + (c + 1) * P], kl[:, c, t * P:(t + 1) * P], ident[:])
            ins.then_inc(turned, 1)
            pe.wait_ge(copied, 1)
            for n in range(NC - 1):
                r = slice(64 * (n % 2), 64 * (n % 2) + 64)
                col = ((n // 2) % 2) * 2 * P
                for h in range(H):
                    c0 = col + (h // 2) * P
                    ins = pe.matmul(U[head(h), (n % 2) * 2 + n // 4, c0:c0 + P], klT[r, n // 2, 64 * h:64 * h + 64],
                                    v[r, n // 2, h * P:(h + 1) * P], start=True, stop=True)
            ins.then_inc(updates, 1)
            pe.wait_ge(ready, 3)
            pe.wait_ge(mined, 1)

            def score(t):
                if t >= 1:
                    pe.wait_ge(masked, t)
                for h in range(H):
                    ins = pe.matmul(S[:, h % 2, (h // 2) * P:(h // 2 + 1) * P], km[head(h), h // 2, t * P:(t + 1) * P],
                                    qm[head(h), h // 2, t * P:(t + 1) * P], start=True, stop=True)
                ins.then_inc(scored, 1)

            def attend(t):
                pe.wait_ge(masked, t + 1)
                if t >= 2:
                    pe.wait_ge(normed, t - 1)
                pe.wait_ge(stated, 1 if t == 0 else NC - 1)
                for h in range(H):
                    out = out_of(t, h)
                    pe.matmul(out, sm[:, t % 2, 2 * (h % 2) + h // 2, :], v[:, t, h * P:(h + 1) * P], start=True, stop=True)
                    for n in (2 * t, 2 * t + 1):
                        r = slice(64 * (n % 2), 64 * (n % 2) + 64)
                        ins = pe.matmul(out[r], qe[head(h), h // 2, n * C:(n + 1) * C], st[head(h), n, h // 2, :],
                                        start=False, stop=False, skip_group_check=True)
                ins.then_inc(attended, 1)

            def turn(t):
                pe.wait_ge(normed, t + 1)
                if t >= 2:
                    pe.wait_ge(gated, t - 1)
                if t == 0:
                    pe.wait_ge(stated, NC - 1)
                for h in range(H):
                    ins = pe.transpose(U[:, t % 2, h * P:(h + 1) * P], on[:, t % 2, h, :], ident[:])
                ins.then_inc(oturned, 1)

            score(0)
            for t in range(NT):
                if t + 1 < NT:
                    score(t + 1)
                attend(t)
                if t >= 1:
                    turn(t - 1)
            turn(NT - 1)


def ffn_loads(w_dram):
    return lambda raw: [(raw[:, r], w_dram[r]) for r in range(2)]


def ffn_up(nc, hs, w_dram, cw, cb, gT, ring, early):
    R = 2
    steps = NF // R
    with Phase(nc, "ffn") as ph:
        raw = ring.raw
        cut = ph.sb("cut", [P, R, 2, 2, KD, P], F32R)
        u = ph.sb("u", [P, R, 2, SEQ])
        sl = ph.sb("sl", [P, R, SEQ])
        acc = ph.ps("acc", [P, 2 * R, BANK])
        landed = [ph.sem(f"landed{r}") for r in range(R)]
        names = ("early_landed", "hi_made", "lo_made", "done", "biased", "tap1", "conved", "silued", "out")
        early_landed, hi_made, lo_made, done, biased, tap1, conved, silued, out = (ph.sem(x) for x in names)
        block = ph.block()

        @block.sync
        def _(sp):
            def load(r, i):
                sp.dma_start(raw[:, r], w_dram[bass.ds(i * R + r, 1)].rearrange("o p g k n -> (o p) g k n")).then_inc(landed[r], 16)

            with sp.Fori(1, steps) as i:
                for r in range(R):
                    sp.wait_ge(lo_made, (i - 1) * R + r + 1)
                    load(r, i)
            load_early(sp, early_landed, early)

        @block.tensor
        def _(pe):
            def chunk(r, i):
                pe.wait_ge(lo_made, i * R + r + 1)
                for g in range(2):
                    bank = acc[:, 2 * r + g, :]
                    for k in range(KD):
                        pe.matmul(bank, cut[:, r, 0, g, k, :], hs[:, 0, k, :], start=(k == 0), stop=False)
                        pe.matmul(bank, cut[:, r, 0, g, k, :], hs[:, 1, k, :], start=False, stop=False)
                        ins = pe.matmul(bank, cut[:, r, 1, g, k, :], hs[:, 0, k, :], start=False, stop=(k == KD - 1))
                ins.then_inc(done, 1)

            for r in range(R):
                chunk(r, 0)
            with pe.Fori(1, steps) as i:
                for r in range(R):
                    pe.wait_ge(conved, (i - 1) * R + r + 1)
                    chunk(r, i)

        @block.scalar
        def _(act):
            def split(r, i, first=False):
                if not first:
                    act.wait_ge(landed[r], i * 16)
                    act.wait_ge(done, (i - 1) * R + r + 1)
                act.activation(cut[:, r, 0], raw[:, r], ACT.Copy).then_inc(hi_made, 1)

            def chunk(r, i, first=False):
                c = i * R + r
                if not first:
                    act.wait_ge(out, c - R + 1)
                act.wait_ge(done, c + 1)
                for g in range(2):
                    ins = act.activation(u[:, r, g, :], acc[:, 2 * r + g, :], ACT.Identity, bias=cb[:, bass.ds(c * 2 + g, 1)],
                                         scale=cw[:, bass.ds(c * 6 + g * 3 + 2, 1)])
                ins.then_inc(biased, 1)
                act.wait_ge(conved, c + 1)
                act.activation(sl[:, r, :], u[:, r, 0, :], ACT.Silu).then_inc(silued, 1)

            split(0, 0, first=True)
            split(1, 0, first=True)
            for r in range(R):
                split(r, 1)
                chunk(r, 0, first=True)
            with act.Fori(1, steps - 1) as i:
                for r in range(R):
                    split(r, i + 1)
                    chunk(r, i)
            for r in range(R):
                chunk(r, steps - 1)

        @block.vector
        def _(dve):
            def split(r, i):
                dve.wait_ge(hi_made, i * R + r + 1)
                dve.tensor_tensor(cut[:, r, 1], raw[:, r], cut[:, r, 0].bitcast(F32), ALU.subtract).then_inc(lo_made, 1)

            def chunk(r, i):
                c = i * R + r
                dve.wait_ge(biased, c + 1)
                for j, s in ((1, tap1), (0, conved)):
                    lag = 2 - j
                    for g in range(2):
                        ins = dve.scalar_tensor_tensor(u[:, r, g, lag:], acc[:, 2 * r + g, 0:SEQ - lag], cw[:, bass.ds(c * 6 + g * 3 + j, 1)],
                                                       u[:, r, g, lag:], ALU.mult, ALU.add)
                    ins.then_inc(s, 1)
                    if j == 1:
                        dve.wait_ge(tap1, c + 1)
                dve.wait_ge(conved, c + 1)
                dve.wait_ge(silued, c + 1)
                dve.tensor_tensor(gT[:, bass.ds(c, 1), :], sl[:, r:r + 1, :], u[:, r, 1:2, :], ALU.mult).then_inc(out, 1)

            split(0, 0)
            split(1, 0)
            with dve.Fori(0, steps - 1) as i:
                for r in range(R):
                    split(r, i + 1)
                    chunk(r, i)
            for r in range(R):
                chunk(r, steps - 1)


def second_block(nc, consts, resid, mod, d, out, stop):
    with Phase(nc, "m2") as ph:
        rows = ph.sb("rows", [P, 2, D])
        part = lambda i: mod[:, i * KD:(i + 1) * KD]
        modulation(nc, consts, d["b_ada"], mod, rows)
        with Phase(nc, "m2m") as ph2:
            mixT = ph2.sb("mixT", [P, KD, SEQ])
            out_ring = Early(ph2.sb("out_ring", [P, 2, D]), out_loads(d["w_out_2"]))
            aq, ak, av = (ph2.sb(n, [P, NT, 512]) for n in ("aq", "ak", "av"))
            dilated = Tables(ph2, g_q=([P, 1], d["q_norm_g"]), g_k=([P, 1], d["k_norm_g"]), table=([P, DIL_H, SEQ], d["c_dilated"]))
            with Phase(nc, "m2g") as ph3:
                gla_tables = Tables(ph3, wg=([GLA_RANK, 2, P], d["gla_w_gate"].rearrange("r (c p) -> r c p", p=P)), bg=([P, 2], d["gla_b_gate"]),
                                    gn=([P, 1], d["gla_norm_g"]), mask=([P, P], d["c_gla_mask"]), keep=([P, SEQ], d["c_scan_keep"]))
                qkT = ph3.sb("qkT", [P, 4, SEQ])
                gv = ph3.sb("gv", [P, NT, 512])
                grT = ph3.sb("grT", [P, 4, SEQ])
                lowT = ph3.sb("lowT", [GLA_RANK, SEQ])
                with Phase(nc, "m2h") as ph4:
                    hs = ph4.sb("hs", [P, 2, KD, SEQ], F32R)
                    ring = Early(ph4.sb("raw", [P, KD, BANK]), project_loads([(d["w_in_2"][:, 0:512], None)]))
                    norm_transpose(nc, "n3", consts, resid, hs, d["norm1_g"], mod=(part(1), part(0)), early=[ring])
                    tok = lambda dst: ("tok", [(P, t * P, dst[:, t, :]) for t in range(NT)])
                    feat = lambda fn, dst: ("feat", fn, [dst[:, j, :] for j in range(4)])
                    jobs, c = [], 0
                    for n, o in ((512, feat(ACT.Copy, qkT)), (512, tok(gv)), (512, feat(ACT.Silu, grT)),
                                 (GLA_RANK, ("feat", ACT.Copy, [lowT[:, :]])), (512, tok(aq)), (512, tok(ak)), (512, tok(av))):
                        jobs.append((d["w_in_2"][:, c:c + n], o))
                        c += n
                    project(nc, "p3", hs, jobs, ring, [gla_tables])
                gla(nc, consts, qkT, gv, lowT, grT, gla_tables, mixT, [dilated])
            with Phase(nc, "m2a") as ph3:
                qT = ph3.sb("qT", [P, 4, SEQ])
                kT = ph3.sb("kT", [P, 4, SEQ])
                dilated_prepare(nc, consts, aq, ak, (dilated["g_q"], dilated["g_k"]), qT, kT, ())
                at = lambda x: lambda h: x[64 * (h % 2):64 * (h % 2) + 64, h // 2, :]
                attention(nc, "at2", consts, at(qT), at(kT), av, None, dilated["table"], 0, DIL_E ** -0.5, mixT[:, 4:8, :], [out_ring])
            out_project(nc, "o2", mixT, d["w_out_2"], KD, resid, out_ring, gate=rows[:, 0, :])
        if stop == 3:
            return
        gT = ph.sb("gT", [P, NF, SEQ])
        out_ring = Early(ph.sb("down_ring", [P, 2, D]), out_loads(d["w_down"]))
        with Phase(nc, "m2f") as ph2:
            ring = Early(ph2.sb("raw", [P, 2, 2, KD, P]), ffn_loads(d["w_up"]))
            conv = Tables(ph2, cw=([P, NF * 6], d["conv_w"].rearrange("p i g j -> p (i g j)")), cb=([P, NF * 2], d["conv_b"].rearrange("p i g -> p (i g)")))
            hs = ph2.sb("hs", [P, 2, KD, SEQ], F32R)
            norm_transpose(nc, "n4", consts, resid, hs, d["norm2_g"], mod=(part(4), part(3)), early=[ring, conv])
            ffn_up(nc, hs, d["w_up"], conv["cw"], conv["cb"], gT, ring, [out_ring])
        out_project(nc, "o3", gT, d["w_down"], NF, resid, out_ring, gate=rows[:, 1, :], out_dram=out)


def program(nc, d, out, stop=9):
    Phase.past = []
    with Phase(nc, "all") as ph:
        resid = ph.sb("resid", [P, NT, D])
        ident = ph.sb("ident", [P, P])
        mod = ph.sb("mod", [P, 6 * KD])
        consts = {"ident": ident}
        with Phase(nc, "c") as ph2:
            s = ph2.sem("consts")
            block = ph2.block()

            @block.sync
            def _(sp):
                sp.dma_start(ident[:], d["c_ident"]).then_inc(s, 16)
                sp.wait_ge(s, 16)
        first_mixer(nc, consts, resid, d)
        if stop > 1:
            peer(nc, consts, resid, mod, d)
        if stop > 2:
            second_block(nc, consts, resid, mod, d, out, stop)
        if stop < 4:
            with Phase(nc, "dump") as ph2:
                s = ph2.sem("dumped")
                block = ph2.block()

                @block.sync
                def _(sp):
                    sp.dma_start(out.rearrange("(t p) n -> p t n", p=P), resid[:]).then_inc(s, 16)
                    sp.wait_ge(s, 16)


def lay_out(inputs):
    a = {k: np.asarray(v) for k, v in inputs.items()}
    cols = lambda g: np.ascontiguousarray(g.reshape(-1, P).T)
    o = {"x": a["x"][0], "meta": a["meta_tokens"]}
    for n in ("w_in", "w_uq", "w_ukv", "w_mla_out", "w_ret_out", "w_mix_out"):
        o[n] = a[n][0]
    for n in ("g_mix", "g_q_lora", "g_kv_lora", "g_ret_gn", "g_ffn"):
        o[n] = cols(a[n][0])
    o["g_qk_q"], o["g_qk_k"] = a["g_qk_q"][0], a["g_qk_k"][0]
    o["peer_keys"] = np.concatenate([a["peer_keys_1"][0].T, a["peer_keys_2"][0].T], 0)
    o["w_peer_q"] = a["w_peer_q"][0].reshape(KD, P, PEER_H, P).transpose(2, 1, 0, 3)
    o["peer_u"] = a["peer_u"][0].reshape(P, P, KD, P).transpose(1, 3, 2, 0)
    o["peer_v"] = a["peer_v"][0].reshape(P, P, D)
    o["c"] = a["c_2"][0]
    o["w_ada"] = a["w_ada_2"][0].T
    o["b_ada"] = cols(a["b_ada_2"][0])
    for n in ("norm1_g", "norm2_g"):
        o[n] = cols(a[n + "_2"][0])
    o["w_in_2"], o["w_out_2"], o["w_down"] = a["w_in_2"][0], a["w_out_2"][0], a["w_down_2"][0]
    o["gla_w_gate"], o["gla_b_gate"] = a["gla_w_gate_2"][0], cols(a["gla_b_gate_2"][0])
    o["gla_norm_g"] = cols(a["gla_norm_g_2"][0])
    o["q_norm_g"] = cols(np.concatenate([a["q_norm_g_2"][0]] * 2))
    o["k_norm_g"] = cols(np.concatenate([a["k_norm_g_2"][0]] * 2))
    o["w_up"] = a["w_up_2"][0].reshape(KD, P, 2, NF, P).transpose(3, 1, 2, 0, 4)
    o["conv_w"] = a["conv_w_2"][0].reshape(3, 2, NF, P).transpose(3, 2, 1, 0)
    o["conv_b"] = a["conv_b_2"][0].reshape(2, NF, P).transpose(2, 1, 0)
    o.update(shape_constants())
    return {k: np.ascontiguousarray(v) for k, v in o.items()}


def build(nc, arrays, stop=9):
    d = {n: nc.dram_tensor(f"in_{n}", a.shape, mybir.dt.from_np(a.dtype), kind="ExternalInput").ap() for n, a in arrays.items()}
    out = nc.dram_tensor("out", (SEQ, D), F32, kind="ExternalOutput").ap()
    program(nc, d, out, stop)


def kernel(**inputs):
    import concourse.bacc as bacc
    from concourse.bass_utils import run_bass_kernel_spmd

    arrays = lay_out(inputs)
    nc = bacc.Bacc("TRN2", target_bir_lowering=False, num_devices=1)
    build(nc, arrays)
    r = run_bass_kernel_spmd(nc, [{f"in_{n}": a for n, a in arrays.items()}], core_ids=[0])
    return r.results[0]["out"].reshape(1, SEQ, D)
```

```python
from contextlib import ExitStack

import numpy as np
import concourse.bass as bass
from concourse import mybir
from concourse.alu_op_type import AluOpType as ALU

ACT = mybir.ActivationFunctionType
AX = mybir.AxisListType
F32 = mybir.dt.float32
F32R = mybir.dt.float32r
U32 = mybir.dt.uint32

P = 128
D = 1024
KD = D // P
SEQ = 512
NT = SEQ // P
META = 16
KEYS = SEQ + META
EPS = 1e-6
NEG = -1e30
BANK = 512

MLA_H, MLA_QL, MLA_KVL, NOPE, ROPE, MLA_V = 8, 384, 256, 64, 32, 64
QK = NOPE + ROPE
RET_H, RET_DK, RET_DV = 8, 64, 128
PEER_H, NKEYS, TOPK = 8, 128, 16
PICKS = PEER_H * TOPK
HALF = SEQ // 2
GLA_H, GLA_DK, GLA_DV, GLA_CHUNK, GLA_RANK, GLA_TAU = 4, 64, 128, 64, 16, 16.0
DIL_H, DIL_E = 8, 64
DFF = 2816
NF = DFF // P


def shape_constants():
    out = {}
    pos = np.concatenate([META + np.arange(SEQ), np.arange(META)]).astype(np.float32)

    def rope_table(half, heads_dim):
        inv = (10000.0 ** (-np.arange(half, dtype=np.float32) / half)).astype(np.float32)
        ang = pos[:, None] * inv[None, :]
        c, s = np.cos(ang), np.sin(ang)
        full = np.zeros((5 * P, 2, 2 * half), np.float32)
        full[:KEYS, 0] = np.concatenate([c, c], 1)
        full[:KEYS, 1] = np.concatenate([-s, s], 1)
        return full.reshape(5, P, 2, 2 * half).transpose(1, 0, 2, 3).copy()

    out["c_rope_ret"] = rope_table(RET_DK // 2, RET_DK)
    out["c_rope_mla"] = rope_table(ROPE // 2, ROPE)
    p = np.arange(P)[:, None].astype(np.float64)
    gamma = 1.0 - 2.0 ** (-5.0 - np.arange(RET_H))
    c = np.arange(SEQ)[None, :].astype(np.float64)
    diff = c - p
    dec = np.where(diff >= 0, gamma[:, None, None] ** np.maximum(diff, 0)[None], 0.0)
    out["c_decay"] = (dec * RET_DK ** -0.5).transpose(1, 0, 2).astype(np.float32).copy()
    dm = META + c - p[:META]
    out["c_decay_meta"] = (gamma[:, None, None] ** dm[None] * RET_DK ** -0.5).transpose(1, 0, 2).astype(np.float32).copy()
    col = np.arange(KEYS)[None, :]
    delta = META + 3 * P + p - col
    out["c_causal"] = np.where(delta >= 0, 0.0, NEG).astype(np.float32)[:, None, :].copy()
    delta = 3 * P + p - np.arange(SEQ)[None, :]
    mult = (delta <= 128).astype(int) + (delta % 4 == 0) + (delta % 16 == 0)
    scale = DIL_E ** -0.5
    bias = []
    for h in range(DIL_H):
        slope = 2.0 ** (-8.0 * (h + 1) / DIL_H)
        b = (-slope * delta + np.log(np.maximum(mult, 1))) / scale
        bias.append(np.where((delta >= 0) & (mult > 0), b, NEG))
    out["c_dilated"] = np.stack(bias, 1).astype(np.float32)
    j, i = np.arange(P)[:, None], np.arange(P)[None, :]
    out["c_gla_mask"] = np.where((j <= i) & (j // GLA_CHUNK == i // GLA_CHUNK), GLA_DK ** -0.5, 0.0).astype(np.float32)
    keep = np.ones((P, SEQ), np.float32)
    keep[:, ::GLA_CHUNK] = 0.0
    out["c_scan_keep"] = keep
    out["c_ident"] = np.eye(P, dtype=np.float32)
    out["c_iota"] = np.tile(np.arange(P, dtype=np.float32), (P, 1))
    return out


class Link:

    def __init__(self, engine, sem):
        self.engine, self.sem, self.n = engine, sem, 0

    def __call__(self, ins):
        ins.then_inc(self.sem, 1)
        self.n += 1
        self.engine.wait_ge(self.sem, self.n)


class Phase:

    KEEP = 90
    past = []

    def __init__(self, nc, name):
        self.nc, self.name, self.stack, self.sems = nc, name, ExitStack(), []

    def __enter__(self):
        return self

    def __exit__(self, *a):
        self.stack.__exit__(*a)
        Phase.past.extend(self.sems)
        if len(Phase.past) > Phase.KEEP:
            self.nc.clear_and_free_semaphores(Phase.past)
            self.nc.all_engine_barrier(sem_only=True)
            Phase.past = []

    def sb(self, name, shape, dt=F32):
        return self.stack.enter_context(self.nc.sbuf_tensor(f"{self.name}_{name}", list(shape), dt))

    def ps(self, name, shape, dt=F32):
        return self.stack.enter_context(self.nc.psum_tensor(f"{self.name}_{name}", list(shape), dt))

    def sem(self, name):
        self.sems.append(self.nc.alloc_semaphore(name=f"{self.name}_{name}"))
        return self.sems[-1]

    def block(self):
        return self.stack.enter_context(self.nc.Block())


def bc(ap, axis, n):
    v = ap.unsqueeze(axis)
    shape = list(v.shape)
    shape[axis] = n
    return v.to_broadcast(shape)


class Early:

    def __init__(self, raw, loads):
        self.raw, self.loads = raw, loads(raw)


class Tables:

    def __init__(self, ph, **tables):
        self.tiles = {name: ph.sb(name, shape) for name, (shape, _) in tables.items()}
        self.loads = [(self.tiles[name][:], src) for name, (_, src) in tables.items()]

    def __getitem__(self, name):
        return self.tiles[name]


def load_early(sp, sem, early):
    loads = [x for e in early for x in e.loads]
    for dst, src in loads:
        sp.dma_start(dst, src).then_inc(sem, 16)
    if loads:
        sp.wait_ge(sem, 16 * len(loads))


def norm_transpose(nc, name, consts, resid, hs, gain_dram, meta=None, mod=None, load=None, tokens=range(NT), early=()):
    ident = consts["ident"]
    with Phase(nc, name) as ph:
        gain = ph.sb("gain", [P, KD])
        shift = ph.sb("shift", [P, KD])
        fac = ph.sb("fac", [P, KD])
        ssq = ph.sb("ssq", [P, 5])
        ms = ph.sb("ms", [P, 5])
        rstd = ph.sb("rstd", [P, 5])
        half = ph.sb("half", [P, 5])
        junk = ph.ps("junk", [P, D])
        xn = ph.sb("xn", [P, 2, D])
        whole = ph.sb("whole", [P, 2, KD, P])
        tp = ph.ps("tp", [P, 4, BANK])
        loaded = [ph.sem(f"loaded{t}") for t in range(NT + 1)]
        early_landed, gained, sums, means, roots, scaled, turned = (
            ph.sem(n) for n in ("early_landed", "gained", "sums", "means", "roots", "scaled", "turned"))
        act_out, dve_out, hi_made, lo_made, lo_dve, ready, dve_link, pool_link = (
            ph.sem(n) for n in ("act_out", "dve_out", "hi_made", "lo_made", "lo_dve", "ready", "dve_link", "pool_link"))
        tiles = [(t, P, i * P) for i, t in enumerate(tokens)] + ([(NT, META, SEQ)] if meta is not None else [])
        src = lambda t, rows: resid[:, t, :] if t < NT else meta[0:META, :]
        block = ph.block()

        @block.sync
        def _(sp):
            sp.dma_start(gain[:], gain_dram).then_inc(gained, 16)
            if load is not None:
                x_dram, meta_dram = load
                for t in range(NT):
                    sp.dma_start(resid[:, t, :], x_dram[t * P:(t + 1) * P, :]).then_inc(loaded[t], 16)
                sp.dma_start(meta[0:META, :], meta_dram).then_inc(loaded[NT], 16)
            load_early(sp, early_landed, early)

        @block.scalar
        def _(act):
            for i, (t, rows, col) in enumerate(tiles):
                if load is not None:
                    act.wait_ge(loaded[t], 16)
                act.activation(junk[0:rows, :], src(t, rows), ACT.Square, accum_out=ssq[0:rows, t:t + 1]).then_inc(sums, 1)
                act.wait_ge(sums, i + 1)
            act.wait_ge(ready, 1)
            for i, (t, rows, col) in enumerate(tiles):
                act.wait_ge(turned, 2 * i + 1)
                if i >= 2:
                    act.wait_ge(lo_made, i - 1)
                    act.wait_ge(lo_dve, i - 1)
                for k in range(4):
                    ins = act.activation(whole[:, i % 2, k, 0:rows], tp[:, (2 * i) % 4, k * P:k * P + rows], ACT.Identity,
                                         bias=shift[:, k:k + 1], scale=fac[:, k:k + 1])
                ins.then_inc(act_out, 1)
                act.wait_ge(act_out, i + 1)
                act.wait_ge(dve_out, i + 1)
                act.activation(hs[:, 0, :, col:col + rows], whole[:, i % 2, :, 0:rows], ACT.Copy).then_inc(hi_made, 1)

        @block.gpsimd
        def _(pool):
            link = Link(pool, pool_link)
            link(pool.memset(half[:], -0.5))

            def split(i):
                t, rows, col = tiles[i]
                pool.wait_ge(hi_made, i + 1)
                pool.tensor_tensor(hs[:, 1, 0:4, col:col + rows], whole[:, i % 2, 0:4, 0:rows],
                                   hs[:, 0, 0:4, col:col + rows].bitcast(F32), ALU.subtract).then_inc(lo_made, 1)

            for i, (t, rows, col) in enumerate(tiles):
                if i >= 3:
                    split(i - 3)
                pool.wait_ge(means, i + 1)
                pool.tensor_tensor(rstd[0:rows, t:t + 1], ms[0:rows, t:t + 1], half[0:rows, t:t + 1], ALU.pow).then_inc(roots, 1)
            for i in range(max(0, len(tiles) - 3), len(tiles)):
                split(i)

        @block.vector
        def _(dve):
            link = Link(dve, dve_link)
            dve.wait_ge(gained, 16)
            if mod is None:
                link(dve.memset(shift[:], 0.0))
                dve.tensor_copy(fac[:], gain[:]).then_inc(ready, 1)
            else:
                sc, sh = mod
                link(dve.tensor_copy(shift[:], sh))
                dve.scalar_tensor_tensor(fac[:], sc, 1.0, gain[:], ALU.add, ALU.mult).then_inc(ready, 1)
            dve.wait_ge(ready, 1)
            n = len(tiles)
            for i in range(n + 2):
                if i < n:
                    t, rows, col = tiles[i]
                    dve.wait_ge(sums, i + 1)
                    dve.tensor_scalar(ms[0:rows, t:t + 1], ssq[0:rows, t:t + 1], 1.0 / D, EPS, ALU.mult, ALU.add).then_inc(means, 1)
                    dve.wait_ge(roots, i + 1)
                    if i >= 2:
                        dve.wait_ge(turned, 2 * (i - 1))
                    dve.tensor_scalar(xn[0:rows, i % 2, :], src(t, rows), rstd[0:rows, t:t + 1], None, ALU.mult).then_inc(scaled, 1)
                if 1 <= i <= n:
                    t, rows, col = tiles[i - 1]
                    dve.wait_ge(turned, 2 * i)
                    if i >= 3:
                        dve.wait_ge(lo_made, i - 2)
                        dve.wait_ge(lo_dve, i - 2)
                    for k in range(4):
                        ins = dve.tensor_scalar(whole[:, (i - 1) % 2, 4 + k, 0:rows], tp[:, (2 * i - 1) % 4, k * P:k * P + rows],
                                                fac[:, 4 + k:5 + k], shift[:, 4 + k:5 + k], ALU.mult, ALU.add)
                    ins.then_inc(dve_out, 1)
                if i >= 2:
                    t, rows, col = tiles[i - 2]
                    dve.wait_ge(hi_made, i - 1)
                    dve.tensor_tensor(hs[:, 1, 4:, col:col + rows], whole[:, (i - 2) % 2, 4:, 0:rows],
                                      hs[:, 0, 4:, col:col + rows].bitcast(F32), ALU.subtract).then_inc(lo_dve, 1)

        @block.tensor
        def _(pe):
            for i, (t, rows, col) in enumerate(tiles):
                pe.wait_ge(scaled, i + 1)
                if i >= 2:
                    pe.wait_ge(act_out, i - 1)
                for k in range(4):
                    ins = pe.transpose(tp[:, (2 * i) % 4, k * P:k * P + rows], xn[0:rows, i % 2, k * P:(k + 1) * P], ident[0:rows, 0:rows])
                ins.then_inc(turned, 1)
                if i >= 2:
                    pe.wait_ge(dve_out, i - 1)
                for k in range(4, 8):
                    ins = pe.transpose(tp[:, (2 * i + 1) % 4, (k - 4) * P:(k - 4) * P + rows], xn[0:rows, i % 2, k * P:(k + 1) * P], ident[0:rows, 0:rows])
                ins.then_inc(turned, 1)


class HeadNorm:

    FIRST, STEP = 2 * KD + 5, 3
    TURN, TAKE = 2, 8
    BANKS = 2

    def __init__(self, ph, consts, aq, ak, gains, qT, kT):
        H = DIL_H
        self.ident = consts["ident"]
        self.items = [(src, c, t) for c, src in enumerate((aq, ak)) for t in range(NT)]
        self.gains, self.dst = gains, (qT, kT)
        self.sq = ph.sb("sq", [P, 2, 512])
        self.ss8, self.ms8, self.rstd8 = (ph.sb(n, [P, 8, H]) for n in ("ss8", "ms8", "rstd8"))
        self.half = ph.sb("half", [P, H])
        names = ("squared", "summed", "means", "roots", "normed", "turned", "copied", "halved")
        self.squared, self.summed, self.means, self.roots, self.normed, self.turned, self.copied, self.halved = (ph.sem(x) for x in names)

    def item(self, u, after=0):
        j, rest = divmod(u - after - self.FIRST, self.STEP)
        return j if rest == 0 and 0 <= j < len(self.items) else None

    def scalar(self, act, u, T):
        j = self.item(u)
        if j is not None:
            src, c, t = self.items[j]
            if j >= 2:
                act.wait_ge(self.summed, j - 1)
            act.activation(self.sq[:, j % 2, :], src[:, t, :], ACT.Square).then_inc(self.squared, 1)
        j = self.item(u, self.TAKE)
        if j is not None:
            src, c, t = self.items[j]
            act.wait_ge(self.turned, j + 1)
            act.activation(self.dst[c][:, :, t * P:(t + 1) * P], T[:, j % 2, :].rearrange("p (c q) -> p c q", q=P), ACT.Copy,
                           scale=self.gains[c][:, 0:1]).then_inc(self.copied, 1)

    def vector(self, dve, u):
        j = self.item(u)
        if j is not None:
            dve.wait_ge(self.squared, j + 1)
            dve.tensor_reduce(self.ss8[:, j, :], self.sq[:, j % 2, :].rearrange("p (h e) -> p h e", e=DIL_E), AX.X, ALU.add).then_inc(self.summed, 1)
            dve.wait_ge(self.summed, j + 1)
            dve.tensor_scalar(self.ms8[:, j, :], self.ss8[:, j, :], 1.0 / DIL_E, EPS, ALU.mult, ALU.add).then_inc(self.means, 1)
        j = self.item(u, self.TURN - 1)
        if j is not None:
            src, c, t = self.items[j]
            x = src[:, t, :].rearrange("p (h e) -> p h e", e=DIL_E)
            dve.wait_ge(self.roots, j + 1)
            dve.tensor_tensor(x, x, bc(self.rstd8[:, j, :], 2, DIL_E), ALU.mult).then_inc(self.normed, 1)

    def gpsimd(self, pool):
        pool.memset(self.half[:], -0.5).then_inc(self.halved, 1)
        pool.wait_ge(self.halved, 1)
        for j in range(len(self.items)):
            pool.wait_ge(self.means, j + 1)
            pool.tensor_tensor(self.rstd8[:, j, :], self.ms8[:, j, :], self.half[:], ALU.pow).then_inc(self.roots, 1)

    def tensor(self, pe, u, T):
        j = self.item(u, self.TURN)
        if j is not None:
            src, c, t = self.items[j]
            pe.wait_ge(self.normed, j + 1)
            if j >= 2:
                pe.wait_ge(self.copied, j - 1)
            for k in range(4):
                ins = pe.transpose(T[:, j % 2, k * P:(k + 1) * P], src[:, t, k * P:(k + 1) * P], self.ident[:])
            ins.then_inc(self.turned, 1)


def project_loads(jobs):
    wd = jobs[0][0]
    return lambda raw: [(raw[:, k, 0:wd.shape[1]], wd[k * P:(k + 1) * P, :]) for k in range(KD)]


def project(nc, name, hs, jobs, ring, early=(), guest=None):
    RAW, CUT, AHEAD = KD, 4, 3
    with Phase(nc, name) as ph:
        raw = ring.raw
        cut = ph.sb("cut", [P, CUT, 2, BANK], F32R)
        NB = 6 if guest is not None else 8
        acc = ph.ps("acc", [P, 8, BANK])
        T = acc[:, NB:8, :]
        landed = [ph.sem(f"landed{i}") for i in range(RAW)]
        early_landed, hi_made, lo_made, used, done, tok_out, feat_out = (
            ph.sem(n) for n in ("early_landed", "hi_made", "lo_made", "used", "done", "tok_out", "feat_out"))
        units = [(i, k) for i in range(len(jobs)) for k in range(KD)]
        outs = [(o[1] if o[0] == "tok" else o[2]) for _, o in jobs]
        first_out = np.cumsum([0] + [len(o) for o in outs]).tolist()
        left, n_tok, n_feat = [], 0, 0
        for i, (_, o) in enumerate(jobs):
            for _ in outs[i]:
                if o[0] == "tok":
                    n_tok += 1
                    left.append((tok_out, n_tok))
                else:
                    n_feat += 1
                    left.append((feat_out, n_feat))

        def freed(u):
            i, k = units[u]
            return (used, i * (KD - 1) + k + 1) if k < KD - 1 else (done, first_out[i + 1])

        block = ph.block()

        @block.sync
        def _(sp):
            for u, (i, k) in enumerate(units):
                if u < RAW:
                    continue
                sp.wait_ge(lo_made, u - RAW + 1)
                wd = jobs[i][0]
                sp.dma_start(raw[:, u % RAW, 0:wd.shape[1]], wd[k * P:(k + 1) * P, :]).then_inc(landed[u % RAW], 16)
            load_early(sp, early_landed, early)

        if guest is not None:
            @block.gpsimd
            def _(pool):
                guest.gpsimd(pool)

        @block.tensor
        def _(pe):
            for u, (i, k) in enumerate(units):
                wd, out = jobs[i]
                n = wd.shape[1]
                hi, lo = cut[:, u % CUT, 0], cut[:, u % CUT, 1]
                pe.wait_ge(lo_made, u + 1)
                for j, dst in enumerate(outs[i]):
                    o = first_out[i] + j
                    if k == 0 and o >= NB:
                        pe.wait_ge(*left[o - NB])
                    first, last = k == 0, k == KD - 1
                    if out[0] == "tok":
                        rows, col, _ = dst
                        bank = acc[0:rows, o % NB, 0:n]
                        pe.matmul(bank, hs[:, 0, k, col:col + rows], hi[:, 0:n], start=first, stop=False)
                        pe.matmul(bank, hs[:, 0, k, col:col + rows], lo[:, 0:n], start=False, stop=False)
                        ins = pe.matmul(bank, hs[:, 1, k, col:col + rows], hi[:, 0:n], start=False, stop=last)
                    else:
                        c = slice(j * P, min((j + 1) * P, n))
                        bank = acc[0:c.stop - c.start, o % NB, :]
                        pe.matmul(bank, hi[:, c], hs[:, 0, k, 0:SEQ], start=first, stop=False)
                        pe.matmul(bank, hi[:, c], hs[:, 1, k, 0:SEQ], start=False, stop=False)
                        ins = pe.matmul(bank, lo[:, c], hs[:, 0, k, 0:SEQ], start=False, stop=last)
                    if last:
                        ins.then_inc(done, 1)
                if k < KD - 1:
                    ins.then_inc(used, 1)
                if guest is not None:
                    guest.tensor(pe, u, T)

        @block.vector
        def _(dve):
            def copy_out(i):
                wd, out = jobs[i]
                if out[0] == "tok":
                    for j, (rows, col, dst) in enumerate(outs[i]):
                        o = first_out[i] + j
                        dve.wait_ge(done, o + 1)
                        dve.tensor_copy(dst, acc[0:rows, o % NB, 0:wd.shape[1]]).then_inc(tok_out, 1)

            for u, (i, k) in enumerate(units):
                n = jobs[i][0].shape[1]
                if k == AHEAD and i >= 1:
                    copy_out(i - 1)
                dve.wait_ge(hi_made, u + 1)
                dve.tensor_tensor(cut[:, u % CUT, 1, 0:n], raw[:, u % RAW, 0:n], cut[:, u % CUT, 0, 0:n].bitcast(F32),
                                  ALU.subtract).then_inc(lo_made, 1)
                if guest is not None:
                    guest.vector(dve, u)
            copy_out(len(jobs) - 1)

        @block.scalar
        def _(act):
            def copy_out(i):
                out = jobs[i][1]
                if out[0] == "feat":
                    for j, dst in enumerate(outs[i]):
                        o = first_out[i] + j
                        act.wait_ge(done, o + 1)
                        act.activation(dst, acc[0:dst.shape[0], o % NB, :], out[1]).then_inc(feat_out, 1)

            for u, (i, k) in enumerate(units):
                n = jobs[i][0].shape[1]
                if k == AHEAD and i >= 1:
                    copy_out(i - 1)
                if u >= RAW:
                    act.wait_ge(landed[u % RAW], 16 * (u // RAW))
                if u >= CUT:
                    act.wait_ge(*freed(u - CUT))
                act.activation(cut[:, u % CUT, 0, 0:n], raw[:, u % RAW, 0:n], ACT.Copy).then_inc(hi_made, 1)
                if guest is not None:
                    guest.scalar(act, u, T)
            copy_out(len(jobs) - 1)


def out_loads(w_dram):
    return lambda raw: [(raw[:, r, :], w_dram[r * P:(r + 1) * P, :]) for r in range(2)]


def out_project(nc, name, actT, w_dram, kchunks, resid, ring, gate=None, out_dram=None):
    R = 2
    steps = kchunks // R
    with Phase(nc, name) as ph:
        raw = ring.raw
        wcut = ph.sb("wcut", [P, R, 2, D], F32R)
        acut = ph.sb("acut", [P, R, 2, SEQ], F32R)
        tmp = ph.sb("tmp", [P, 2, BANK])
        acc = ph.ps("acc", [P, 8, BANK])
        landed = [ph.sem(f"landed{i}") for i in range(R)]
        hi_made, lo_made, used, done, gated, added, stored = (
            ph.sem(n) for n in ("hi_made", "lo_made", "used", "done", "gated", "added", "stored"))
        block = ph.block()

        @block.sync
        def _(sp):
            def load(r, i):
                sp.dma_start(raw[:, r, :], w_dram[bass.ds((i * R + r) * P, P), :]).then_inc(landed[r], 16)

            with sp.Fori(1, steps) as i:
                for r in range(R):
                    sp.wait_ge(lo_made, (i - 1) * R + r + 1)
                    load(r, i)
            if out_dram is not None:
                for t in range(NT):
                    sp.wait_ge(added, 2 * (t + 1))
                    sp.dma_start(out_dram[t * P:(t + 1) * P, :], resid[:, t, :]).then_inc(stored, 16)
                sp.wait_ge(stored, 16 * NT)

        @block.scalar
        def _(act):
            def split(r, i, first=False):
                if not first:
                    act.wait_ge(landed[r], i * 16)
                    act.wait_ge(used, (i - 1) * R + r + 1)
                act.activation(acut[:, r, 0:1, :], actT[:, bass.ds(i * R + r, 1), :], ACT.Copy)
                act.activation(wcut[:, r, 0, :], raw[:, r, :], ACT.Copy).then_inc(hi_made, 1)

            for r in range(R):
                split(r, 0, first=True)
            with act.Fori(1, steps) as i:
                for r in range(R):
                    split(r, i)

        @block.tensor
        def _(pe):
            def product(o, r, first=False, last=False):
                t, h = divmod(o, 2)
                rows, cols = slice(t * P, (t + 1) * P), slice(h * BANK, (h + 1) * BANK)
                pe.matmul(acc[:, o, :], acut[:, r, 0, rows], wcut[:, r, 0, cols], start=first, stop=False)
                pe.matmul(acc[:, o, :], acut[:, r, 0, rows], wcut[:, r, 1, cols], start=False, stop=False)
                return pe.matmul(acc[:, o, :], acut[:, r, 1, rows], wcut[:, r, 0, cols], start=False, stop=last)

            def chunk(r, i, first=False):
                pe.wait_ge(lo_made, i * R + r + 1)
                for o in range(2 * NT):
                    ins = product(o, r, first=first)
                ins.then_inc(used, 1)

            for r in range(R):
                chunk(r, 0, first=(r == 0))
            with pe.Fori(1, steps - 1) as i:
                for r in range(R):
                    chunk(r, i)
            LEAD = 5
            pe.wait_ge(lo_made, kchunks - 1)
            for o in range(2 * NT + LEAD):
                if o < 2 * NT:
                    product(o, 0)
                if o == LEAD:
                    pe.wait_ge(lo_made, kchunks)
                if o >= LEAD:
                    product(o - LEAD, 1, last=True).then_inc(done, 1)

        @block.vector
        def _(dve):
            with dve.Fori(0, steps) as i:
                for r in range(R):
                    dve.wait_ge(hi_made, i * R + r + 1)
                    dve.tensor_tensor(acut[:, r, 1:2, :], actT[:, bass.ds(i * R + r, 1), :], acut[:, r, 0:1, :].bitcast(F32), ALU.subtract)
                    dve.tensor_tensor(wcut[:, r, 1, :], raw[:, r, :], wcut[:, r, 0, :].bitcast(F32), ALU.subtract).then_inc(lo_made, 1)
            for i in range(2 * NT):
                t, h = divmod(i, 2)
                dst = resid[:, t, h * BANK:(h + 1) * BANK]
                dve.wait_ge(done, i + 1)
                if gate is None:
                    dve.tensor_tensor(dst, acc[:, i, :], dst, ALU.add).then_inc(added, 1)
                else:
                    dve.tensor_tensor(tmp[:, i % 2, :], acc[:, i, :], gate[:, h * BANK:(h + 1) * BANK], ALU.mult).then_inc(gated, 1)
                    dve.wait_ge(gated, i + 1)
                    dve.tensor_tensor(dst, tmp[:, i % 2, :], dst, ALU.add).then_inc(added, 1)


def attention(nc, name, consts, qT, kT, v, vmeta, table, meta, scale, oT, early):
    ident = consts["ident"]
    keys = meta + SEQ
    H = 8
    nh = table.shape[1]
    with Phase(nc, name) as ph:
        s = ph.sb("s", [P, 3, keys])
        prob = ph.sb("prob", [P, 3, keys])
        probT = ph.sb("probT", [P, 2, NT, SEQ])
        probTm = ph.sb("probTm", [META, 2, SEQ])
        negmax = ph.sb("negmax", [P, 4 * H])
        rsum = ph.sb("rsum", [P, 4 * H])
        rinv = ph.sb("rinv", [P, 4 * H])
        S = ph.ps("S", [P, 2, 2 * BANK])
        T = ph.ps("T", [P, 2, BANK])
        M = ph.ps("M", [P, BANK])
        O = ph.ps("O", [P, BANK])
        early_landed, scores, biased, exped, inverted, normed, turned, turned_m, copied, copied_m, pv, out = (
            ph.sem(n) for n in ("early_landed", "scores", "biased", "exped", "inverted", "normed", "turned",
                                "turned_m", "copied", "copied_m", "pv", "out"))
        units = [(h, n) for h in range(H) for n in range(NT)]
        block = ph.block()

        @block.sync
        def _(sp):
            load_early(sp, early_landed, early)

        @block.tensor
        def _(pe):
            def score(u):
                h, n = units[u]
                L = meta + (n + 1) * P
                if u >= 2:
                    pe.wait_ge(biased, u - 1)
                q = qT(h)[:, n * P:(n + 1) * P]
                first = min(L, BANK)
                ins = pe.matmul(S[:, u % 2, 0:first], q, kT(h)[:, 0:first], start=True, stop=True)
                if L > BANK:
                    ins = pe.matmul(S[:, u % 2, BANK:L], q, kT(h)[:, BANK:L], start=True, stop=True)
                ins.then_inc(scores, 1)

            def turn(u):
                h, n = units[u]
                pe.wait_ge(normed, u + 1)
                if u >= 2:
                    pe.wait_ge(copied, u - 1)
                for j in range(n + 1):
                    ins = pe.transpose(T[:, u % 2, j * P:(j + 1) * P], prob[:, u % 3, meta + j * P:meta + (j + 1) * P], ident[:])
                ins.then_inc(turned, 1)
                if meta:
                    if n == 0 and h >= 1:
                        pe.wait_ge(copied_m, h)
                    pe.transpose(M[0:meta, n * P:(n + 1) * P], prob[:, u % 3, 0:meta], ident[:]).then_inc(turned_m, 1)

            def values(h):
                pe.wait_ge(copied, NT * (h + 1))
                if meta:
                    pe.wait_ge(copied_m, h + 1)
                if h >= 1:
                    pe.wait_ge(out, h)
                base = 64 * (h % 2)
                for j in range(NT):
                    ins = pe.matmul(O[base:base + 64, j * P:], v[:, j, h * 64:(h + 1) * 64], probT[:, h % 2, j, j * P:],
                                    start=(j == 0), stop=(j == NT - 1 and not meta))
                if meta:
                    ins = pe.matmul(O[base:base + 64, :], vmeta[0:meta, h * 64:(h + 1) * 64], probTm[0:meta, h % 2, :],
                                    start=False, stop=True)
                ins.then_inc(pv, 1)

            n_u = len(units)
            for u in range(n_u + 4):
                if u < n_u:
                    score(u)
                if 2 <= u <= n_u + 1:
                    turn(u - 2)
                if u >= NT + 3 and (u - 3) % NT == 0 and (u - 3) // NT <= H:
                    values((u - 3) // NT - 1)

        @block.vector
        def _(dve):
            def bias(u):
                h, n = units[u]
                L = meta + (n + 1) * P
                off = (NT - 1 - n) * P
                dve.wait_ge(scores, u + 1)
                if u >= 3:
                    dve.wait_ge(exped, u - 2)
                dve.tensor_tensor_reduce(s[:, u % 3, 0:L], S[:, u % 2, 0:L], table[:, h % nh, off:off + L], -scale, 3e38,
                                         ALU.add, ALU.min, negmax[:, u:u + 1]).then_inc(biased, 1)

            def norm(u):
                h, n = units[u]
                L = meta + (n + 1) * P
                dve.wait_ge(exped, u + 1)
                dve.reciprocal(rinv[:, u:u + 1], rsum[:, u:u + 1]).then_inc(inverted, 1)
                dve.wait_ge(inverted, u + 1)
                dve.tensor_scalar(prob[:, u % 3, 0:L], prob[:, u % 3, 0:L], rinv[:, u:u + 1], None, ALU.mult).then_inc(normed, 1)

            def collect(h):
                base = 64 * (h % 2)
                dve.wait_ge(pv, h + 1)
                dve.tensor_copy(oT[base:base + 64, h // 2, :], O[base:base + 64, :]).then_inc(out, 1)

            n_u = len(units)
            for u in range(n_u + 6):
                if u < n_u:
                    bias(u)
                if 1 <= u <= n_u:
                    norm(u - 1)
                if u >= NT + 5 and (u - 5) % NT == 0 and (u - 5) // NT <= H:
                    collect((u - 5) // NT - 1)

        @block.scalar
        def _(act):
            def expo(u):
                h, n = units[u]
                L = meta + (n + 1) * P
                act.wait_ge(biased, u + 1)
                if u >= 3:
                    act.wait_ge(turned, u - 2)
                    if meta:
                        act.wait_ge(turned_m, u - 2)
                act.activation(prob[:, u % 3, 0:L], s[:, u % 3, 0:L], ACT.Exp, bias=negmax[:, u:u + 1], scale=-1.0,
                               accum_out=rsum[:, u:u + 1]).then_inc(exped, 1)

            def copy(u):
                h, n = units[u]
                act.wait_ge(turned, u + 1)
                if n == 0 and h >= 2:
                    act.wait_ge(pv, h - 1)
                act.activation(probT[:, h % 2, 0:n + 1, n * P:(n + 1) * P],
                               T[:, u % 2, 0:(n + 1) * P].rearrange("p (j q) -> p j q", q=P), ACT.Copy).then_inc(copied, 1)
                if meta and n == NT - 1:
                    act.wait_ge(turned_m, u + 1)
                    act.activation(probTm[0:meta, h % 2, :], M[0:meta, :], ACT.Copy).then_inc(copied_m, 1)

            n_u = len(units)
            for u in range(n_u + 2):
                if u < n_u:
                    expo(u)
                if u >= 2:
                    copy(u - 2)


def retention(nc, consts, rq, rk, rv, rgT, gain, rope, decay_dram, decay_meta_dram, early):
    ident = consts["ident"]
    H = RET_H
    with Phase(nc, "ret") as ph:
        decay = ph.sb("decay", [P, H, SEQ])
        decay_m = ph.sb("decay_m", [META, H, SEQ])
        a = ph.sb("a", [P, 2, BANK])
        b = ph.sb("b", [P, 2, BANK])
        qT = ph.sb("qT", [P, 4, SEQ])
        kT = ph.sb("kT", [P, 4, KEYS])
        wide = [SEQ - j * P for j in range(NT)]
        at = [sum(wide[:j]) for j in range(NT)]
        m = ph.sb("m", [P, 2, sum(wide)])
        mm = ph.sb("mm", [META, 2, SEQ])
        stats = ph.sb("stats", [P, NT, 6])
        mv = ph.sb("mv", [P, H, NT, 2])
        var = ph.sb("var", [P, H, NT])
        rstd = ph.sb("rstd", [P, H, NT])
        half = ph.sb("half", [P, NT])
        yn = a[:].rearrange("p s (n e) -> p s n e", n=NT)
        S = ph.ps("S", [P, 4, BANK])
        Y = ph.ps("Y", [P, 2, BANK])
        T = ph.ps("T", [P, 2, BANK])
        names = ("early_landed", "tables", "cosed", "swapped", "roped", "turned", "copied", "scored", "decayed", "pv",
                 "meaned", "rooted", "normed", "yturned", "gated", "dve_link", "pool_link")
        (early_landed, tables, cosed, swapped, roped, turned, copied, scored, decayed, pv, meaned, rooted, normed,
         yturned, gated, dve_link, pool_link) = (ph.sem(n) for n in names)
        jobs = [(rq, t, P, qT, t * P) for t in range(NT)] + [(rk, t, P, kT, t * P) for t in range(NT)] + [(rk, NT, META, kT, SEQ)]
        heads = lambda x: x.rearrange("p (h e) -> p h e", e=RET_DK)
        block = ph.block()

        @block.sync
        def _(sp):
            sp.dma_start(decay[:], decay_dram).then_inc(tables, 16)
            sp.dma_start(decay_m[:], decay_meta_dram).then_inc(tables, 16)
            load_early(sp, early_landed, early)

        @block.gpsimd
        def _(pool):
            link = Link(pool, pool_link)
            link(pool.memset(half[:], -0.5))
            for i, (src, t, rows, dst, col) in enumerate(jobs):
                x, o = heads(src[0:rows, t, :]), heads(b[0:rows, i % 2, :])
                if i >= 2:
                    pool.wait_ge(roped, i - 1)
                e = RET_DK // 2
                for lo, hi in ((0, e), (e, 0)):
                    ins = pool.tensor_tensor(o[:, :, lo:lo + e], x[:, :, hi:hi + e], bc(rope[0:rows, t, 1, lo:lo + e], 1, H), ALU.mult)
                ins.then_inc(swapped, 1)
            for h in range(H):
                pool.wait_ge(meaned, h + 1)
                pool.tensor_tensor(rstd[:, h, :], var[:, h, :], half[:], ALU.pow).then_inc(rooted, 1)

        @block.vector
        def _(dve):
            link = Link(dve, dve_link)
            for i, (src, t, rows, dst, col) in enumerate(jobs):
                if i >= 2:
                    dve.wait_ge(turned, i - 1)
                x, o = heads(src[0:rows, t, :]), heads(a[0:rows, i % 2, :])
                dve.tensor_tensor(o, x, bc(rope[0:rows, t, 0, :], 1, H), ALU.mult).then_inc(cosed, 1)
                dve.wait_ge(cosed, i + 1)
                dve.wait_ge(swapped, i + 1)
                dve.tensor_tensor(a[0:rows, i % 2, :], a[0:rows, i % 2, :], b[0:rows, i % 2, :], ALU.add).then_inc(roped, 1)

            def mask(h):
                for j in range(NT + 1):
                    i = h * (NT + 1) + j
                    dve.wait_ge(scored, i + 1)
                    if h >= 2 and j == 0:
                        dve.wait_ge(pv, h - 1)
                    if j < NT:
                        dve.tensor_tensor(m[:, h % 2, at[j]:at[j] + wide[j]], S[:, i % 4, 0:wide[j]], decay[:, h, 0:wide[j]], ALU.mult).then_inc(decayed, 1)
                    else:
                        dve.tensor_tensor(mm[0:META, h % 2, :], S[0:META, i % 4, :], decay_m[0:META, h, :], ALU.mult).then_inc(decayed, 1)

            def norm(h):
                dve.wait_ge(pv, h + 1)
                for n in range(NT):
                    ins = dve.bn_stats(stats[:, n, :], Y[:, h % 2, n * P:(n + 1) * P])
                link(ins)
                for n in range(NT):
                    ins = dve.bn_aggr(mv[:, h, n, :], stats[:, n, :])
                link(ins)
                dve.tensor_scalar(var[:, h, :], mv[:, h, :, 1], EPS, None, ALU.add).then_inc(meaned, 1)
                dve.wait_ge(rooted, h + 1)
                if h >= 2:
                    dve.wait_ge(yturned, h - 1)
                for n in range(NT):
                    ins = dve.tensor_scalar(yn[:, h % 2, n, :], Y[:, h % 2, n * P:(n + 1) * P], mv[:, h, n, 0:1], rstd[:, h, n:n + 1], ALU.subtract, ALU.mult)
                ins.then_inc(normed, 1)

            def gate(h):
                dve.wait_ge(yturned, h + 1)
                dve.scalar_tensor_tensor(rgT[:, h, :], T[:, h % 2, :], gain[:, h:h + 1], rgT[:, h, :], ALU.mult, ALU.mult).then_inc(gated, 1)

            dve.wait_ge(tables, 32)
            for h in range(H + 3):
                if h < H:
                    mask(h)
                if 2 <= h <= H + 1:
                    norm(h - 2)
                if h >= 3:
                    gate(h - 3)

        @block.scalar
        def _(act):
            for i, (src, t, rows, dst, col) in enumerate(jobs):
                act.wait_ge(turned, i + 1)
                act.activation(dst[:, :, col:col + rows], T[:, i % 2, :].rearrange("p (c q) -> p c q", q=P)[:, :, 0:rows], ACT.Copy).then_inc(copied, 1)

        @block.tensor
        def _(pe):
            for i, (src, t, rows, dst, col) in enumerate(jobs):
                pe.wait_ge(roped, i + 1)
                if i >= 2:
                    pe.wait_ge(copied, i - 1)
                for c in range(4):
                    ins = pe.transpose(T[:, i % 2, c * P:c * P + rows], a[0:rows, i % 2, c * P:(c + 1) * P], ident[0:rows, 0:rows])
                ins.then_inc(turned, 1)
            pe.wait_ge(copied, len(jobs))

            def score(h):
                base = 64 * (h % 2)
                for j in range(NT + 1):
                    i = h * (NT + 1) + j
                    if i >= 4:
                        pe.wait_ge(decayed, i - 3)
                    k = kT[base:base + 64, h // 2, j * P:(j + 1) * P] if j < NT else kT[base:base + 64, h // 2, SEQ:KEYS]
                    if j < NT:
                        pe.matmul(S[:, i % 4, 0:wide[j]], k, qT[base:base + 64, h // 2, j * P:], start=True, stop=True).then_inc(scored, 1)
                    else:
                        pe.matmul(S[0:META, i % 4, :], k, qT[base:base + 64, h // 2, :], start=True, stop=True).then_inc(scored, 1)

            def values(h):
                pe.wait_ge(decayed, (NT + 1) * (h + 1))
                if h >= 2:
                    pe.wait_ge(normed, h - 1)
                e = slice(h * RET_DV, (h + 1) * RET_DV)
                for n in range(NT):
                    o = Y[:, h % 2, n * P:(n + 1) * P]
                    pe.matmul(o, mm[0:META, h % 2, n * P:(n + 1) * P], rv[0:META, NT, e], start=True, stop=False)
                    for j in range(n + 1):
                        c = at[j] + (n - j) * P
                        ins = pe.matmul(o, m[:, h % 2, c:c + P], rv[:, j, e], start=False, stop=(j == n))
                ins.then_inc(pv, 1)

            def turn(h):
                pe.wait_ge(normed, h + 1)
                if h >= 2:
                    pe.wait_ge(gated, h - 1)
                for n in range(NT):
                    ins = pe.transpose(T[:, h % 2, n * P:(n + 1) * P], yn[:, h % 2, n, :], ident[:])
                ins.then_inc(yturned, 1)

            for h in range(H + 3):
                if h < H:
                    score(h)
                if h >= 3:
                    turn(h - 3)
                if 1 <= h <= H:
                    values(h - 1)


def mla_prepare(nc, consts, cq, ckv, tables, qT, kT, v, early):
    ident = consts["ident"]
    H = MLA_H
    with Phase(nc, "mla") as ph:
        wq, wkv, rope = (tables[n] for n in ("wq", "wkv", "rope_mla"))
        gl = [tables["g_ql"][:, k:k + 1] for k in range(3)] + [tables["g_kvl"][:, k:k + 1] for k in range(2)]
        gqk = (tables["g_q"], tables["g_k"])
        ssq = ph.sb("ssq", [P, 9])
        ms = ph.sb("ms", [P, 9])
        rstd = ph.sb("rstd", [P, 9])
        ss8 = ph.sb("ss8", [P, 9, H])
        ms8 = ph.sb("ms8", [P, 9, H])
        rstd8 = ph.sb("rstd8", [P, 9, H])
        half = ph.sb("half", [P, 9])
        cn = ph.sb("cn", [P, 2, MLA_QL])
        cqT = ph.sb("cqT", [P, 3, SEQ])
        ckvT = ph.sb("ckvT", [P, 2, KEYS])
        x = ph.sb("x", [P, 4, H, QK])
        sq = ph.sb("sq", [P, 2, H * QK])
        ra = ph.sb("ra", [P, H, ROPE])
        rb = ph.sb("rb", [P, H, ROPE])
        A = ph.ps("A", [P, 2, 2, BANK])
        T = ph.ps("T", [P, 2, 2, BANK])
        names = ("early_landed", "squares", "means", "roots", "scaled", "turned1", "copied1", "made", "filled",
                 "squared", "means8", "roots8", "normed", "swapped", "roped", "turned2", "copied2", "pool_link", "dve_link")
        (early_landed, squares, means, roots, scaled, turned1, copied1, made, filled, squared, means8, roots8,
         normed, swapped, roped, turned2, copied2, pool_link, dve_link) = (ph.sem(n) for n in names)
        lat = [(cq[:, t, :], P, 3, cqT, t * P, 0) for t in range(NT)]
        lat += [(ckv[:, t, 0:MLA_KVL], P, 2, ckvT, t * P, 3) for t in range(NT)]
        lat += [(ckv[0:META, NT, 0:MLA_KVL], META, 2, ckvT, SEQ, 3)]
        jobs = [(0, t, P) for t in range(NT)] + [(1, t, P) for t in range(NT)] + [(1, NT, META)]
        block = ph.block()

        @block.sync
        def _(sp):
            load_early(sp, early_landed, early)

        @block.scalar
        def _(act):
            for i, (src, rows, nch, dst, col, g) in enumerate(lat):
                act.activation(sq[0:rows, 0, 0:nch * P], src, ACT.Square, accum_out=ssq[0:rows, i:i + 1]).then_inc(squares, 1)
                act.wait_ge(squares, i + 1)
            for i, (src, rows, nch, dst, col, g) in enumerate(lat):
                act.wait_ge(turned1, i + 1)
                for k in range(nch):
                    ins = act.activation(dst[:, k, col:col + rows], T[:, i % 2, 0, k * P:k * P + rows], ACT.Copy, scale=gl[g + k])
                ins.then_inc(copied1, 1)

            def front(j):
                which, t, rows = jobs[j]
                act.wait_ge(made, j + 1)
                if j >= 4:
                    act.wait_ge(turned2, j - 3)
                if which == 0:
                    for b in range(2):
                        ins = act.activation(x[0:rows, j % 4, 4 * b:4 * b + 4, :], A[0:rows, j % 2, b, 0:4 * QK].rearrange("p (h e) -> p h e", e=QK), ACT.Copy)
                else:
                    for b in range(2):
                        kv = A[0:rows, j % 2, b, :].rearrange("p (h e) -> p h e", e=NOPE + MLA_V)
                        act.activation(x[0:rows, j % 4, 4 * b:4 * b + 4, 0:NOPE], kv[:, :, 0:NOPE], ACT.Copy)
                        act.activation(v[0:rows, t, 4 * b * 64:(4 * b + 4) * 64].rearrange("p (h e) -> p h e", e=MLA_V), kv[:, :, NOPE:], ACT.Copy)
                    ins = act.activation(x[0:rows, j % 4, :, NOPE:], bc(ckv[0:rows, t, MLA_KVL:], 1, H), ACT.Copy)
                ins.then_inc(filled, 1)
                act.wait_ge(filled, j + 1)
                if j >= 2:
                    act.wait_ge(means8, j - 1)
                act.activation(sq[0:rows, j % 2, :], x[0:rows, j % 4].rearrange("p h e -> p (h e)"), ACT.Square).then_inc(squared, 1)

            def back(j):
                which, t, rows = jobs[j]
                act.wait_ge(turned2, j + 1)
                col = 0 if t == NT else t * P + META * which
                dst = (qT, kT)[which][:, :, col:col + rows]
                for b in range(2):
                    ins = act.activation(dst[:, 4 * b:4 * b + 4, :], T[0:QK, j % 2, b, :].rearrange("p (h q) -> p h q", q=P)[:, :, 0:rows], ACT.Copy)
                ins.then_inc(copied2, 1)

            for j in range(len(jobs) + 3):
                if j < len(jobs):
                    front(j)
                if j >= 3:
                    back(j - 3)

        @block.gpsimd
        def _(pool):
            link = Link(pool, pool_link)
            link(pool.memset(half[:], -0.5))
            for i, (src, rows, nch, dst, col, g) in enumerate(lat):
                pool.wait_ge(means, i + 1)
                pool.tensor_tensor(rstd[0:rows, i:i + 1], ms[0:rows, i:i + 1], half[0:rows, 0:1], ALU.pow).then_inc(roots, 1)
            e = ROPE // 2
            for j in range(len(jobs) + 1):
                if j < len(jobs):
                    which, t, rows = jobs[j]
                    pool.wait_ge(means8, j + 1)
                    pool.tensor_tensor(rstd8[0:rows, j, :], ms8[0:rows, j, :], half[0:rows, 0:H], ALU.pow).then_inc(roots8, 1)
                if j == 0:
                    continue
                which, t, rows = jobs[j - 1]
                pool.wait_ge(normed, j)
                for lo, hi in ((0, e), (e, 0)):
                    ins = pool.tensor_tensor(rb[0:rows, :, lo:lo + e], x[0:rows, (j - 1) % 4, :, NOPE + hi:NOPE + hi + e], bc(rope[0:rows, t, 1, lo:lo + e], 1, H), ALU.mult)
                ins.then_inc(swapped, 1)

        @block.vector
        def _(dve):
            link = Link(dve, dve_link)
            for i in range(len(lat) + 1):
                if i < len(lat):
                    src, rows, nch, dst, col, g = lat[i]
                    dve.wait_ge(squares, i + 1)
                    dve.tensor_scalar(ms[0:rows, i:i + 1], ssq[0:rows, i:i + 1], 1.0 / (nch * P), EPS, ALU.mult, ALU.add).then_inc(means, 1)
                if i == 0:
                    continue
                src, rows, nch, dst, col, g = lat[i - 1]
                dve.wait_ge(roots, i)
                if i >= 3:
                    dve.wait_ge(turned1, i - 2)
                dve.tensor_scalar(cn[0:rows, (i - 1) % 2, 0:nch * P], src, rstd[0:rows, i - 1:i], None, ALU.mult).then_inc(scaled, 1)

            def mean_square(j):
                which, t, rows = jobs[j]
                dve.wait_ge(squared, j + 1)
                link(dve.tensor_reduce(ss8[0:rows, j, :], sq[0:rows, j % 2, :].rearrange("p (h e) -> p h e", e=QK), AX.X, ALU.add))
                dve.tensor_scalar(ms8[0:rows, j, :], ss8[0:rows, j, :], 1.0 / QK, EPS, ALU.mult, ALU.add).then_inc(means8, 1)

            def normalise(j):
                which, t, rows = jobs[j]
                xj = x[0:rows, j % 4]
                dve.wait_ge(roots8, j + 1)
                link(dve.tensor_tensor(xj, xj, bc(rstd8[0:rows, j, :], 2, QK), ALU.mult))
                dve.tensor_tensor(xj, xj, bc(gqk[which][0:rows, :], 1, H), ALU.mult).then_inc(normed, 1)
                dve.wait_ge(normed, j + 1)
                link(dve.tensor_tensor(ra[0:rows], xj[:, :, NOPE:], bc(rope[0:rows, t, 0, :], 1, H), ALU.mult))
                dve.wait_ge(swapped, j + 1)
                dve.tensor_tensor(xj[:, :, NOPE:], ra[0:rows], rb[0:rows], ALU.add).then_inc(roped, 1)

            for j in range(len(jobs) + 1):
                if j < len(jobs):
                    mean_square(j)
                if j >= 1:
                    normalise(j - 1)

        @block.tensor
        def _(pe):
            for i, (src, rows, nch, dst, col, g) in enumerate(lat):
                pe.wait_ge(scaled, i + 1)
                if i >= 2:
                    pe.wait_ge(copied1, i - 1)
                for k in range(nch):
                    ins = pe.transpose(T[:, i % 2, 0, k * P:k * P + rows], cn[0:rows, i % 2, k * P:(k + 1) * P], ident[0:rows, 0:rows])
                ins.then_inc(turned1, 1)
            pe.wait_ge(copied1, len(lat))

            def make(j):
                which, t, rows = jobs[j]
                if j >= 2:
                    pe.wait_ge(filled, j - 1)
                srcT, w, nch, n = ((cqT, wq, 3, 4 * QK), (ckvT, wkv, 2, BANK))[which]
                for b in range(2):
                    for k in range(nch):
                        ins = pe.matmul(A[0:rows, j % 2, b, 0:n], srcT[:, k, t * P:t * P + rows], w[:, k, b * n:(b + 1) * n],
                                        start=(k == 0), stop=(k == nch - 1))
                ins.then_inc(made, 1)

            def turn(j):
                which, t, rows = jobs[j]
                pe.wait_ge(roped, j + 1)
                if j >= 2:
                    pe.wait_ge(copied2, j - 1)
                for h in range(H):
                    ins = pe.transpose(T[0:QK, j % 2, h // 4, (h % 4) * P:(h % 4) * P + rows], x[0:rows, j % 4, h, :], ident[0:rows, 0:rows])
                ins.then_inc(turned2, 1)

            for j in range(len(jobs) + 3):
                if j < len(jobs):
                    make(j)
                if j >= 3:
                    turn(j - 3)


def merge_loads(w_mla_dram, w_ret_dram):
    cols = lambda w, c: w[:, c * P:(c + 1) * P].rearrange("(k p) n -> p k n", p=P)
    return lambda raw, c: [(raw[:, c % 2, 0:4, :], cols(w_mla_dram, c)), (raw[:, c % 2, 4:, :], cols(w_ret_dram, c))]


def merge(nc, oT, ygT, zaT, zrT, w_mla_dram, w_ret_dram, ring, early):
    KO, KY = 4, KD
    chunk_loads = merge_loads(w_mla_dram, w_ret_dram)
    with Phase(nc, "merge") as ph:
        N = 2
        raw = ring.raw
        wcut = ph.sb("wcut", [P, N, 2, KO + KY, P], F32R)
        acut = ph.sb("acut", [P, 2, KO + KY, SEQ], F32R)
        t1 = ph.sb("t1", [P, 2, BANK])
        t2 = ph.sb("t2", [P, 2, BANK])
        A = ph.ps("A", [P, 2, BANK])
        R = ph.ps("R", [P, 2, BANK])
        landed = [ph.sem(f"landed{i}") for i in range(N)]
        names = ("early_landed", "a_hi", "a_lo", "w_hi", "w_lo", "a_done", "r_done", "gated", "added")
        early_landed, a_hi, a_lo, w_hi, w_lo, a_done, r_done, gated, added = (ph.sem(n) for n in names)
        block = ph.block()

        @block.sync
        def _(sp):
            for c in range(KD):
                if c < N:
                    continue
                sp.wait_ge(w_lo, c - N + 1)
                for dst, src in chunk_loads(raw, c):
                    sp.dma_start(dst, src).then_inc(landed[c % N], 16)
            load_early(sp, early_landed, early)

        @block.scalar
        def _(act):
            def split(c):
                if c >= N:
                    act.wait_ge(landed[c % N], 32 * (c // N))
                    act.wait_ge(r_done, c - N + 1)
                act.activation(wcut[:, c % N, 0], raw[:, c % N], ACT.Copy).then_inc(w_hi, 1)

            split(0)
            for k in range(KO + KY):
                act.activation(acut[:, 0, k, :], oT[:, k, :] if k < KO else ygT[:, k - KO, :], ACT.Copy).then_inc(a_hi, 1)
            for c in range(1, KD):
                split(c)

        @block.tensor
        def _(pe):
            def product(bank, c, ks):
                for k in ks:
                    if c == 0:
                        pe.wait_ge(a_lo, k + 1)
                    pe.matmul(bank, wcut[:, c % N, 0, k, :], acut[:, 0, k, :], start=(k == ks[0]), stop=False)
                    pe.matmul(bank, wcut[:, c % N, 0, k, :], acut[:, 1, k, :], start=False, stop=False)
                    ins = pe.matmul(bank, wcut[:, c % N, 1, k, :], acut[:, 0, k, :], start=False, stop=(k == ks[-1]))
                return ins

            for c in range(KD):
                pe.wait_ge(w_lo, c + 1)
                if c >= 2:
                    pe.wait_ge(gated, 2 * (c - 1))
                product(A[:, c % 2, :], c, range(KO)).then_inc(a_done, 1)
                product(R[:, c % 2, :], c, range(KO, KO + KY)).then_inc(r_done, 1)

        @block.vector
        def _(dve):
            def split(c):
                dve.wait_ge(w_hi, c + 1)
                dve.tensor_tensor(wcut[:, c % N, 1], raw[:, c % N], wcut[:, c % N, 0].bitcast(F32), ALU.subtract).then_inc(w_lo, 1)

            split(0)
            for k in range(KO + KY):
                dve.wait_ge(a_hi, k + 1)
                dve.tensor_tensor(acut[:, 1, k, :], oT[:, k, :] if k < KO else ygT[:, k - KO, :], acut[:, 0, k, :].bitcast(F32), ALU.subtract).then_inc(a_lo, 1)
            split(1)
            for c in range(KD):
                if c >= 2:
                    dve.wait_ge(added, c - 1)
                dve.wait_ge(a_done, c + 1)
                dve.tensor_tensor(t1[:, c % 2, :], A[:, c % 2, :], zaT[:, c, :], ALU.mult).then_inc(gated, 1)
                dve.wait_ge(r_done, c + 1)
                dve.tensor_tensor(t2[:, c % 2, :], R[:, c % 2, :], zrT[:, c, :], ALU.mult).then_inc(gated, 1)
                if c + 2 < KD:
                    split(c + 2)
                dve.wait_ge(gated, 2 * (c + 1))
                dve.tensor_tensor(zaT[:, c, :], t1[:, c % 2, :], t2[:, c % 2, :], ALU.add).then_inc(added, 1)


def up_loads(wq_dram):
    KU = KD // 2
    return lambda raw: [(raw[:, r, :, :], wq_dram[r // 2, :, KU * (r % 2):KU * (r % 2) + KU]) for r in range(8)]


def peer_up(nc, consts, half, xs, wq_dram, u_dram, keys_dram, iota_dram, act_buf, picksT, ring, early):
    ident = consts["ident"]
    C, KU = 4, KD // 2
    R = 2 * C
    CUT = 4
    Q = PEER_H // C
    steps = Q + NKEYS // C
    H, K, TILES = PEER_H, TOPK, HALF // P
    SCORE, EXP, TURN, STORE = (Q, Q + 1), (Q + 5, Q + 9), (Q + 6, Q + 11), (Q + 7, Q + 12)
    POOL = STORE[1] + 1

    free = NKEYS * HALF

    def take(*shape):
        nonlocal free
        free -= int(np.prod(shape))
        piece = act_buf[:].rearrange("p e t -> p (e t)")[:, free:free + int(np.prod(shape))]
        names = "abcd"[:len(shape)]
        return piece.rearrange(f"p ({' '.join(names)}) -> p {' '.join(names)}", **dict(zip(names, shape)))

    with Phase(nc, f"up{half}") as ph:
        raw = ring.raw
        cut = ph.sb("cut", [P, CUT, 2, KU, P], F32R)
        acc = ph.ps("acc", [P, 2, BANK])
        qT = take(H, HALF)
        first_query = NKEYS - H
        keys = take(NKEYS)
        iota = take(P)
        s = take(H * 2, NKEYS)
        s2 = take(H, 2, NKEYS)
        best = take(H, 2, K)
        idx = take(H, 2, K).bitcast(U32)
        idxf = take(H, 2, K)
        cand = take(H, K, K)
        cand2 = take(H, K * K)
        top = take(H, K)
        ci = take(H * K).bitcast(U32)
        parts = take(2, H * K).bitcast(U32)
        partsf = take(2, H * K)
        hot = take(2, H * K, K)
        shifted = take(H, K)
        ex = take(H, K)
        den = take(H)
        rden = take(H)
        picks = take(3, H * K)
        assert (STORE[1] + 1 - Q) * C < free // HALF
        S = ph.ps("S", [P, 4, BANK])
        T = ph.ps("T", [P, BANK])
        landed = [ph.sem(f"landed{r}") for r in range(R)]
        names = ("early_landed", "loaded", "hi_made", "lo_pool", "lo_dve", "used", "out", "scored", "copied", "shiftd", "exped", "picked", "turned", "stored", "dve_link")
        early_landed, loaded, hi_made, lo_pool, lo_dve, used, out, scored, copied, shiftd, exped, picked, turned, stored, dve_link = (ph.sem(n) for n in names)
        block = ph.block()

        def wait_lo(engine, i, r, pool):
            if pool:
                engine.wait_ge(lo_pool, i * R + r + 1)
            else:
                engine.wait_ge(lo_dve, (i - POOL) * R + r + 1)

        @block.sync
        def _(sp):
            def load(r, i, src):
                ks = slice(KU * (r % 2), KU * (r % 2) + KU)
                sp.dma_start(raw[:, r], src[bass.ds(i * C + r // 2, 1), :, ks].rearrange("o p k e -> (o p) k e")).then_inc(landed[r], 16)

            sp.dma_start(keys, keys_dram).then_inc(loaded, 16)
            sp.dma_start(iota, iota_dram).then_inc(loaded, 16)
            for i in range(1, Q):
                for r in range(R):
                    wait_lo(sp, i - 1, r, True)
                    load(r, i, wq_dram)
            for lo, hi, pool in ((Q, POOL + 1, True), (POOL + 1, steps, False)):
                with sp.Fori(lo, hi) as i:
                    for r in range(R):
                        wait_lo(sp, i - 1, r, pool)
                        load(r, i - Q, u_dram)
            load_early(sp, early_landed, early)

        @block.scalar
        def _(act):
            def split(r, i, first=False):
                if not first:
                    act.wait_ge(landed[r], i * 16)
                if not first or r >= CUT:
                    act.wait_ge(used, i * R + r - CUT + 1)
                act.activation(cut[:, r % CUT, 0], raw[:, r], ACT.Copy).then_inc(hi_made, 1)

            def query(c):
                act.wait_ge(used, 2 * c + 2)
                act.activation(act_buf[:, first_query + c:first_query + c + 1, :], acc[:, c % 2:c % 2 + 1, 0:HALF], ACT.Copy).then_inc(out, 1)

            def gelu(b, c):
                act.wait_ge(used, 2 * (c + H) + 2)
                act.activation(act_buf[:, bass.ds(c, 1), :], acc[:, b:b + 1, 0:HALF], ACT.Gelu).then_inc(out, 1)

            def step(i):
                for r in range(R):
                    split(r, i)
                    if r % 2:
                        gelu((r // 2 - 1) % 2, (i - Q) * C + r // 2 - 1)

            def exponent(t):
                act.wait_ge(shiftd, t + 1)
                act.activation(ex, shifted, ACT.Exp).then_inc(exped, 1)

            def store(t):
                act.wait_ge(turned, t + 1)
                ins = act.activation(picksT[:, :, t * P:(t + 1) * P], T[:, 0:3 * P].rearrange("p (j t) -> p j t", j=3), ACT.Copy)
                ins.then_inc(stored, 1)

            for i in range(Q + 1):
                for r in range(R):
                    split(r, i, first=(i == 0))
                    c = i * C + r // 2 - 1
                    if r % 2 and 0 <= c < H:
                        query(c)
                    elif r % 2 and c >= H:
                        gelu(c % 2, c - H)
            last = Q + 1
            for at, serve, t in sorted([(EXP[t], exponent, t) for t in range(TILES)] +
                                       [(STORE[t], store, t) for t in range(TILES)], key=lambda x: x[0]):
                with act.Fori(last, at + 1) as i:
                    step(i)
                serve(t)
                last = at + 1
                if serve is exponent:
                    step(last)
                    last += 1
            with act.Fori(last, steps) as i:
                step(i)
            gelu(1, NKEYS - 1)

        @block.gpsimd
        def _(pool):
            with pool.Fori(0, POOL) as i:
                for r in range(R):
                    pool.wait_ge(hi_made, i * R + r + 1)
                    pool.tensor_tensor(cut[:, r % CUT, 1], raw[:, r], cut[:, r % CUT, 0].bitcast(F32), ALU.subtract).then_inc(lo_pool, 1)

        @block.vector
        def _(dve):
            link = Link(dve, dve_link)
            dve.wait_ge(loaded, 32)
            for t in range(TILES):
                st = s.rearrange("p (h c) k -> p h c k", h=H)
                lists = [(h, c) for h in range(H) for c in range(2)]
                dve.wait_ge(scored, t + 1)
                for b in range(4):
                    hs = slice(4 * (b % 2), 4 * (b % 2) + 4)
                    ins = dve.tensor_copy(st[:, hs, b // 2, :], S[:, b, :].rearrange("p (h k) -> p h k", h=4))
                ins.then_inc(copied, 1)
                dve.wait_ge(copied, t + 1)
                for h, c in lists:
                    ins = dve.max(best[:, h, c, 0:8], st[:, h, c, :])
                link(ins)
                for h, c in lists:
                    ins = dve.max_index(idx[:, h, c, 0:8], best[:, h, c, 0:8], st[:, h, c, :])
                for h, c in lists:
                    ins = dve.match_replace(s2[:, h, c, :], best[:, h, c, 0:8], st[:, h, c, :], NEG)
                link(ins)
                for h, c in lists:
                    ins = dve.max(best[:, h, c, 8:16], s2[:, h, c, :])
                link(ins)
                for h, c in lists:
                    ins = dve.max_index(idx[:, h, c, 8:16], best[:, h, c, 8:16], s2[:, h, c, :])
                link(dve.tensor_tensor(cand, bc(best[:, :, 0, :], 3, K), bc(best[:, :, 1, :], 2, K), ALU.add))
                link(dve.tensor_copy(idxf, idx))
                flat = cand.rearrange("p h a b -> p h (a b)")
                for h in range(H):
                    ins = dve.max(top[:, h, 0:8], flat[:, h, :])
                link(ins)
                for h in range(H):
                    ins = dve.max_index(ci[:, h * K:h * K + 8], top[:, h, 0:8], flat[:, h, :])
                for h in range(H):
                    ins = dve.match_replace(cand2[:, h, :], top[:, h, 0:8], flat[:, h, :], NEG)
                link(ins)
                for h in range(H):
                    ins = dve.max(top[:, h, 8:16], cand2[:, h, :])
                link(ins)
                for h in range(H):
                    ins = dve.max_index(ci[:, h * K + 8:h * K + 16], top[:, h, 8:16], cand2[:, h, :])
                link(ins)
                dve.tensor_tensor(shifted, top, bc(top[:, :, 0], 2, K), ALU.subtract).then_inc(shiftd, 1)
                dve.tensor_scalar(parts[:, 0, :], ci, 4, None, ALU.logical_shift_right)
                link(dve.tensor_scalar(parts[:, 1, :], ci, K - 1, None, ALU.bitwise_and))
                link(dve.tensor_copy(partsf, parts))
                for c in range(2):
                    ins = dve.tensor_tensor(hot[:, c], bc(partsf[:, c, :], 2, K), bc(iota[:, 0:K], 1, H * K), ALU.is_equal)
                link(ins)
                for c in range(2):
                    o = hot[:, c].rearrange("p (h k) a -> p h k a", h=H)
                    ins = dve.tensor_tensor(o, o, bc(idxf[:, :, c, :], 2, K), ALU.mult)
                link(ins)
                if t >= 1:
                    dve.wait_ge(turned, t)
                for c in range(2):
                    dve.tensor_reduce(picks[:, 1 - c, :], hot[:, c], AX.X, ALU.add)
                dve.wait_ge(exped, t + 1)
                link(dve.tensor_reduce(den, ex, AX.X, ALU.add))
                link(dve.reciprocal(rden, den))
                dve.tensor_tensor(picks[:, 2, :].rearrange("p (h k) -> p h k", h=H), ex, bc(rden, 2, K), ALU.mult).then_inc(picked, 1)
            with dve.Fori(POOL, steps) as i:
                for r in range(R):
                    dve.wait_ge(hi_made, i * R + r + 1)
                    dve.tensor_tensor(cut[:, r % CUT, 1], raw[:, r], cut[:, r % CUT, 0].bitcast(F32), ALU.subtract).then_inc(lo_dve, 1)

        @block.tensor
        def _(pe):
            def unit(r, i, pool, first=False):
                wait_lo(pe, i, r, pool)
                if r % 2 == 0 and (not first or r >= 4):
                    pe.wait_ge(out, i * C + r // 2 - 1)
                bank = acc[:, (r // 2) % 2, 0:HALF]
                for k in range(KU):
                    kx = KU * (r % 2) + k
                    pe.matmul(bank, cut[:, r % CUT, 0, k, :], xs[:, 0, kx, :], start=(kx == 0), stop=False)
                    pe.matmul(bank, cut[:, r % CUT, 0, k, :], xs[:, 1, kx, :], start=False, stop=False)
                    ins = pe.matmul(bank, cut[:, r % CUT, 1, k, :], xs[:, 0, kx, :], start=False, stop=(kx == KD - 1))
                ins.then_inc(used, 1)

            def score(t):
                if t == 0:
                    pe.wait_ge(loaded, 32)
                    pe.wait_ge(out, H)
                else:
                    pe.wait_ge(copied, t)
                for h in range(H):
                    for side in range(2):
                        r = slice(64 * side, 64 * side + 64)
                        ins = pe.matmul(S[:, 2 * side + h // 4, (h % 4) * NKEYS:(h % 4 + 1) * NKEYS], qT[r, h, t * P:(t + 1) * P], keys[r, :], start=True, stop=True)
                ins.then_inc(scored, 1)

            def turn(t):
                pe.wait_ge(picked, t + 1)
                if t >= 1:
                    pe.wait_ge(stored, t)
                for i in range(3):
                    ins = pe.transpose(T[:, i * P:(i + 1) * P], picks[:, i, :], ident[:])
                ins.then_inc(turned, 1)

            for r in range(R):
                unit(r, 0, True, first=True)
            last = 1
            for at, serve, t in sorted([(SCORE[t], score, t) for t in range(TILES)] + [(TURN[t], turn, t) for t in range(TILES)], key=lambda x: x[0]):
                with pe.Fori(last, at + 1) as i:
                    for r in range(R):
                        unit(r, i, True)
                serve(t)
                last = at + 1
            with pe.Fori(last, POOL) as i:
                for r in range(R):
                    unit(r, i, True)
            with pe.Fori(POOL, steps) as i:
                for r in range(R):
                    unit(r, i, False)


def peer_gate(nc, half, iota, picksT, act_buf, early):
    G = 4
    R = 4
    N = HALF // G
    steps = N // R
    e2T, e1T, gateT = (picksT[:, j, :] for j in range(3))
    with Phase(nc, f"gate{half}") as ph:
        scalars = ph.sb("scalars", [P, R, 2, 2])
        minus = ph.sb("minus", [P, HALF])
        square = ph.sb("square", [P, R, G // 2, P])
        hot1 = ph.sb("hot1", [P, R, G, P])
        hot2 = ph.sb("hot2", [P, R, G, P])
        acc = ph.ps("acc", [P, R, BANK])
        names = ("early_landed", "negated", "squared", "built_dve", "built_act", "fetched", "built_pool", "done", "out")
        early_landed, negated, squared, built_dve, built_act, fetched, built_pool, done, out = (ph.sem(n) for n in names)
        block = ph.block()

        @block.sync
        def _(sp):
            load_early(sp, early_landed, early)

        @block.vector
        def _(dve):
            def hots(r, n):
                t = n * G
                if r != R - 1:
                    dve.tensor_scalar(hot1[:, r, 1, :], iota[:], e1T[:, bass.ds(t + 1, 1)], gateT[:, bass.ds(t + 1, 1)], ALU.is_equal, ALU.mult)
                dve.tensor_tensor(hot2[:, r], bc(iota[:], 1, G), bc(e2T[:, bass.ds(t, G)], 2, P), ALU.is_equal).then_inc(built_dve, 1)

            def weigh(r, n):
                a = act_buf[:, :, bass.ds(n * G, G)]
                dve.wait_ge(done, n + 1)
                dve.tensor_tensor(a, acc[:, r, :].rearrange("p (g e) -> p e g", g=G), a, ALU.mult).then_inc(out, 1)

            dve.tensor_scalar(minus[:], gateT[:], -1.0, None, ALU.mult).then_inc(negated, 1)
            hots(0, 0)
            hots(1, 1)
            with dve.Fori(0, steps - 1) as i:
                for r in range(R):
                    hots((r + 2) % R, i * R + r + 2)
                    weigh(r, i * R + r)
            for r in range(R):
                if r < 2:
                    hots(r + 2, N - R + r + 2)
                weigh(r, N - R + r)

        @block.scalar
        def _(act):
            def squares(r, n, first=False):
                if not first:
                    act.wait_ge(done, n - R + 1)
                for g in range(G // 2):
                    t = n * G + G // 2 + g
                    ins = act.activation(square[:, r, g, :], iota[:], ACT.Square, bias=e1T[:, bass.ds(t, 1)], scale=-1.0)
                ins.then_inc(squared, 1)

            def hots(r, n):
                act.wait_ge(squared, n + 1)
                for g in range(G // 2):
                    t = n * G + G // 2 + g
                    ins = act.activation(hot1[:, r, G // 2 + g, :], square[:, r, g, :], ACT.Relu, bias=gateT[:, bass.ds(t, 1)], scale=minus[:, bass.ds(t, 1)])
                ins.then_inc(built_act, 1)

            act.wait_ge(negated, 1)
            squares(0, 0, first=True)
            for n in range(1, R):
                squares(n, n, first=True)
                hots(n - 1, n - 1)
            with act.Fori(1, steps) as i:
                for r in range(R):
                    squares(r, i * R + r)
                    hots((r - 1) % R, i * R + r - 1)
            hots(R - 1, N - 1)

        @block.gpsimd
        def _(pool):
            def fetch(r, n, first=False):
                if not first:
                    pool.wait_ge(done, n - R + 1)
                pool.tensor_copy(scalars[:, r], picksT[:, 1:3, bass.ds(n * G, 2)]).then_inc(fetched, 1)

            def hot(r):
                for g in range(2 if r == R - 1 else 1):
                    ins = pool.tensor_scalar(hot1[:, r, g, :], iota[:], scalars[:, r, 0, g:g + 1], scalars[:, r, 1, g:g + 1], ALU.is_equal, ALU.mult)
                ins.then_inc(built_pool, 1)

            fetch(0, 0, first=True)
            for n in range(1, R):
                pool.wait_ge(fetched, n)
                fetch(n, n, first=True)
                hot(n - 1)
            with pool.Fori(1, steps) as i:
                for r in range(R):
                    pool.wait_ge(fetched, i * R + r)
                    fetch(r, i * R + r)
                    hot((r - 1) % R)
            pool.wait_ge(fetched, N)
            hot(R - 1)

        @block.tensor
        def _(pe):
            def products(r, n, first=False):
                if not first:
                    pe.wait_ge(out, n - R + 1)
                pe.wait_ge(built_dve, n + 1)
                pe.wait_ge(built_act, n + 1)
                pe.wait_ge(built_pool, n + 1)
                for g in range(G):
                    ins = pe.matmul(acc[:, r, g * P:(g + 1) * P], hot1[:, r, g, :], hot2[:, r, g, :], start=True, stop=True)
                ins.then_inc(done, 1)

            for r in range(R):
                products(r, r, first=True)
            with pe.Fori(1, steps) as i:
                for r in range(R):
                    products(r, i * R + r)


def down_loads(v_dram):
    return lambda raw: [(raw[:, r], v_dram[:, r // 2, BANK * (r % 2):BANK * (r % 2) + BANK].rearrange("p (k e) -> p k e", e=P)) for r in range(8)]


def peer_down(nc, half, v_dram, act_buf, resid, ring, c_dram, w_dram, b, mod):
    C = 4
    R = 2 * C
    CUT = 4
    steps = NKEYS // C
    SUMS = 3 * KD
    with Phase(nc, f"down{half}") as ph:
        raw = ring.raw[:].rearrange("p r k e -> p r (k e)")
        vcut = ph.sb("vcut", [P, CUT, 2, BANK], F32R)
        acut = ph.sb("acut", [P, 2, 2, HALF], F32R)
        cond = ph.sb("cond", [P, D])
        ada = ph.sb("ada", [P, D])
        junk = ph.sb("junk", [P, D])
        total = ph.sb("total", [P, 1])
        Y = ph.ps("Y", [P, 4, BANK])
        landed = [ph.sem(f"landed{r}") for r in range(R)]
        names = ("hi_made", "lo_made", "used", "added", "c_loaded", "c_active", "ada_loaded", "summed", "noted", "shifted")
        hi_made, lo_made, used, added, c_loaded, c_active, ada_loaded, summed, noted, shifted = (ph.sem(n) for n in names)
        block = ph.block()

        @block.sync
        def _(sp):
            def load(r, i):
                h = r % 2
                sp.dma_start(raw[:, r:r + 1, :], v_dram[:, bass.ds(i * C + r // 2, 1), h * BANK:(h + 1) * BANK]).then_inc(landed[r], 16)

            def step(i):
                for r in range(R):
                    sp.wait_ge(lo_made, (i - 1) * R + r + 1)
                    load(r, i)

            sp.dma_start(cond[:], c_dram.partition_broadcast(P)).then_inc(c_loaded, 16)
            sp.dma_start(ada[:], w_dram[half * SUMS * P:(half * SUMS + 1) * P, :]).then_inc(ada_loaded, 16)
            step(1)
            with sp.Fori(1, SUMS) as j:
                step(j + 1)
                sp.wait_ge(summed, j)
                sp.dma_start(ada[:], w_dram[bass.ds((half * SUMS + j) * P, P), :]).then_inc(ada_loaded, 16)
            with sp.Fori(SUMS + 1, steps) as i:
                step(i)

        @block.scalar
        def _(act):
            def split(r, i, first=False):
                c, b = r // 2, r // 2 % 2
                if r % 2 == 0:
                    if not first or r >= CUT:
                        act.wait_ge(used, i * R + r - CUT + 2)
                    act.activation(acut[:, b, 0:1, :], act_buf[:, bass.ds(i * C + c, 1), :], ACT.Copy)
                if not first:
                    act.wait_ge(landed[r], i * 16)
                act.activation(vcut[:, r % CUT, 0, :], raw[:, r, :], ACT.Copy).then_inc(hi_made, 1)

            for r in range(R):
                split(r, 0, first=True)
            act.wait_ge(c_loaded, 16)
            act.activation(cond[:], cond[:], ACT.Silu).then_inc(c_active, 1)
            with act.Fori(1, steps) as i:
                for r in range(R):
                    split(r, i)

        @block.vector
        def _(dve):
            def step(i, units=range(R)):
                for r in units:
                    c, b = r // 2, r // 2 % 2
                    dve.wait_ge(hi_made, i * R + r + 1)
                    if r % 2 == 0:
                        dve.tensor_tensor(acut[:, b, 1:2, :], act_buf[:, bass.ds(i * C + c, 1), :], acut[:, b, 0:1, :].bitcast(F32), ALU.subtract)
                    dve.tensor_tensor(vcut[:, r % CUT, 1, :], raw[:, r, :], vcut[:, r % CUT, 0, :].bitcast(F32), ALU.subtract).then_inc(lo_made, 1)
            step(0)
            dve.wait_ge(c_active, 1)
            with dve.Fori(0, SUMS) as j:
                step(j + 1, range(R - 2))
                dve.wait_ge(ada_loaded, 16 * (j + 1))
                dve.tensor_tensor_reduce(junk[:], ada[:], cond[:], 1.0, 0.0, ALU.mult, ALU.add, total[:]).then_inc(summed, 1)
                step(j + 1, range(R - 2, R))
                dve.wait_ge(summed, j + 1)
                dve.tensor_copy(mod[:, bass.ds(half * SUMS + j, 1)], total[:]).then_inc(noted, 1)
                dve.wait_ge(noted, j + 1)
            part = mod[:, half * SUMS:(half + 1) * SUMS]
            dve.tensor_tensor(part, part, b[:, half * SUMS:(half + 1) * SUMS], ALU.add).then_inc(shifted, 1)
            with dve.Fori(SUMS + 1, steps) as i:
                step(i)
            for h in range(2):
                dve.wait_ge(used, 2 * NKEYS - 1 + h)
                for t in range(2):
                    dst = resid[:, 2 * half + t, h * BANK:(h + 1) * BANK]
                    dve.tensor_tensor(dst, Y[:, 2 * t + h, :], dst, ALU.add).then_inc(added, 1)

        @block.tensor
        def _(pe):
            def unit(r, i, first=False, last=False):
                h, b = r % 2, r // 2 % 2
                pe.wait_ge(lo_made, i * R + r + 1)
                for t in range(2):
                    bank, rows = Y[:, 2 * t + h, :], slice(t * P, (t + 1) * P)
                    pe.matmul(bank, acut[:, b, 0, rows], vcut[:, r % CUT, 0, :], start=first, stop=False)
                    pe.matmul(bank, acut[:, b, 0, rows], vcut[:, r % CUT, 1, :], start=False, stop=False)
                    ins = pe.matmul(bank, acut[:, b, 1, rows], vcut[:, r % CUT, 0, :], start=False, stop=last)
                ins.then_inc(used, 1)

            for r in range(R):
                unit(r, 0, first=(r < 2))
            with pe.Fori(1, steps - 1) as i:
                for r in range(R):
                    unit(r, i)
            for r in range(R):
                unit(r, steps - 1, last=(r >= R - 2))


def peer(nc, consts, resid, mod, d):
    for half in range(2):
        with Phase(nc, f"peer{half}") as ph:
            picksT = ph.sb("picksT", [P, 3, HALF])
            with Phase(nc, f"experts{half}") as ph2:
                tables = Tables(ph2, iota=([P, P], d["c_iota"]), b_ada=([P, 6 * KD], d["b_ada"]))
                raw = ph2.sb("raw", [P, 8, KD // 2, P])
                up_ring = Early(raw, up_loads(d["w_peer_q"]))
                down_ring = Early(raw, down_loads(d["peer_v"]))
                act_buf = ph2.sb("act_buf", [P, NKEYS, HALF])
                with Phase(nc, f"x{half}") as ph3:
                    xs = ph3.sb("xs", [P, 2, KD, HALF], F32R)
                    norm_transpose(nc, f"n2{half}", consts, resid, xs, d["g_ffn"], tokens=range(2 * half, 2 * half + 2), early=[up_ring])
                    peer_up(nc, consts, half, xs, d["w_peer_q"], d["peer_u"], d["peer_keys"], d["c_iota"], act_buf, picksT, up_ring, [tables])
                peer_gate(nc, half, tables["iota"], picksT, act_buf, [down_ring])
                peer_down(nc, half, d["peer_v"], act_buf, resid, down_ring, d["c"], d["w_ada"], tables["b_ada"], mod)


def first_mixer(nc, consts, resid, d):
    with Phase(nc, "m1") as ph:
        gates = ph.sb("gates", [P, 3, KD, SEQ])
        rgT, zaT, zrT = gates[:, 0], gates[:, 1], gates[:, 2]
        cq = ph.sb("cq", [P, NT, MLA_QL])
        ckv = ph.sb("ckv", [P, 5, MLA_KVL + ROPE])
        mla_tables = Tables(
            ph, g_ql=([P, 3], d["g_q_lora"]), g_kvl=([P, 2], d["g_kv_lora"]), g_q=([P, QK], d["g_qk_q"].partition_broadcast(P)),
            g_k=([P, QK], d["g_qk_k"].partition_broadcast(P)), rope_mla=([P, 5, 2, ROPE], d["c_rope_mla"]),
            wq=([P, 3, MLA_H * QK], d["w_uq"].rearrange("(k p) n -> p k n", p=P)),
            wkv=([P, 2, MLA_H * (NOPE + MLA_V)], d["w_ukv"].rearrange("(k p) n -> p k n", p=P)))
        ret_tables = Tables(ph, rope_ret=([P, 5, 2, RET_DK], d["c_rope_ret"]), g_ret=([P, RET_H], d["g_ret_gn"]))
        with Phase(nc, "m1r") as ph2:
            rq = ph2.sb("rq", [P, NT, 512])
            rk = ph2.sb("rk", [P, 5, 512])
            rv = ph2.sb("rv", [P, 5, 1024])
            with Phase(nc, "m1h") as ph3:
                hs = ph3.sb("hs", [P, 2, KD, KEYS], F32R)
                ring = Early(ph3.sb("raw", [P, KD, BANK]), project_loads([(d["w_in"][:, 0:MLA_QL], None)]))
                with Phase(nc, "m1x") as ph4:
                    meta = ph4.sb("meta", [META, D])
                    norm_transpose(nc, "n1", consts, resid, hs, d["g_mix"], meta=meta, load=(d["x"], d["meta"]), early=[ring])
                w = d["w_in"]
                x_tiles = lambda dst, a, b: [(P, t * P, dst[:, t, a:b]) for t in range(NT)]
                all_tiles = lambda dst, a, b: x_tiles(dst, a, b) + [(META, SEQ, dst[0:META, NT, a:b])]
                jobs, c = [], 0
                for n, out in ((MLA_QL, ("tok", x_tiles(cq, 0, MLA_QL))), (288, ("tok", all_tiles(ckv, 0, 288))),
                               (512, ("tok", x_tiles(rq, 0, 512))), (512, ("tok", all_tiles(rk, 0, 512))),
                               (512, ("tok", all_tiles(rv, 0, 512))), (512, ("tok", all_tiles(rv, 512, 1024)))):
                    jobs.append((w[:, c:c + n], out))
                    c += n
                for g, fn in ((rgT, ACT.Silu), (zaT, ACT.Sigmoid), (zrT, ACT.Sigmoid)):
                    for half in range(2):
                        jobs.append((w[:, c:c + 512], ("feat", fn, [g[:, 4 * half + j, :] for j in range(4)])))
                        c += 512
                project(nc, "p1", hs, jobs, ring, [ret_tables])
            retention(nc, consts, rq, rk, rv, rgT, ret_tables["g_ret"], ret_tables["rope_ret"], d["c_decay"], d["c_decay_meta"], [mla_tables])
        oT = ph.sb("oT", [P, 4, SEQ])
        out_ring = Early(ph.sb("out_ring", [P, 2, D]), out_loads(d["w_mix_out"]))
        two_chunks = merge_loads(d["w_mla_out"], d["w_ret_out"])
        merge_ring = Early(ph.sb("merge_ring", [P, 2, 12, P]), lambda raw: two_chunks(raw, 0) + two_chunks(raw, 1))
        with Phase(nc, "m1a") as ph2:
            qT = ph2.sb("qT", [QK, MLA_H, SEQ])
            kT = ph2.sb("kT", [QK, MLA_H, KEYS])
            v = ph2.sb("v", [P, 5, MLA_H * MLA_V])
            causal = Tables(ph2, causal=([P, 1, KEYS], d["c_causal"]))
            mla_prepare(nc, consts, cq, ckv, mla_tables, qT, kT, v, [causal])
            attention(nc, "at1", consts, lambda h: qT[:, h, :], lambda h: kT[:, h, :], v, v[0:META, NT, :], causal["causal"],
                      META, QK ** -0.5, oT, [merge_ring])
        merge(nc, oT, rgT, zaT, zrT, d["w_mla_out"], d["w_ret_out"], merge_ring, [out_ring])
        out_project(nc, "o1", zaT, d["w_mix_out"], KD, resid, out_ring)


def gla(nc, consts, qkT, v, lowT, grT, tables, mixT, mod, rows, early):
    ident = consts["ident"]
    H, C = GLA_H, GLA_CHUNK
    NC = SEQ // C
    with Phase(nc, "gla") as ph:
        wg, bg, gn, mask, keep = (tables[n] for n in ("wg", "bg", "gn", "mask", "keep"))
        wide = ph.sb("wide", [P, 2 * KD, P])
        absz = ph.sb("absz", [P, 2, SEQ])
        minz = ph.sb("minz", [P, 2, SEQ])
        b = ph.sb("b", [P, 2, SEQ])
        dm = ph.sb("dm", [P, 2, SEQ])
        dl = ph.sb("dl", [P, 2, SEQ])
        e1 = ph.sb("e1", [P, 2, SEQ])
        e2 = ph.sb("e2", [P, 2, SEQ])
        e3 = ph.sb("e3", [P, 2, SEQ])
        e4 = ph.sb("e4", [P, 2, SEQ])
        qe = ph.sb("qe", [P, 2, SEQ])
        klT = ph.sb("klT", [P, NT, 2 * P])
        st = ph.sb("st", [P, NC, 2, GLA_DV])
        sm = ph.sb("sm", [P, 2, H, P])
        junk = ph.sb("junk", [P, H, P])
        ssq = ph.sb("ssq", [P, NT, H])
        ms = ph.sb("ms", [P, NT, H])
        rstd = ph.sb("rstd", [P, NT, H])
        half = ph.sb("half", [P, H])
        on = ph.sb("on", [P, 2, H, P])
        S = ph.ps("S", [P, 2, BANK])
        O = ph.ps("O", [P, 2, BANK])
        U = ph.ps("U", [P, 4, BANK])
        names = ("early_landed", "widened", "rows_turned", "rows_done", "logits", "absed", "mined", "exped", "logged", "decays", "relative", "e1_done", "e2_done", "e3_done",
                 "e4_done", "kl_done", "ready", "turned", "copied", "updates", "stated", "scored", "masked", "attended",
                 "squares", "means", "roots", "normed", "oturned", "gated", "dve_link", "pool_link")
        (early_landed, widened, rows_turned, rows_done, logits, absed, mined, exped, logged, decays, relative, e1_done, e2_done, e3_done, e4_done, kl_done, ready,
         turned, copied, updates, stated, scored, masked, attended, squares, means, roots, normed, oturned, gated,
         dve_link, pool_link) = (ph.sem(x) for x in names)
        q, k = qkT[:, 0:2, :], qkT[:, 2:4, :]
        qm, km, kl = e2, e3, e4
        chunks = lambda x: x[:].rearrange("p c (n i) -> p (c n) i", i=C)
        head = lambda h: slice(64 * (h % 2), 64 * (h % 2) + 64)
        out_of = lambda t, h: (O[:, h % 2] if t % 2 == 0 else U[:, 2 + h % 2])[:, (h // 2) * P:(h // 2 + 1) * P]
        block = ph.block()

        @block.sync
        def _(sp):
            load_early(sp, early_landed, early)

        @block.gpsimd
        def _(pool):
            link = Link(pool, pool_link)
            link(pool.memset(half[:], -0.5))
            for t in range(NT):
                pool.wait_ge(means, t + 1)
                pool.tensor_tensor(rstd[:, t, :], ms[:, t, :], half[:], ALU.pow).then_inc(roots, 1)

        @block.scalar
        def _(act):
            act.wait_ge(logits, 1)
            for c in range(2):
                ins = act.activation(absz[:, c, :], S[:, c, :], ACT.Abs, bias=bg[:, c:c + 1])
            ins.then_inc(absed, 1)
            act.wait_ge(absed, 1)
            act.activation(absz[:], absz[:], ACT.Exp, scale=-1.0).then_inc(exped, 1)
            act.wait_ge(exped, 1)
            act.activation(absz[:], absz[:], ACT.Ln, bias=1.0).then_inc(logged, 1)
            for i in range(4):
                act.wait_ge(rows_turned, i + 1)
                act.activation(rows[:, i // 2, (i % 2) * BANK:(i % 2 + 1) * BANK], U[:, i, :], ACT.Copy).then_inc(rows_done, 1)
            act.wait_ge(decays, 2)
            act.activation(e1[:], b[:], ACT.Exp, scale=1.0 / GLA_TAU).then_inc(e1_done, 1)
            act.wait_ge(relative, 1)
            act.activation(e4[:], dl[:], ACT.Exp, scale=1.0 / GLA_TAU).then_inc(e4_done, 1)
            act.wait_ge(relative, 2)
            act.activation(e2[:], dm[:], ACT.Exp, scale=1.0 / GLA_TAU).then_inc(e2_done, 1)
            act.activation(e3[:], dm[:], ACT.Exp, scale=-1.0 / GLA_TAU).then_inc(e3_done, 1)
            act.wait_ge(turned, 1)
            for i in range(2):
                ins = act.activation(klT[:, 2 * i:2 * i + 2, :], O[:, i, :].rearrange("p (t e) -> p t e", t=2), ACT.Copy)
            ins.then_inc(copied, 1)
            for t in range(NT):
                if t >= 1:
                    act.wait_ge(squares, t)
                act.wait_ge(attended, t + 1)
                for h in range(H):
                    ins = act.activation(junk[:, h, :], out_of(t, h), ACT.Square, accum_out=ssq[:, t, h:h + 1])
                ins.then_inc(squares, 1)

        @block.vector
        def _(dve):
            link = Link(dve, dve_link)
            dve.tensor_copy(wide[:, 0:KD, :], bc(mod[:, 2 * KD:3 * KD], 2, P)).then_inc(widened, 1)
            dve.tensor_copy(wide[:, KD:, :], bc(mod[:, 5 * KD:], 2, P)).then_inc(widened, 1)
            dve.wait_ge(logits, 1)
            dve.wait_ge(absed, 1)
            for c in range(2):
                ins = dve.tensor_scalar(minz[:, c, :], S[:, c, :], bg[:, c:c + 1], 0.0, ALU.add, ALU.min)
            ins.then_inc(mined, 1)
            dve.wait_ge(mined, 1)
            dve.wait_ge(logged, 1)
            link(dve.tensor_tensor(minz[:], minz[:], absz[:], ALU.subtract))
            for c in range(2):
                dve.tensor_tensor_scan(b[:, c, :], keep[:], minz[:, c, :], 0.0, ALU.mult, ALU.add).then_inc(decays, 1)
            dve.wait_ge(decays, 2)
            dve.tensor_tensor(chunks(dl), bc(chunks(b)[:, :, C - 1], 2, C), chunks(b), ALU.subtract).then_inc(relative, 1)
            dve.tensor_tensor(chunks(dm), chunks(b), bc(chunks(b)[:, :, C // 2 - 1], 2, C), ALU.subtract).then_inc(relative, 1)
            dve.wait_ge(e4_done, 1)
            dve.tensor_tensor(kl[:], k, e4[:], ALU.mult).then_inc(kl_done, 1)
            dve.wait_ge(e1_done, 1)
            dve.scalar_tensor_tensor(qe[:].rearrange("p c t -> p (c t)"), q.rearrange("p c t -> p (c t)"), GLA_DK ** -0.5,
                                     e1[:].rearrange("p c t -> p (c t)"), ALU.mult, ALU.mult).then_inc(ready, 1)
            dve.wait_ge(e2_done, 1)
            dve.tensor_tensor(qm[:], q, e2[:], ALU.mult).then_inc(ready, 1)
            dve.wait_ge(e3_done, 1)
            dve.tensor_tensor(km[:], k, e3[:], ALU.mult).then_inc(ready, 1)
            link(dve.memset(st[:, 0], 0.0))
            dve.wait_ge(updates, 1)
            for n in range(1, NC):
                m = n - 1
                col = ((m // 2) % 2) * 2 * P
                for c in range(2):
                    up = U[:, (m % 2) * 2 + m // 4, col + c * P:col + (c + 1) * P]
                    ins = dve.scalar_tensor_tensor(st[:, n, c, :], st[:, m, c, :], e1[:, c, m * C + C - 1:m * C + C], up, ALU.mult, ALU.add)
                ins.then_inc(stated, 1)
                dve.wait_ge(stated, n)

            def mask_scores(t):
                dve.wait_ge(scored, t + 1)
                if t >= 2:
                    dve.wait_ge(attended, t - 1)
                for odd in range(2):
                    ins = dve.tensor_tensor(sm[:, t % 2, 2 * odd:2 * odd + 2, :], S[:, odd, 0:2 * P].rearrange("p (h i) -> p h i", i=P),
                                            bc(mask[:], 1, 2), ALU.mult)
                ins.then_inc(masked, 1)

            def norm(t):
                dve.wait_ge(squares, t + 1)
                dve.tensor_scalar(ms[:, t, :], ssq[:, t, :], 1.0 / GLA_DV, EPS, ALU.mult, ALU.add).then_inc(means, 1)
                dve.wait_ge(roots, t + 1)
                if t >= 2:
                    dve.wait_ge(oturned, t - 1)
                for h in range(H):
                    ins = dve.tensor_scalar(on[:, t % 2, h, :], out_of(t, h), rstd[:, t, h:h + 1], None, ALU.mult)
                ins.then_inc(normed, 1)

            def gate(t):
                dve.wait_ge(oturned, t + 1)
                dve.scalar_tensor_tensor(mixT[:, 0:H, t * P:(t + 1) * P], U[:, t % 2, :].rearrange("p (h i) -> p h i", i=P), gn[:, 0:1],
                                         grT[:, :, t * P:(t + 1) * P], ALU.mult, ALU.mult).then_inc(gated, 1)

            mask_scores(0)
            for t in range(NT):
                if t + 1 < NT:
                    mask_scores(t + 1)
                norm(t)
                if t >= 1:
                    gate(t - 1)
            gate(NT - 1)

        @block.tensor
        def _(pe):
            for c in range(2):
                ins = pe.matmul(S[:, c, :], wg[:, c, :], lowT[0:GLA_RANK, :], start=True, stop=True)
            ins.then_inc(logits, 1)
            for i in range(4):
                pe.wait_ge(widened, 1 + i // 2)
                for j in range(4):
                    ins = pe.transpose(U[:, i, j * P:(j + 1) * P], wide[:, 4 * i + j, :], ident[:])
                ins.then_inc(rows_turned, 1)
            pe.wait_ge(kl_done, 1)
            for t in range(NT):
                for c in range(2):
                    ins = pe.transpose(O[:, t // 2, (t % 2) * 2 * P + c * P:(t % 2) * 2 * P + (c + 1) * P], kl[:, c, t * P:(t + 1) * P], ident[:])
            ins.then_inc(turned, 1)
            pe.wait_ge(copied, 1)
            pe.wait_ge(rows_done, 4)
            for n in range(NC - 1):
                r = slice(64 * (n % 2), 64 * (n % 2) + 64)
                col = ((n // 2) % 2) * 2 * P
                for h in range(H):
                    c0 = col + (h // 2) * P
                    ins = pe.matmul(U[head(h), (n % 2) * 2 + n // 4, c0:c0 + P], klT[r, n // 2, 64 * h:64 * h + 64],
                                    v[r, n // 2, h * P:(h + 1) * P], start=True, stop=True)
            ins.then_inc(updates, 1)
            pe.wait_ge(ready, 3)
            pe.wait_ge(mined, 1)

            def score(t):
                if t >= 1:
                    pe.wait_ge(masked, t)
                for h in range(H):
                    ins = pe.matmul(S[:, h % 2, (h // 2) * P:(h // 2 + 1) * P], km[head(h), h // 2, t * P:(t + 1) * P],
                                    qm[head(h), h // 2, t * P:(t + 1) * P], start=True, stop=True)
                ins.then_inc(scored, 1)

            def attend(t):
                pe.wait_ge(masked, t + 1)
                if t >= 2:
                    pe.wait_ge(normed, t - 1)
                pe.wait_ge(stated, 1 if t == 0 else NC - 1)
                for h in range(H):
                    out = out_of(t, h)
                    pe.matmul(out, sm[:, t % 2, 2 * (h % 2) + h // 2, :], v[:, t, h * P:(h + 1) * P], start=True, stop=True)
                    for n in (2 * t, 2 * t + 1):
                        r = slice(64 * (n % 2), 64 * (n % 2) + 64)
                        ins = pe.matmul(out[r], qe[head(h), h // 2, n * C:(n + 1) * C], st[head(h), n, h // 2, :],
                                        start=False, stop=False, skip_group_check=True)
                ins.then_inc(attended, 1)

            def turn(t):
                pe.wait_ge(normed, t + 1)
                if t >= 2:
                    pe.wait_ge(gated, t - 1)
                if t == 0:
                    pe.wait_ge(stated, NC - 1)
                for h in range(H):
                    ins = pe.transpose(U[:, t % 2, h * P:(h + 1) * P], on[:, t % 2, h, :], ident[:])
                ins.then_inc(oturned, 1)

            score(0)
            for t in range(NT):
                if t + 1 < NT:
                    score(t + 1)
                attend(t)
                if t >= 1:
                    turn(t - 1)
            turn(NT - 1)


def ffn_loads(w_dram):
    return lambda raw: [(raw[:, r], w_dram[r]) for r in range(2)]


def ffn_up(nc, hs, w_dram, cw, cb, gT, ring, early):
    R = 2
    steps = NF // R
    with Phase(nc, "ffn") as ph:
        raw = ring.raw
        cut = ph.sb("cut", [P, R, 2, 2, KD, P], F32R)
        u = ph.sb("u", [P, R, 2, SEQ])
        sl = ph.sb("sl", [P, R, SEQ])
        acc = ph.ps("acc", [P, 2 * R, BANK])
        landed = [ph.sem(f"landed{r}") for r in range(R)]
        names = ("early_landed", "hi_made", "lo_made", "done", "biased", "tap1", "conved", "silued", "out")
        early_landed, hi_made, lo_made, done, biased, tap1, conved, silued, out = (ph.sem(x) for x in names)
        block = ph.block()

        @block.sync
        def _(sp):
            def load(r, i):
                sp.dma_start(raw[:, r], w_dram[bass.ds(i * R + r, 1)].rearrange("o p g k n -> (o p) g k n")).then_inc(landed[r], 16)

            with sp.Fori(1, steps) as i:
                for r in range(R):
                    sp.wait_ge(lo_made, (i - 1) * R + r + 1)
                    load(r, i)
            load_early(sp, early_landed, early)

        @block.tensor
        def _(pe):
            def chunk(r, i):
                pe.wait_ge(lo_made, i * R + r + 1)
                for g in range(2):
                    bank = acc[:, 2 * r + g, :]
                    for k in range(KD):
                        pe.matmul(bank, cut[:, r, 0, g, k, :], hs[:, 0, k, :], start=(k == 0), stop=False)
                        pe.matmul(bank, cut[:, r, 0, g, k, :], hs[:, 1, k, :], start=False, stop=False)
                        ins = pe.matmul(bank, cut[:, r, 1, g, k, :], hs[:, 0, k, :], start=False, stop=(k == KD - 1))
                ins.then_inc(done, 1)

            for r in range(R):
                chunk(r, 0)
            with pe.Fori(1, steps) as i:
                for r in range(R):
                    pe.wait_ge(conved, (i - 1) * R + r + 1)
                    chunk(r, i)

        @block.scalar
        def _(act):
            def split(r, i, first=False):
                if not first:
                    act.wait_ge(landed[r], i * 16)
                    act.wait_ge(done, (i - 1) * R + r + 1)
                act.activation(cut[:, r, 0], raw[:, r], ACT.Copy).then_inc(hi_made, 1)

            def chunk(r, i, first=False):
                c = i * R + r
                if not first:
                    act.wait_ge(out, c - R + 1)
                act.wait_ge(done, c + 1)
                for g in range(2):
                    ins = act.activation(u[:, r, g, :], acc[:, 2 * r + g, :], ACT.Identity, bias=cb[:, bass.ds(c * 2 + g, 1)],
                                         scale=cw[:, bass.ds(c * 6 + g * 3 + 2, 1)])
                ins.then_inc(biased, 1)
                act.wait_ge(conved, c + 1)
                act.activation(sl[:, r, :], u[:, r, 0, :], ACT.Silu).then_inc(silued, 1)

            split(0, 0, first=True)
            split(1, 0, first=True)
            for r in range(R):
                split(r, 1)
                chunk(r, 0, first=True)
            with act.Fori(1, steps - 1) as i:
                for r in range(R):
                    split(r, i + 1)
                    chunk(r, i)
            for r in range(R):
                chunk(r, steps - 1)

        @block.vector
        def _(dve):
            def split(r, i):
                dve.wait_ge(hi_made, i * R + r + 1)
                dve.tensor_tensor(cut[:, r, 1], raw[:, r], cut[:, r, 0].bitcast(F32), ALU.subtract).then_inc(lo_made, 1)

            def chunk(r, i):
                c = i * R + r
                dve.wait_ge(biased, c + 1)
                for j, s in ((1, tap1), (0, conved)):
                    lag = 2 - j
                    for g in range(2):
                        ins = dve.scalar_tensor_tensor(u[:, r, g, lag:], acc[:, 2 * r + g, 0:SEQ - lag], cw[:, bass.ds(c * 6 + g * 3 + j, 1)],
                                                       u[:, r, g, lag:], ALU.mult, ALU.add)
                    ins.then_inc(s, 1)
                    if j == 1:
                        dve.wait_ge(tap1, c + 1)
                dve.wait_ge(conved, c + 1)
                dve.wait_ge(silued, c + 1)
                dve.tensor_tensor(gT[:, bass.ds(c, 1), :], sl[:, r:r + 1, :], u[:, r, 1:2, :], ALU.mult).then_inc(out, 1)

            split(0, 0)
            split(1, 0)
            with dve.Fori(0, steps - 1) as i:
                for r in range(R):
                    split(r, i + 1)
                    chunk(r, i)
            for r in range(R):
                chunk(r, steps - 1)


def second_block(nc, consts, resid, mod, d, out, stop):
    with Phase(nc, "m2") as ph:
        rows = ph.sb("rows", [P, 2, D])
        part = lambda i: mod[:, i * KD:(i + 1) * KD]
        with Phase(nc, "m2m") as ph2:
            mixT = ph2.sb("mixT", [P, KD, SEQ])
            out_ring = Early(ph2.sb("out_ring", [P, 2, D]), out_loads(d["w_out_2"]))
            aq, ak, av = (ph2.sb(n, [P, NT, 512]) for n in ("aq", "ak", "av"))
            head_gains = Tables(ph2, g_q=([P, 1], d["q_norm_g"]), g_k=([P, 1], d["k_norm_g"]))
            dilated = Tables(ph2, table=([P, DIL_H, SEQ], d["c_dilated"]))
            qT = ph2.sb("qT", [P, 4, SEQ])
            kT = ph2.sb("kT", [P, 4, SEQ])
            with Phase(nc, "m2g") as ph3:
                gla_tables = Tables(ph3, wg=([GLA_RANK, 2, P], d["gla_w_gate"].rearrange("r (c p) -> r c p", p=P)), bg=([P, 2], d["gla_b_gate"]),
                                    gn=([P, 1], d["gla_norm_g"]), mask=([P, P], d["c_gla_mask"]), keep=([P, SEQ], d["c_scan_keep"]))
                qkT = ph3.sb("qkT", [P, 4, SEQ])
                gv = ph3.sb("gv", [P, NT, 512])
                grT = ph3.sb("grT", [P, 4, SEQ])
                lowT = ph3.sb("lowT", [GLA_RANK, SEQ])
                with Phase(nc, "m2h") as ph4:
                    hs = ph4.sb("hs", [P, 2, KD, SEQ], F32R)
                    ring = Early(ph4.sb("raw", [P, KD, BANK]), project_loads([(d["w_in_2"][:, 3 * 512 + GLA_RANK:4 * 512 + GLA_RANK], None)]))
                    norm_transpose(nc, "n3", consts, resid, hs, d["norm1_g"], mod=(part(1), part(0)), early=[ring, head_gains])
                    tok = lambda dst: ("tok", [(P, t * P, dst[:, t, :]) for t in range(NT)])
                    feat = lambda fn, dst: ("feat", fn, [dst[:, j, :] for j in range(4)])
                    jobs = []
                    c_att = 3 * 512 + GLA_RANK
                    for c, n, o in ((c_att, 512, tok(aq)), (c_att + 512, 512, tok(ak)), (c_att + 1024, 512, tok(av)),
                                    (0, 512, feat(ACT.Copy, qkT)), (512, 512, tok(gv)), (1024, 512, feat(ACT.Silu, grT)),
                                    (1536, GLA_RANK, ("feat", ACT.Copy, [lowT[:, :]]))):
                        jobs.append((d["w_in_2"][:, c:c + n], o))
                    with Phase(nc, "hn") as ph5:
                        guest = HeadNorm(ph5, consts, aq, ak, (head_gains["g_q"], head_gains["g_k"]), qT, kT)
                        project(nc, "p3", hs, jobs, ring, [gla_tables], guest)
                gla(nc, consts, qkT, gv, lowT, grT, gla_tables, mixT, mod, rows, [dilated])
            at = lambda x: lambda h: x[64 * (h % 2):64 * (h % 2) + 64, h // 2, :]
            attention(nc, "at2", consts, at(qT), at(kT), av, None, dilated["table"], 0, DIL_E ** -0.5, mixT[:, 4:8, :], [out_ring])
            out_project(nc, "o2", mixT, d["w_out_2"], KD, resid, out_ring, gate=rows[:, 0, :])
        if stop == 3:
            return
        gT = ph.sb("gT", [P, NF, SEQ])
        out_ring = Early(ph.sb("down_ring", [P, 2, D]), out_loads(d["w_down"]))
        with Phase(nc, "m2f") as ph2:
            ring = Early(ph2.sb("raw", [P, 2, 2, KD, P]), ffn_loads(d["w_up"]))
            conv = Tables(ph2, cw=([P, NF * 6], d["conv_w"].rearrange("p i g j -> p (i g j)")), cb=([P, NF * 2], d["conv_b"].rearrange("p i g -> p (i g)")))
            hs = ph2.sb("hs", [P, 2, KD, SEQ], F32R)
            norm_transpose(nc, "n4", consts, resid, hs, d["norm2_g"], mod=(part(4), part(3)), early=[ring, conv])
            ffn_up(nc, hs, d["w_up"], conv["cw"], conv["cb"], gT, ring, [out_ring])
        out_project(nc, "o3", gT, d["w_down"], NF, resid, out_ring, gate=rows[:, 1, :], out_dram=out)


def program(nc, d, out, stop=9):
    Phase.past = []
    with Phase(nc, "all") as ph:
        resid = ph.sb("resid", [P, NT, D])
        ident = ph.sb("ident", [P, P])
        mod = ph.sb("mod", [P, 6 * KD])
        consts = {"ident": ident}
        with Phase(nc, "c") as ph2:
            s = ph2.sem("consts")
            block = ph2.block()

            @block.sync
            def _(sp):
                sp.dma_start(ident[:], d["c_ident"]).then_inc(s, 16)
                sp.wait_ge(s, 16)
        first_mixer(nc, consts, resid, d)
        if stop > 1:
            peer(nc, consts, resid, mod, d)
        if stop > 2:
            second_block(nc, consts, resid, mod, d, out, stop)
        if stop < 4:
            with Phase(nc, "dump") as ph2:
                s = ph2.sem("dumped")
                block = ph2.block()

                @block.sync
                def _(sp):
                    sp.dma_start(out.rearrange("(t p) n -> p t n", p=P), resid[:]).then_inc(s, 16)
                    sp.wait_ge(s, 16)


def lay_out(inputs):
    a = {k: np.asarray(v) for k, v in inputs.items()}
    cols = lambda g: np.ascontiguousarray(g.reshape(-1, P).T)
    o = {"x": a["x"][0], "meta": a["meta_tokens"]}
    for n in ("w_in", "w_uq", "w_ukv", "w_mla_out", "w_ret_out", "w_mix_out"):
        o[n] = a[n][0]
    for n in ("g_mix", "g_q_lora", "g_kv_lora", "g_ret_gn", "g_ffn"):
        o[n] = cols(a[n][0])
    o["g_qk_q"], o["g_qk_k"] = a["g_qk_q"][0], a["g_qk_k"][0]
    o["peer_keys"] = np.concatenate([a["peer_keys_1"][0].T, a["peer_keys_2"][0].T], 0)
    o["w_peer_q"] = a["w_peer_q"][0].reshape(KD, P, PEER_H, P).transpose(2, 1, 0, 3)
    o["peer_u"] = a["peer_u"][0].reshape(P, P, KD, P).transpose(1, 3, 2, 0)
    o["peer_v"] = a["peer_v"][0].reshape(P, P, D)
    o["c"] = a["c_2"][0]
    o["w_ada"] = a["w_ada_2"][0].T
    o["b_ada"] = cols(a["b_ada_2"][0])
    for n in ("norm1_g", "norm2_g"):
        o[n] = cols(a[n + "_2"][0])
    o["w_in_2"], o["w_out_2"], o["w_down"] = a["w_in_2"][0], a["w_out_2"][0], a["w_down_2"][0]
    o["gla_w_gate"], o["gla_b_gate"] = a["gla_w_gate_2"][0], cols(a["gla_b_gate_2"][0])
    o["gla_norm_g"] = cols(a["gla_norm_g_2"][0])
    o["q_norm_g"] = cols(np.concatenate([a["q_norm_g_2"][0]] * 2))
    o["k_norm_g"] = cols(np.concatenate([a["k_norm_g_2"][0]] * 2))
    o["w_up"] = a["w_up_2"][0].reshape(KD, P, 2, NF, P).transpose(3, 1, 2, 0, 4)
    o["conv_w"] = a["conv_w_2"][0].reshape(3, 2, NF, P).transpose(3, 2, 1, 0)
    o["conv_b"] = a["conv_b_2"][0].reshape(2, NF, P).transpose(2, 1, 0)
    o.update(shape_constants())
    return {k: np.ascontiguousarray(v) for k, v in o.items()}


def build(nc, arrays, stop=9):
    d = {n: nc.dram_tensor(f"in_{n}", a.shape, mybir.dt.from_np(a.dtype), kind="ExternalInput").ap() for n, a in arrays.items()}
    out = nc.dram_tensor("out", (SEQ, D), F32, kind="ExternalOutput").ap()
    program(nc, d, out, stop)


def kernel(**inputs):
    import concourse.bacc as bacc
    from concourse.bass_utils import run_bass_kernel_spmd

    arrays = lay_out(inputs)
    nc = bacc.Bacc("TRN2", target_bir_lowering=False, num_devices=1)
    build(nc, arrays)
    r = run_bass_kernel_spmd(nc, [{f"in_{n}": a for n, a in arrays.items()}], core_ids=[0])
    return r.results[0]["out"].reshape(1, SEQ, D)
```
